# Optimizing a Trainium2 kernel written in Bass

```python
import jax
import jax.numpy as jnp
from jax import lax
import numpy as np

D_MODEL = 1024
BATCH = 1
SEQ = 128
DEPTH = 1
DEC_BATCH = 1
DEC_SEQ = 256
PAST_LEN = 128

GRID_W = 64
EPS = 1e-6
D_RNN = 1024
LRU_BLOCKS = 16
LRU_BLOCK = D_RNN // LRU_BLOCKS
CONV_WIDTH = 4
LRU_C = 8.0
N_HEADS = 8
Q_LORA = 384
KV_LORA = 256
NOPE_DIM = 64
ROPE_DIM = 32
QK_DIM = NOPE_DIM + ROPE_DIM
V_DIM = 64
ROPE_BASE = 10000.0
Q_BLOCK = 128
N_BRANCHES = 2
IN_WIDTH = 2 * D_RNN + Q_LORA + KV_LORA + ROPE_DIM + N_BRANCHES * D_MODEL
SPLITS = (D_RNN, 2 * D_RNN, 2 * D_RNN + Q_LORA, 2 * D_RNN + Q_LORA + KV_LORA, 2 * D_RNN + Q_LORA + KV_LORA + ROPE_DIM)
N_GROUPS = 4
EXPERTS_PER_GROUP = 4
N_EXPERTS = N_GROUPS * EXPERTS_PER_GROUP
TOP_K_IN_GROUP = 2
D_EXPERT = 512

kernel_name = 'hybrid_rglru_mla_hmoe_diffusion_step'

def rms_norm(x, g):
    xf = x.astype(jnp.float32)
    y = xf * lax.rsqrt(jnp.mean(xf * xf, axis=-1, keepdims=True) + EPS)
    return (y * g.astype(jnp.float32)).astype(x.dtype)

def modulation(cond, w_mod, b_mod):
    m = jax.nn.silu(cond) @ w_mod + b_mod
    return [t[:, None, :] for t in jnp.split(m, 6, axis=-1)]

def centred_depthwise_conv(x, w, b):
    t_len = x.shape[1]
    left = (CONV_WIDTH - 1) // 2
    right = CONV_WIDTH - 1 - left
    xp = jnp.pad(x, ((0, 0), (left, right), (0, 0)))
    y = b
    for k in range(CONV_WIDTH):
        y = y + xp[:, k:k + t_len, :] * w[k]
    return y

def linear_scan(a, b, h0, reverse):
    if reverse:
        a, b = jnp.flip(a, axis=1), jnp.flip(b, axis=1)

    def combine(left, right):
        a_l, b_l = left
        a_r, b_r = right
        return a_l * a_r, a_r * b_l + b_r

    a_cum, b_cum = lax.associative_scan(combine, (a, b), axis=1)
    h = a_cum * h0[:, None, :] + b_cum
    return jnp.flip(h, axis=1) if reverse else h

def rglru_direction(xc, h0, wa, ba, wx, bx, lam, reverse):
    bsz, t_len, _ = xc.shape
    xb = xc.reshape(bsz, t_len, LRU_BLOCKS, LRU_BLOCK)
    r = jax.nn.sigmoid(jnp.einsum('btnk,nkj->btnj', xb, wa).reshape(bsz, t_len, D_RNN) + ba)
    i = jax.nn.sigmoid(jnp.einsum('btnk,nkj->btnj', xb, wx).reshape(bsz, t_len, D_RNN) + bx)
    log_a = -LRU_C * r.astype(jnp.float32) * jax.nn.softplus(-lam.astype(jnp.float32))
    a = jnp.exp(log_a)
    b = jnp.sqrt(-jnp.expm1(2.0 * log_a)) * (i * xc).astype(jnp.float32)
    return linear_scan(a, b, h0.astype(jnp.float32), reverse)

def rglru_branch(x_rnn, g_rnn, h0, lw):
    xc = centred_depthwise_conv(x_rnn, lw['conv_w'], lw['conv_b'])
    h_f = rglru_direction(xc, h0[:, 0], lw['lru_wa'][0], lw['lru_ba'][0], lw['lru_wx'][0], lw['lru_bx'][0], lw['lru_lam'][0], False)
    h_b = rglru_direction(xc, h0[:, 1], lw['lru_wa'][1], lw['lru_ba'][1], lw['lru_wx'][1], lw['lru_bx'][1], lw['lru_lam'][1], True)
    y = (h_f + h_b).astype(x_rnn.dtype) * jax.nn.gelu(g_rnn)
    h_final = jnp.stack([h_f[:, -1], h_b[:, 0]], axis=1)
    return y, h_final

def axial_rope_tables(n_tokens):
    rows = n_tokens // GRID_W
    row = jnp.repeat(jnp.arange(rows), GRID_W).astype(jnp.float32)
    col = jnp.tile(jnp.arange(GRID_W), rows).astype(jnp.float32)
    axis_dim = ROPE_DIM // 2
    inv = ROPE_BASE ** (-jnp.arange(0, axis_dim, 2, dtype=jnp.float32) / axis_dim)
    ang = jnp.concatenate([row[:, None] * inv, col[:, None] * inv], axis=-1)
    return jnp.cos(ang), jnp.sin(ang)

def apply_rope(x, cos, sin):
    x1 = x[..., 0::2].astype(jnp.float32)
    x2 = x[..., 1::2].astype(jnp.float32)
    cs = cos[None, :, None, :]
    sn = sin[None, :, None, :]
    out = jnp.stack([x1 * cs - x2 * sn, x1 * sn + x2 * cs], axis=-1)
    return out.reshape(x.shape).astype(x.dtype)

def mla_keys_values(ckv, k_rope, lw):
    bsz, t_len, _ = ckv.shape
    k_nope = (ckv @ lw['w_uk']).reshape(bsz, t_len, N_HEADS, NOPE_DIM)
    k_r = jnp.broadcast_to(k_rope[:, :, None, :], (bsz, t_len, N_HEADS, ROPE_DIM))
    k = rms_norm(jnp.concatenate([k_nope, k_r], axis=-1), lw['k_norm'])
    v = (ckv @ lw['w_uv']).reshape(bsz, t_len, N_HEADS, V_DIM)
    return k, v

def block_attention(q, k, v):
    bsz, t_len, n_h, dk = q.shape
    n_blk = t_len // Q_BLOCK
    qb = jnp.moveaxis(q.reshape(bsz, n_blk, Q_BLOCK, n_h, dk), 1, 0)

    def one_block(qi):
        s = jnp.einsum('bqhd,bkhd->bhqk', qi, k).astype(jnp.float32) * (QK_DIM ** -0.5)
        p = jax.nn.softmax(s, axis=-1).astype(v.dtype)
        return jnp.einsum('bhqk,bkhd->bqhd', p, v)

    o = lax.map(one_block, qb)
    return jnp.moveaxis(o, 0, 1).reshape(bsz, t_len, n_h * V_DIM)

def token_mixer(h, rnn_h0, ctx_ckv, ctx_krope, rope, lw):
    bsz, t_len, _ = h.shape
    proj = h @ lw['w_in']
    x_rnn, g_rnn, q_lat, kv_lat, k_rope, gate_logits = jnp.split(proj, list(SPLITS), axis=-1)
    y_rnn, h_final = rglru_branch(x_rnn, g_rnn, rnn_h0, lw)
    q = (rms_norm(q_lat, lw['q_a_norm']) @ lw['w_uq']).reshape(bsz, t_len, N_HEADS, QK_DIM)
    q = rms_norm(q, lw['q_norm'])
    ckv = rms_norm(kv_lat, lw['kv_a_norm'])
    k, v = mla_keys_values(ckv, k_rope, lw)
    if rope is not None:
        cos, sin = rope
        q = jnp.concatenate([q[..., :NOPE_DIM], apply_rope(q[..., NOPE_DIM:], cos, sin)], axis=-1)
        k = jnp.concatenate([k[..., :NOPE_DIM], apply_rope(k[..., NOPE_DIM:], cos, sin)], axis=-1)
    if ctx_ckv is not None:
        k_ctx, v_ctx = mla_keys_values(ctx_ckv, ctx_krope, lw)
        k = jnp.concatenate([k_ctx, k], axis=1)
        v = jnp.concatenate([v_ctx, v], axis=1)
    y_att = block_attention(q, k, v)
    gates = jax.nn.sigmoid(gate_logits).reshape(bsz, t_len, N_BRANCHES, D_MODEL)
    merged = gates[:, :, 0] * (y_rnn @ lw['w_o_rnn']) + gates[:, :, 1] * (y_att @ lw['w_o_mla'])
    return merged @ lw['w_out'], h_final, ckv, k_rope

def hier_moe(h, lw):
    bsz, t_len, d = h.shape
    xt = h.reshape(bsz * t_len, d)
    n_tok = xt.shape[0]
    g_logits = (xt @ lw['router_wg'] + lw['router_bg']).astype(jnp.float32)
    g_prob = jax.nn.softmax(g_logits, axis=-1)
    g_idx = jnp.argmax(g_logits, axis=-1)
    g_w = jnp.take_along_axis(g_prob, g_idx[:, None], axis=-1)
    e_logits = (xt @ lw['router_we'] + lw['router_be']).astype(jnp.float32).reshape(n_tok, N_GROUPS, EXPERTS_PER_GROUP)
    sel = jnp.broadcast_to(g_idx[:, None, None], (n_tok, 1, EXPERTS_PER_GROUP))
    e_in = jnp.take_along_axis(e_logits, sel, axis=1)[:, 0]
    top_v, top_i = lax.top_k(e_in, TOP_K_IN_GROUP)
    w = jax.nn.softmax(top_v, axis=-1) * g_w
    expert_id = g_idx[:, None] * EXPERTS_PER_GROUP + top_i
    combine = jnp.sum(jax.nn.one_hot(expert_id, N_EXPERTS, dtype=jnp.float32) * w[..., None], axis=1)
    out = jnp.zeros((n_tok, d), jnp.float32)
    for e in range(N_EXPERTS):
        he = jax.nn.silu(xt @ lw['exp_w1'][e]) * (xt @ lw['exp_w3'][e])
        out = out + combine[:, e:e + 1] * (he @ lw['exp_w2'][e]).astype(jnp.float32)
    return out.astype(h.dtype).reshape(bsz, t_len, d)

def context_layer(x, c_ctx, lw):
    bsz = x.shape[0]
    sh1, sc1, g1, sh2, sc2, g2 = modulation(c_ctx[None, :], lw['w_mod'], lw['b_mod'])
    h = rms_norm(x, lw['norm1_g']) * (1.0 + sc1) + sh1
    h0 = jnp.zeros((bsz, 2, D_RNN), jnp.float32)
    mix, h_final, ckv, k_rope = token_mixer(h, h0, None, None, None, lw)
    x = x + g1 * mix
    h = rms_norm(x, lw['norm2_g']) * (1.0 + sc2) + sh2
    x = x + g2 * hier_moe(h, lw)
    return x, ckv, k_rope, h_final.astype(x.dtype)

def latent_layer(x, cond, rnn_h0, ctx_ckv, ctx_krope, rope, lw):
    sh1, sc1, g1, sh2, sc2, g2 = modulation(cond, lw['w_mod'], lw['b_mod'])
    h = rms_norm(x, lw['norm1_g']) * (1.0 + sc1) + sh1
    mix = token_mixer(h, rnn_h0, ctx_ckv, ctx_krope, rope, lw)[0]
    x = x + g1 * mix
    h = rms_norm(x, lw['norm2_g']) * (1.0 + sc2) + sh2
    return x + g2 * hier_moe(h, lw)

def setup_inputs(seed: int = 0) -> dict:
    key = jax.random.key(seed)
    ks = iter(jax.random.split(key, 48))
    f32 = jnp.float32

    def nrm(shape, scale):
        return jax.random.normal(next(ks), shape, f32) * scale

    L = DEPTH
    u = jax.random.uniform(next(ks), (L, 2, D_RNN), f32, minval=0.9, maxval=0.999)
    s = u ** (1.0 / LRU_C)
    return {
        'x_prompt': nrm((BATCH, SEQ, D_MODEL), 1.0),
        'x_sample': nrm((DEC_BATCH, DEC_SEQ, D_MODEL), 1.0),
        'cache_mla_ckv': nrm((DEC_BATCH, L, PAST_LEN, KV_LORA), 1.0),
        'cache_mla_krope': nrm((DEC_BATCH, L, PAST_LEN, ROPE_DIM), 1.0),
        'state_rglru': nrm((DEC_BATCH, L, 2, D_RNN), 0.5),
        'c': nrm((DEC_BATCH, D_MODEL), 1.0),
        'c_ctx': nrm((D_MODEL,), 1.0),
        'norm1_g': 1.0 + nrm((L, D_MODEL), 0.05),
        'norm2_g': 1.0 + nrm((L, D_MODEL), 0.05),
        'w_mod': nrm((L, D_MODEL, 6 * D_MODEL), 0.5 * D_MODEL ** -0.5),
        'b_mod': nrm((L, 6 * D_MODEL), 0.01),
        'w_in': nrm((L, D_MODEL, IN_WIDTH), D_MODEL ** -0.5),
        'conv_w': nrm((L, CONV_WIDTH, D_RNN), CONV_WIDTH ** -0.5),
        'conv_b': nrm((L, D_RNN), 0.01),
        'lru_wa': nrm((L, 2, LRU_BLOCKS, LRU_BLOCK, LRU_BLOCK), LRU_BLOCK ** -0.5),
        'lru_ba': nrm((L, 2, D_RNN), 0.01),
        'lru_wx': nrm((L, 2, LRU_BLOCKS, LRU_BLOCK, LRU_BLOCK), LRU_BLOCK ** -0.5),
        'lru_bx': nrm((L, 2, D_RNN), 0.01),
        'lru_lam': jnp.log(s) - jnp.log1p(-s),
        'q_a_norm': 1.0 + nrm((L, Q_LORA), 0.05),
        'kv_a_norm': 1.0 + nrm((L, KV_LORA), 0.05),
        'w_uq': nrm((L, Q_LORA, N_HEADS * QK_DIM), Q_LORA ** -0.5),
        'w_uk': nrm((L, KV_LORA, N_HEADS * NOPE_DIM), KV_LORA ** -0.5),
        'w_uv': nrm((L, KV_LORA, N_HEADS * V_DIM), KV_LORA ** -0.5),
        'q_norm': 1.0 + nrm((L, QK_DIM), 0.05),
        'k_norm': 1.0 + nrm((L, QK_DIM), 0.05),
        'w_o_rnn': nrm((L, D_RNN, D_MODEL), D_RNN ** -0.5),
        'w_o_mla': nrm((L, N_HEADS * V_DIM, D_MODEL), (N_HEADS * V_DIM) ** -0.5),
        'w_out': nrm((L, D_MODEL, D_MODEL), D_MODEL ** -0.5),
        'router_wg': nrm((L, D_MODEL, N_GROUPS), D_MODEL ** -0.5),
        'router_bg': nrm((L, N_GROUPS), 0.01),
        'router_we': nrm((L, D_MODEL, N_EXPERTS), D_MODEL ** -0.5),
        'router_be': nrm((L, N_EXPERTS), 0.01),
        'exp_w1': nrm((L, N_EXPERTS, D_MODEL, D_EXPERT), D_MODEL ** -0.5),
        'exp_w3': nrm((L, N_EXPERTS, D_MODEL, D_EXPERT), D_MODEL ** -0.5),
        'exp_w2': nrm((L, N_EXPERTS, D_EXPERT, D_MODEL), D_EXPERT ** -0.5),
    }

def reference(x_prompt, x_sample, cache_mla_ckv, cache_mla_krope, state_rglru, c, c_ctx,
              norm1_g, norm2_g, w_mod, b_mod, w_in, conv_w, conv_b,
              lru_wa, lru_ba, lru_wx, lru_bx, lru_lam,
              q_a_norm, kv_a_norm, w_uq, w_uk, w_uv, q_norm, k_norm,
              w_o_rnn, w_o_mla, w_out,
              router_wg, router_bg, router_we, router_be,
              exp_w1, exp_w3, exp_w2):
    rope = axial_rope_tables(x_sample.shape[1])
    y_prompt = x_prompt
    y_sample = x_sample
    ckv_list, krope_list, rnn_list = [], [], []
    for l in range(DEPTH):
        lw = {
            'norm1_g': norm1_g[l], 'norm2_g': norm2_g[l], 'w_mod': w_mod[l], 'b_mod': b_mod[l],
            'w_in': w_in[l], 'conv_w': conv_w[l], 'conv_b': conv_b[l],
            'lru_wa': lru_wa[l], 'lru_ba': lru_ba[l], 'lru_wx': lru_wx[l], 'lru_bx': lru_bx[l], 'lru_lam': lru_lam[l],
            'q_a_norm': q_a_norm[l], 'kv_a_norm': kv_a_norm[l], 'w_uq': w_uq[l], 'w_uk': w_uk[l], 'w_uv': w_uv[l],
            'q_norm': q_norm[l], 'k_norm': k_norm[l],
            'w_o_rnn': w_o_rnn[l], 'w_o_mla': w_o_mla[l], 'w_out': w_out[l],
            'router_wg': router_wg[l], 'router_bg': router_bg[l], 'router_we': router_we[l], 'router_be': router_be[l],
            'exp_w1': exp_w1[l], 'exp_w3': exp_w3[l], 'exp_w2': exp_w2[l],
        }
        y_prompt, ckv, krope, h_fin = context_layer(y_prompt, c_ctx, lw)
        ckv_list.append(ckv)
        krope_list.append(krope)
        rnn_list.append(h_fin)
        y_sample = latent_layer(y_sample, c, state_rglru[:, l], cache_mla_ckv[:, l], cache_mla_krope[:, l], rope, lw)
    new_mla_ckv = jnp.stack(ckv_list, axis=1)
    new_mla_krope = jnp.stack(krope_list, axis=1)
    new_state_rglru = jnp.stack(rnn_list, axis=1)
    return (y_prompt, y_sample, new_mla_ckv, new_mla_krope, new_state_rglru)


_drawn_inputs = setup_inputs


def setup_inputs(seed=0):
    import zlib

    import numpy as np

    out = dict(_drawn_inputs(seed))
    spreads = {}
    factors = {'cache_mla_ckv': 4.776,
     'cache_mla_krope': 6.553,
     'norm2_g': 3.629,
     'lru_ba': 33.219,
     'lru_bx': 8.0,
     'q_a_norm': 8.0,
     'w_uq': 2.956,
     'w_uk': 3.332,
     'q_norm': 8.0,
     'k_norm': 8.0,
     'router_bg': 6.545,
     'router_be': 8.0}
    for name, (base, spread) in spreads.items():
        noise = np.random.default_rng([zlib.crc32(name.encode()), seed]).standard_normal(out[name].shape)
        drawn = base * np.exp(spread * noise) if base else spread * noise
        out[name] = jnp.asarray(drawn.astype(out[name].dtype))
    for name, factor in factors.items():
        out[name] = (out[name] * factor).astype(out[name].dtype)
    return out
```

```python
from contextlib import ExitStack

import concourse.bass as bass
from concourse import mybir

ALU = mybir.AluOpType
ACT = mybir.ActivationFunctionType
AX = mybir.AxisListType
F32 = mybir.dt.float32
I32 = mybir.dt.int32

P = 128
D = 1024
KT = D // P
CTX, LAT = 128, 256
NTOK = CTX + LAT
NT = NTOK // P
PADTOK = NTOK + 2
LAT0 = CTX + 2
H, NOPE, ROPE, QK, V = 8, 64, 32, 96, 64
QL, KVL = 384, 256
CK = KVL + ROPE
LRU_C = 8.0
EPS = 1e-6
NE, NG, EG, HID = 16, 4, 4, 512
NR = NG + NE
T = 80
ROUNDS = -(-NTOK // T)
CREDIT = 1
PAIRS = NE // 2
HB = HID // P
C_G, C_Q, C_KV, C_GATE = D, 2 * D, 2 * D + QL, 2 * D + QL + CK
SLOT = 4096
RING = 4
SEGS = ((0, 0, CTX), (1, CTX, NTOK))
PSEGS = ((0, CTX, 0), (CTX, NTOK, 2))

BMOD, N1, N2, CVEC, CONVW, CONVB, NVA = 0, 48, 56, 64, 80, 112, 120
BA, BX, LAM, STATE, NVB = 0, 16, 32, 48, 64
SH1, SC1, G1, SH2, SC2, G2 = (8 * i for i in range(6))
K_ID, K_UP, K_IOTA, K_ROPE, K_FIRST, K_THR, NK = 0, P, 2 * P, 2 * P + T, 2 * P + T + 64, 2 * P + T + 68, 2 * P + T + 68 + ROUNDS
UNITS = [(h, q) for h in range(H) for q in range(NT)]


def stream_plan():
    plan = [("mod", c) for c in range(4)]
    plan += [("xrnn", 0), ("xrnn", 1), ("qlat", 0), ("kvlat", 0), ("uq", 0), ("ukv", 0)]
    plan += [("mod", 4), ("mod", 5), ("grnn", 0), ("grnn", 1)]
    plan += [("mod", c) for c in range(6, 12)]
    plan += [("gate", 0), ("ornn", 0), ("gate", 1), ("ornn", 1), ("gate", 2), ("gate", 3), ("omla", 0)]
    plan += [("wout", 0), ("wout", 1)]
    return plan


def psum_plan():
    g = [("vec", 0, "dve"), ("vec", 1, "dve")]
    g += [("mod", c, "dve") for c in range(4)]
    g += [("hT", f, "dve") for f in range(KT)]
    g += [("xrnn", j, "act") for j in range(KT)]
    g += [("qlat", t, "dve") for t in range(NT)] + [("kvlat", t, "dve") for t in range(NT)]
    g += [("lru", (n, s), "act") for n in range(16) for s in range(2)]
    g += [("qlT", f, "act") for f in range(3)] + [("ckvT", f, "act") for f in range(2)]
    for n in range(8):
        if n < 3:
            g += [("uq", (n, 0), "act"), ("uq", (n, 1), "act")]
        elif n < 7:
            g += [("uk", n - 3, "act"), ("uv", n - 3, "act")]
        if n >= 1:
            g += [("qkT", (n - 1, 0), "act"), ("qkT", (n - 1, 1), "act")]
    g += [("mod", c, "dve") for c in (4, 5)]
    g += [("grnn", j, "act") for j in range(KT)]
    g += [("mod", c, "dve") for c in range(6, 12)]
    for i in range(len(UNITS) + 3):
        if i < len(UNITS):
            g += [("score", i, "act")]
        if 0 <= i - 2 < len(UNITS):
            g += [("pT", i - 2, "act")]
        if i >= 3:
            g += [("pv", i - 3, "dve")]
    g += [("gb1", (c, hf), "act") for c in range(2) for hf in range(2)]
    for c in range(2):
        g += [("gate", 4 * c + b, "act") for b in range(4)] + [("ornn", 4 * c + b, "dve") for b in range(4)]
    g += [("gate", 8 + b, "act") for b in range(8)] + [("omla", b, "dve") for b in range(8)]
    g += [("mix", (hf, t), "dve") for hf in range(2) for t in range(NT)]
    g += [("state", 0, "act")]
    g += [("h2T", f, "act") for f in range(KT)]
    g += [("logit", 0, "dve")]
    g += [("h2tok", (t, hf), "act") for t in range(NT) for hf in range(2)]
    g += [("gb2", (c, hf), "act") for c in range(2) for hf in range(2)]
    g += [("pos", 0, "dve")]
    return g


def hybrid_step(nc, io, y_prompt, y_sample, new_ckv, new_krope, new_state):
    chunks = stream_plan()
    chunk_no = {key: n for n, key in enumerate(chunks)}
    plan = psum_plan()
    group_no = {(k, i): n for n, (k, i, _) in enumerate(plan)}
    emptied_by = []
    count = {"act": 0, "dve": 0}
    for _, _, who in plan:
        count[who] += 1
        emptied_by.append((who, count[who]))

    with ExitStack() as ctx:
        floats = 53200
        mem = ctx.enter_context(nc.sbuf_tensor("mem", [P, floats], F32))
        banks = [ctx.enter_context(nc.psum_tensor(f"bank{b}", [P, 512], F32)) for b in range(8)]

        def sem(name):
            return ctx.enter_context(nc.semaphore(name))

        top = [0]

        def take(n):
            at = top[0]
            top[0] += n
            assert top[0] <= floats, top[0]
            return at

        def view(at, *dims):
            n = 1
            for d in dims:
                n *= d
            ap = mem[:, at:at + n]
            if len(dims) == 2:
                ap = ap.rearrange("p (a b) -> p a b", a=dims[0])
            if len(dims) == 3:
                ap = ap.rearrange("p (a b c) -> p a b c", a=dims[0], b=dims[1])
            return ap

        ring_at = [take(SLOT) for _ in range(RING)]
        extra_at = top[0]
        at_q = take(H * NTOK)
        qT = view(at_q, H, NTOK)
        xpad = [view(at_q + 400 * b, 3 + PADTOK) for b in range(2)]
        values = view(take(4 * H * V), 4, H * V)
        at_work = take(2 * H * QK)
        work = view(at_work, 2, H, QK)
        yatt = view(at_work, 4, NTOK)
        lru_at = take(9 * PADTOK)
        lru = view(lru_at, 3, 3, PADTOK)
        gtmp = view(lru_at, 2, NTOK)
        lru_sq = view(take(PADTOK), PADTOK)
        assert top[0] - extra_at >= 2 * SLOT
        x = view(take(NT * D), NT, D)
        hT = view(take(KT * NTOK), KT, NTOK)
        at_xc = take(KT * PADTOK)
        xc = view(at_xc, KT, PADTOK)
        gbuf = view(at_xc, KT, NTOK)
        acc = view(at_xc, NT, D)
        at_y = take(KT * NTOK)
        xs = view(at_y, NT, D)
        y = view(at_y, KT, NTOK)
        h2 = view(at_y, NT, D)
        at_kl = take(SLOT)
        kT = view(at_kl, H, 512)
        lruw = view(at_kl, 32, P)
        merged = view(at_kl, KT, NTOK)
        at_qln = take(NT * QL)
        qln = view(at_qln, NT, QL)
        prob = view(at_qln, 3, NTOK)
        ckv = view(take(4 * CK), 4, CK)
        at_qlT = take(3 * NTOK)
        qlT = view(at_qlT, 3, NTOK)
        pT = view(at_qlT, 2, NTOK)
        scratch = view(at_qlT, 512)
        ckvT = view(take(2 * 512), 2, 512)
        bc = view(take(2 * D), 2, D)
        mcol = view(take(96), 48, 2)
        va = view(take(NVA), NVA)
        vb = view(take(NVB), NVB)
        silu_c = view(take(16), KT, 2)
        tanh_c = view(take(16), 2, KT)
        scale1 = view(take(16), KT, 2)
        scale2 = view(take(16), KT, 2)
        hbias = view(take(32), 32)
        lam = view(take(16 * 6), 6, 16)
        hc = view(take(16), 16)
        nhc = view(take(16), 16)
        const = view(take(NK), NK)
        ident = const[:, K_ID:K_ID + P]
        upper = const[:, K_UP:K_UP + P]
        iota = const[:, K_IOTA:K_IOTA + T]
        ones = view(take(P), P)
        qan = view(take(QL), QL)
        kvan = view(take(KVL), KVL)
        qk_g = view(take(2 * QK), 2, QK)
        router_b = view(take(NR), NR)
        router_w = view(take(KT * NR), KT, NR)
        ss = view(take(16), 16)
        rs = view(take(16), 16)
        ssh = view(take(56), 7, H)
        rsh = view(take(56), 7, H)
        rmax = view(take(24), 24)
        rsum = view(take(24), 24)
        eps = view(take(1), 1)
        st = view(take(16), 16)
        st_row = view(take(P), P)
        tmp_at = take(H * QK)
        sq = view(tmp_at, H, QK)
        rt = view(tmp_at, 4, H, ROPE // 2)
        at = [tmp_at]

        def small(*dims):
            n = 1
            for d in dims:
                n *= d
            at[0] += n
            assert at[0] <= tmp_at + H * QK
            return view(at[0] - n, *dims)

        lg = small(NT, NR)
        gm, gz, m1, m2, w1c, w2c, e21, gw = (small(NT, 1) for _ in range(8))
        gsh, g1h, ein, o1, o2, t4, wsel, ssel = (small(NT, EG) for _ in range(8))
        eprod, sel, comb, posm = (small(NT, NE) for _ in range(4))
        rcount = small(ROUNDS)
        cmax, nrf = small(1), small(1)
        nri = mem[:, at[0]:at[0] + 1].bitcast(I32)
        small(1)
        pcur, ccur = (small(2, NT) for _ in range(2))
        at = [at_kl]

        def moe(*dims):
            n = 1
            for d in dims:
                n *= d
            at[0] += n
            assert at[0] <= at_qlT
            return view(at[0] - n, *dims)

        xeT = [moe(KT, T) for _ in range(2)]
        heT = [moe(HB, T) for _ in range(2)]
        sil = [moe(HB, T) for _ in range(2)]
        S = [moe(NT, T) for _ in range(2)]
        SW = [moe(NT, T) for _ in range(2)]
        SWT = [mem[0:T, moe_at:moe_at + NTOK] for moe_at in (at[0], at[0] + NTOK)]
        moe(2, NTOK)
        ye = [view(at_qlT + D * u, D)[0:T] for u in range(2)]
        assert 2 * D <= 3 * NTOK + 1024

        nf = len(chunks)
        slot_at = ring_at + [extra_at, extra_at + SLOT]
        expert_slots = [4, 5] + [(nf + i) % RING for i in range(RING)]

        def chunk_ap(key):
            kind, _ = key
            at0 = ring_at[chunk_no[key] % RING]
            if kind in ("mod", "xrnn", "grnn", "gate", "ornn", "wout"):
                return view(at0, KT, 512)
            if kind == "qlat":
                return view(at0, KT, QL)
            if kind == "kvlat":
                return view(at0, KT, CK)
            if kind == "uq":
                return view(at0, 3, H * QK)
            if kind == "ukv":
                return view(at0, 4, 512)
            return view(at0, 4, D)

        reader = {"qlat": ("qlat", NT), "kvlat": ("kvlat", NT), "ukv": ("uv", 4), "omla": ("omla", 8)}
        chunk_end = []
        for kind, c in chunks:
            if kind == "mod":
                last = (kind, c)
            elif kind == "uq":
                last = (kind, (NT - 1, 1))
            elif kind == "wout":
                last = ("mix", (c, NT - 1))
            elif kind in reader:
                last = (reader[kind][0], reader[kind][1] - 1)
            else:
                last = (kind, 4 * c + 3)
            chunk_end.append(group_no[last] + 1)

        def done(kind, which):
            return group_no[(kind, which)] + 1

        def out_of(kind, which):
            who, c = emptied_by[group_no[(kind, which)]]
            return freed[who], c

        filled = sem("psum_filled")
        freed = {"act": sem("psum_freed_by_act"), "dve": sem("psum_freed_by_dve")}
        loaded = [sem(f"ring{s}_loaded") for s in range(RING)]
        const_in, x_in, vec_in, row_in, cache_in, lruw_in = (sem(n) for n in (
            "const_in", "x_in", "vec_in", "row_in", "cache_in", "lruw_in"))
        zeroed, dve_chain, act_chain = sem("zeroed"), sem("dve_chain"), sem("act_chain")
        sumsq, root, xs_ready = sem("sumsq"), sem("root"), sem("xs_ready")
        cols_ready, tanhc_ready, silu_ready, hT_ready = (sem(n) for n in (
            "cols_ready", "tanhc_ready", "silu_ready", "hT_ready"))
        xpad_ready, conv_done = sem("xpad_ready"), sem("conv_done")
        lru_cols, lru_exp, lru_ez, lru_q, lru_root, lru_done = (sem(n) for n in (
            "lru_cols", "lru_exp", "lru_ez", "lru_q", "lru_root", "lru_done"))
        y_ready, gelu_ready = sem("y_ready"), sem("gelu_ready")
        qlT_ready, kv_ready = sem("qlT_ready"), sem("kv_ready")
        work_raw, work_sq, work_root, work_ready = (sem(n) for n in ("work_raw", "work_sq", "work_root", "work_ready"))
        qkT_ready, nmax_ready, exp_ready, prob_ready, pT_ready, yatt_ready = (sem(n) for n in (
            "qkT_ready", "nmax_ready", "exp_ready", "prob_ready", "pT_ready", "yatt_ready"))
        diag_ready, bc_ready, gate_ready, merged_ready, x_ready = (sem(n) for n in (
            "diag_ready", "bc_ready", "gate_ready", "merged_ready", "x_ready"))
        scale2_ready, h2T_ready, h2_ready, sel_ready = (sem(n) for n in (
            "scale2_ready", "h2T_ready", "h2_ready", "sel_ready"))
        final = sem("final")
        stored = sem("stored")
        e_loaded = [sem(f"expert_slot{i}_loaded") for i in range(6)]
        e_used = [sem(f"expert_slot{i}_used") for i in range(6)]
        S_ready, gathered, xe_ready, sil_ready, he_ready = (sem(n) for n in (
            "S_ready", "gathered", "xe_ready", "sil_ready", "he_ready"))
        swt_done, scattered = ([sem(f"{n}{u}") for u in range(2)] for n in ("map_turned", "scattered"))
        y_done, ye_ready, sc_done, swt_ready, pos_cur, acc_step, pos_round = (sem(n) for n in (
            "y_done", "ye_ready", "sc_done", "swt_ready", "pos_cur", "acc_step", "pos_round"))

        block = ctx.enter_context(nc.Block())

        def w1_src(e):
            return io["exp_w1"][0, e].rearrange("(f p) n -> p f n", p=P)

        @block.sync
        def _(sp):
            w_in = io["w_in"][0].rearrange("(f p) n -> p f n", p=P)
            w_mod = io["w_mod"][0].rearrange("(f p) n -> p f n", p=P)
            o_rnn = io["w_o_rnn"][0].rearrange("(f p) n -> p f n", p=P)
            w_out = io["w_out"][0].rearrange("(f p) n -> p f n", p=P)
            for n, (kind, c) in enumerate(chunks):
                if n >= RING:
                    sp.wait_ge(filled, chunk_end[n - RING])
                dst = chunk_ap((kind, c))
                if kind == "ukv":
                    sp.dma_start(dst[:, 0:2, :], io["w_uk"][0].rearrange("(f p) n -> p f n", p=P)).then_inc(loaded[n % RING], 16)
                    sp.dma_start(dst[:, 2:4, :], io["w_uv"][0].rearrange("(f p) n -> p f n", p=P)).then_inc(loaded[n % RING], 16)
                    continue
                src = {"mod": w_mod[:, :, c * 512:(c + 1) * 512],
                       "xrnn": w_in[:, :, (c % 2) * 512:(c % 2 + 1) * 512],
                       "grnn": w_in[:, :, C_G + (c % 2) * 512:C_G + (c % 2 + 1) * 512],
                       "qlat": w_in[:, :, C_Q:C_Q + QL],
                       "kvlat": w_in[:, :, C_KV:C_KV + CK],
                       "gate": w_in[:, :, C_GATE + (c % 4) * 512:C_GATE + (c % 4 + 1) * 512],
                       "uq": io["w_uq"][0].rearrange("(f p) n -> p f n", p=P),
                       "ornn": o_rnn[:, :, (c % 2) * 512:(c % 2 + 1) * 512],
                       "omla": io["w_o_mla"][0].rearrange("(f p) n -> p f n", p=P),
                       "wout": w_out[:, :, (c % 2) * 512:(c % 2 + 1) * 512]}[kind]
                sp.dma_start(dst, src).then_inc(loaded[n % RING], 16)

            def expert_chunk(j, e):
                dst = slot_at[expert_slots[j]]
                if j < 4:
                    src = (io["exp_w1"] if j % 2 == 0 else io["exp_w3"])[0, bass.ds(e + j // 2, 1)]
                    sp.dma_start(view(dst, KT, HID), src.rearrange("e (f p) n -> p (e f) n", p=P)).then_inc(e_loaded[j], 16)
                else:
                    src = io["exp_w2"][0, bass.ds(e + j - 4, 1)]
                    sp.dma_start(view(dst, HB, D), src.rearrange("e (f p) n -> p (e f) n", p=P)).then_inc(e_loaded[j], 16)

            sp.wait_ge(filled, chunk_end[chunk_no[("omla", 0)]])
            for j in range(6):
                if j >= 2:
                    sp.wait_ge(filled, chunk_end[nf - RING + j - 2])
                expert_chunk(j, 0)
            with sp.Fori(1, PAIRS) as i:
                for j in range(6):
                    sp.wait_ge(e_used[j], i + CREDIT)
                    expert_chunk(j, 2 * i)
            sp.wait_ge(*out_of("pos", 0))
            rounds = sp.value_load(nri[0:1, :], min_val=1, max_val=ROUNDS)
            with sp.If(rounds > 1):
                with sp.Fori(1, rounds) as r:
                    with sp.Fori(0, PAIRS) as i:
                        for j in range(6):
                            sp.wait_ge(e_used[j], r * PAIRS + i + CREDIT)
                            expert_chunk(j, 2 * i)

        @block.gpsimd
        def _(pool):
            pool.memset(ones, 1.0).then_inc(zeroed, 1)
            pool.memset(eps, EPS).then_inc(zeroed, 1)
            pool.memset(lruw, 0.0).then_inc(zeroed, 1)
            for b in range(2):
                pool.memset(xpad[b], 0.0).then_inc(zeroed, 1)
            pool.wait_ge(zeroed, 5)
            lv = lruw.rearrange("p (j k) m -> p j k m", k=4)
            for d in range(2):
                for s, name in enumerate(("lru_wa", "lru_wx")):
                    src = io[name][0, d].rearrange("(j h) k m -> h k j m", h=2)
                    for hh in range(2):
                        pool.dma_start(lv[64 * hh:64 * hh + 64, :, 2 * d + s, 64 * hh:64 * hh + 64], src[hh]).then_inc(lruw_in, 16)

            def spread(dst, name, n):
                src = io[name][0].rearrange("(a n) -> a n", a=1)
                pool.dma_start(dst, src.to_broadcast([P, n])).then_inc(row_in, 16)

            spread(qan, "q_a_norm", QL)
            spread(kvan, "kv_a_norm", KVL)
            spread(qk_g[:, 0, :], "q_norm", QK)
            spread(qk_g[:, 1, :], "k_norm", QK)
            spread(router_b[:, 0:NG], "router_bg", NG)
            spread(router_b[:, NG:NR], "router_be", NE)
            pool.dma_start(router_w[:, :, 0:NG], io["router_wg"][0].rearrange("(f p) n -> p f n", p=P)).then_inc(row_in, 16)
            pool.dma_start(router_w[:, :, NG:NR], io["router_we"][0].rearrange("(f p) n -> p f n", p=P)).then_inc(row_in, 16)

        @block.scalar
        def _(act):
            steps = [0]

            def chain(ins):
                steps[0] += 1
                ins.then_inc(act_chain, 1)
                act.wait_ge(act_chain, steps[0])

            def full(kind, which):
                act.wait_ge(filled, done(kind, which))

            act.dma_start(const, io["consts"]).then_inc(const_in, 16)
            va_row, vb_row = mem[0:NVA, at_qln:at_qln + P], mem[0:NVB, at_qln + P:at_qln + 2 * P]

            def rows(dst, lo, ap):
                src = ap.rearrange("(r n) -> r n", n=P)
                act.dma_start(dst[lo:lo + src.shape[0], :], src).then_inc(vec_in, 16)

            rows(va_row, BMOD, io["b_mod"][0])
            rows(va_row, N1, io["norm1_g"][0])
            rows(va_row, N2, io["norm2_g"][0])
            rows(va_row, CVEC, io["c_ctx"])
            rows(va_row, CVEC + KT, io["c"][0])
            rows(va_row, CONVW, io["conv_w"][0].rearrange("k n -> (k n)"))
            rows(va_row, CONVB, io["conv_b"][0])
            rows(vb_row, BA, io["lru_ba"][0].rearrange("d n -> (d n)"))
            rows(vb_row, BX, io["lru_bx"][0].rearrange("d n -> (d n)"))
            rows(vb_row, LAM, io["lru_lam"][0].rearrange("d n -> (d n)"))
            rows(vb_row, STATE, io["state_rglru"][0, 0].rearrange("d n -> (d n)"))
            act.dma_start(x[:, 0, :], io["x_prompt"][0]).then_inc(x_in, 16)
            act.dma_start(x[:, 1:3, :], io["x_sample"][0].rearrange("(t p) n -> p t n", p=P)).then_inc(x_in, 16)
            act.dma_start(ckv[:, 3, 0:KVL], io["cache_mla_ckv"][0, 0]).then_inc(cache_in, 16)
            act.dma_start(ckv[:, 3, KVL:CK], io["cache_mla_krope"][0, 0]).then_inc(cache_in, 16)

            act.wait_ge(zeroed, 5)
            act.wait_ge(x_in, 32)
            for t in range(NT):
                act.activation(xs[:, t, :], x[:, t, :], ACT.Square, accum_out=ss[:, t:t + 1]).then_inc(sumsq, 1)
            act.wait_ge(sumsq, NT)
            act.activation(rs[:, 0:NT], ss[:, 0:NT], ACT.Sqrt, scale=1.0 / D, bias=eps).then_inc(root, 1)
            act.wait_ge(cols_ready, 1)
            act.activation(tanh_c, va[:, CVEC:CVEC + 2 * KT].rearrange("p (a b) -> p a b", a=2), ACT.Tanh, scale=0.5).then_inc(tanhc_ready, 1)
            act.wait_ge(lru_ez, 1)
            act.activation(lam[:, 1, :], lam[:, 0, :], ACT.Exp, scale=-1.0).then_inc(lru_exp, 1)

            n_work = [0]
            for n, (kind, which, who) in enumerate(plan):
                b = banks[n % 8]
                if who == "act":
                    act.wait_ge(filled, n + 1)
                if kind == "xrnn":
                    j = which
                    if j >= 2:
                        act.wait_ge(conv_done, j - 1)
                    act.activation(xpad[j % 2][:, 1:1 + CTX], b[:, 0:CTX], ACT.Copy).then_inc(xpad_ready, 1)
                    act.activation(xpad[j % 2][:, 1 + LAT0:1 + PADTOK], b[:, CTX:NTOK], ACT.Copy).then_inc(freed["act"], 1)
                elif kind in ("qlat", "kvlat"):
                    act.wait_ge(filled, n + 1)
                    width = QL if kind == "qlat" else KVL
                    col = (3 if kind == "qlat" else 6) + which
                    chain(act.activation(lru_sq[:, 0:width], b[:, 0:width], ACT.Square, accum_out=ss[:, col:col + 1]))
                    act.activation(rs[:, col:col + 1], ss[:, col:col + 1], ACT.Sqrt, scale=1.0 / width, bias=eps).then_inc(root, 1)
                elif kind == "lru":
                    m, s = which
                    d, j = m % 2, m // 2
                    cur = lru[:, m % 3]
                    if m == 0 and s == 0:
                        act.wait_ge(lru_cols, 1)
                        act.wait_ge(*out_of("kvlat", NT - 1))
                    if m >= 3 and s == 0:
                        act.wait_ge(lru_done, (m - 3) // 2 + 1)
                    bias = hbias[:, 16 * s + 8 * d + j:16 * s + 8 * d + j + 1]
                    act.activation(cur[:, s, :], b[:, 0:PADTOK], ACT.Tanh, scale=0.5, bias=bias).then_inc(freed["act"], 1)
                    if s == 1:
                        c = 8 * d + j
                        act.wait_ge(freed["act"], emptied_by[n][1])
                        chain(act.activation(cur[:, 2, :], cur[:, 0, :], ACT.Exp, scale=hc[:, c:c + 1], bias=hc[:, c:c + 1]))
                        act.activation(cur[:, 0, :], cur[:, 0, :], ACT.Tanh, scale=nhc[:, c:c + 1], bias=nhc[:, c:c + 1]).then_inc(lru_ez, 1)
                        if m >= 1:
                            act.wait_ge(lru_q, m)
                            prev = lru[:, (m - 1) % 3]
                            act.activation(prev[:, 0, :], prev[:, 0, :], ACT.Sqrt, scale=0.25).then_inc(lru_root, 1)
                elif kind == "qlT":
                    if which == 0:
                        act.wait_ge(lru_q, 16)
                        act.activation(lru[:, 15 % 3, 0, :], lru[:, 15 % 3, 0, :], ACT.Sqrt, scale=0.25).then_inc(lru_root, 1)
                    act.activation(qlT[:, which, :], b[:, 0:NTOK], ACT.Copy).then_inc(freed["act"], 1)
                elif kind == "ckvT":
                    act.activation(ckvT[:, which, :], b[:, :], ACT.Copy).then_inc(freed["act"], 1)
                elif kind == "uq":
                    t, hf = which
                    if t >= 2:
                        act.wait_ge(filled, done("qkT", (t - 2, 1)))
                    act.activation(work[:, t % 2, 4 * hf:4 * hf + 4, :], b[:, 0:4 * QK].rearrange("p (h d) -> p h d", d=QK),
                                   ACT.Copy).then_inc(freed["act"], 1)
                elif kind == "uk":
                    w = which + 3
                    act.wait_ge(filled, done("qkT", (w - 2, 1)))
                    act.activation(work[:, w % 2, :, 0:NOPE], b[:, :].rearrange("p (h d) -> p h d", d=NOPE),
                                   ACT.Copy).then_inc(freed["act"], 1)
                elif kind == "uv":
                    act.activation(values[:, which, :], b[:, :], ACT.Copy).then_inc(freed["act"], 1)
                if (kind == "uq" and which[1] == 1) or kind == "uk":
                    w = which[0] if kind == "uq" else which + 3
                    act.wait_ge(work_sq, w + 1)
                    act.activation(rsh[:, w, :], ssh[:, w, :], ACT.Sqrt, scale=1.0 / QK, bias=eps).then_inc(work_root, 1)
                elif kind == "qkT":
                    w, hf = which
                    src = b[0:QK, :].rearrange("p (h n) -> p h n", n=P)
                    if w == 0 and hf == 0:
                        act.wait_ge(conv_done, KT)
                    dst = qT[0:QK, 4 * hf:4 * hf + 4, w * P:(w + 1) * P] if w < 3 else \
                        kT[0:QK, 4 * hf:4 * hf + 4, (w - 3) * P:(w - 2) * P]
                    act.activation(dst, src, ACT.Copy).then_inc(freed["act"], 1)
                elif kind == "grnn":
                    if which >= 2:
                        act.wait_ge(y_ready, which - 1)
                    else:
                        act.wait_ge(lru_done, 8)
                    act.activation(gtmp[:, which % 2, :], b[:, 0:NTOK], ACT.Gelu_apprx_tanh).then_inc(freed["act"], 1)
                elif kind == "score":
                    i = which
                    nk = CTX if UNITS[i][1] == 0 else NTOK
                    act.wait_ge(nmax_ready, i + 1)
                    if i >= 3:
                        act.wait_ge(filled, done("pT", i - 3))
                    act.activation(prob[:, i % 3, 0:nk], b[:, 0:nk], ACT.Exp, scale=QK ** -0.5, bias=rmax[:, i:i + 1],
                                   accum_out=rsum[:, i:i + 1]).then_inc(freed["act"], 1)
                elif kind == "pT":
                    i = which
                    nk = CTX if UNITS[i][1] == 0 else NTOK
                    if i >= 2:
                        act.wait_ge(filled, done("pv", i - 2))
                    act.activation(pT[:, i % 2, 0:nk], b[:, 0:nk], ACT.Copy).then_inc(freed["act"], 1)
                elif kind in ("gb1", "gb2"):
                    c, hf = which
                    if kind == "gb2" and which == (0, 0):
                        act.wait_ge(x_ready, 6)
                    act.activation(bc[:, c, 512 * hf:512 * hf + 512], b[:, :], ACT.Copy).then_inc(freed["act"], 1)
                elif kind == "gate":
                    if which == 0:
                        act.wait_ge(filled, done("lru", (15, 1)))
                        act.wait_ge(lru_done, 8)
                    if which >= 8:
                        act.wait_ge(*out_of("ornn", which - 8))
                    act.activation(gbuf[:, which % 8, :], b[:, 0:NTOK], ACT.Tanh, scale=0.5).then_inc(freed["act"], 1)
                elif kind == "state":
                    act.activation(st_row[0:16, :], b[0:16, 0:P], ACT.Copy).then_inc(freed["act"], 1)
                    act.wait_ge(freed["act"], emptied_by[n][1])
                    act.dma_start(new_state[0, 0].rearrange("d (j p) -> (d j) p", p=P), st_row[0:16, :]).then_inc(stored, 16)
                elif kind == "h2T":
                    f = which
                    if f == 0:
                        act.wait_ge(scale2_ready, 1)
                    act.activation(hT[:, f, 0:CTX], b[:, 0:CTX], ACT.Identity, scale=scale2[:, f, 0:1], bias=mcol[:, SH2 + f, 0:1])\
                       .then_inc(h2T_ready, 1)
                    act.activation(hT[:, f, CTX:NTOK], b[:, CTX:NTOK], ACT.Identity, scale=scale2[:, f, 1:2], bias=mcol[:, SH2 + f, 1:2])\
                       .then_inc(freed["act"], 1)
                elif kind == "h2tok":
                    t, hf = which
                    if which == (1, 0):
                        act.wait_ge(sel_ready, 1)
                        chain(act.activation(gsh, gsh, ACT.Exp))
                        act.activation(e21, e21, ACT.Exp).then_inc(h2T_ready, 1)
                    act.activation(h2[:, t, 512 * hf:512 * hf + 512], b[:, :], ACT.Copy).then_inc(freed["act"], 1)
                elif kind == "mix" and which == (1, NT - 1):
                    act.wait_ge(x_ready, 6)
                    act.wait_ge(filled, done("ornn", 7))
                    for t in range(NT):
                        act.activation(xs[:, t, :], x[:, t, :], ACT.Square, accum_out=ss[:, 9 + t:10 + t]).then_inc(sumsq, 1)
                    act.wait_ge(sumsq, 2 * NT)
                    act.activation(rs[:, 9:12], ss[:, 9:12], ACT.Sqrt, scale=1.0 / D, bias=eps).then_inc(root, 1)
                if kind == "kvlat" and which == 0:
                    act.wait_ge(*out_of("kvlat", 0))
                    act.dma_start(new_ckv[0, 0], ckv[:, 0, 0:KVL]).then_inc(stored, 16)
                    act.dma_start(new_krope[0, 0], ckv[:, 0, KVL:CK]).then_inc(stored, 16)

            act.sem_inc(xe_ready, CREDIT)
            act.sem_inc(ye_ready, CREDIT)
            act.wait_ge(*out_of("pos", 0))
            rounds = act.value_load(nri[0:1, :], min_val=1, max_val=ROUNDS)
            with act.Fori(0, rounds) as r:
                with act.Fori(0, PAIRS) as i:
                    k = r * PAIRS + i
                    for u in range(2):
                        act.wait_ge(e_used[2 * u + 1], k + CREDIT)
                        for hf in range(2):
                            act.wait_ge(gathered, 4 * k + 2 * u + hf + 1)
                            act.activation(xeT[u][:, 4 * hf:4 * hf + 4, :], banks[hf][:, 0:4 * T].rearrange("p (f t) -> p f t", t=T),
                                           ACT.Copy).then_inc(xe_ready, 1)
                    for u in range(2):
                        act.wait_ge(e_used[2 * u + 1], k + 1 + CREDIT)
                        act.activation(sil[u], banks[2][:, 0:HB * T].rearrange("p (f t) -> p f t", t=T), ACT.Silu).then_inc(sil_ready, 1)
                    for u in range(2):
                        act.wait_ge(scattered[u], k + CREDIT)
                        for hf in range(2):
                            if hf == 0:
                                act.wait_ge(y_done, 2 * k + u + 1)
                            else:
                                act.wait_ge(e_used[4 + u], k + 1 + CREDIT)
                            act.activation(ye[u][:, 512 * hf:512 * hf + 512], banks[4 + hf][0:T, :], ACT.Copy).then_inc(ye_ready, 1)
            for t in range(NT):
                act.wait_ge(final, t + 1)
                dst = y_prompt[0] if t == 0 else y_sample[0, (t - 1) * P:t * P]
                act.dma_start(dst, x[:, t, :]).then_inc(stored, 16)
            act.wait_ge(stored, 16 * 6)

        @block.vector
        def _(dve):
            steps = [0]

            def chain(ins):
                steps[0] += 1
                ins.then_inc(dve_chain, 1)
                dve.wait_ge(dve_chain, steps[0])

            def tt(out, a, b, op, **kw):
                return dve.tensor_tensor(out, a, b, op, **kw)

            def ts(out, a, s1, op0, s2=None, op1=None):
                if op1 is None:
                    return dve.tensor_scalar(out, a, s1, None, op0)
                return dve.tensor_scalar(out, a, s1, s2, op0, op1)

            def stt(out, a, s, b, op0, op1):
                return dve.scalar_tensor_tensor(out=out, in0=a, scalar=s, in1=b, op0=op0, op1=op1)

            def norm_x(col, n_root):
                dve.wait_ge(root, n_root)
                chain(dve.reciprocal(rs[:, col:col + NT], rs[:, col:col + NT]))
                for t in range(NT):
                    ts(xs[:, t, :], x[:, t, :], rs[:, col + t:col + t + 1], ALU.mult).then_inc(xs_ready, 1)

            def softplus_cols():
                dve.wait_ge(lru_exp, 1)
                z, w, w2, acc16, t16 = lam[:, 1, :], lam[:, 2, :], lam[:, 3, :], lam[:, 4, :], lam[:, 5, :]
                chain(ts(t16, z, 2.0, ALU.add))
                chain(dve.reciprocal(t16, t16))
                chain(tt(w, z, t16, ALU.mult))
                chain(tt(w2, w, w, ALU.mult))
                chain(ts(acc16, w2, 1.0 / 17, ALU.mult, 1.0 / 15, ALU.add))
                for odd in (13, 11, 9, 7, 5, 3, 1):
                    chain(tt(acc16, acc16, w2, ALU.mult))
                    chain(ts(acc16, acc16, 1.0 / odd, ALU.add))
                chain(tt(acc16, acc16, w, ALU.mult))
                chain(ts(t16, vb[:, LAM:LAM + 16], -1.0, ALU.mult, 0.0, ALU.max))
                chain(stt(acc16, acc16, 2.0, t16, ALU.mult, ALU.add))
                chain(ts(hbias, vb[:, BA:BA + 32], 0.5, ALU.mult))
                chain(ts(nhc, acc16, LRU_C / 2, ALU.mult))
                ts(hc, acc16, -LRU_C / 2, ALU.mult).then_inc(lru_cols, 1)

            def lru_finish(m):
                d, j = m % 2, m // 2
                cur = lru[:, m % 3]
                chain(stt(cur[:, 1, :], cur[:, 1, :], 1.0, xc[:, j, :], ALU.add, ALU.mult))
                dve.wait_ge(lru_root, m + 1)
                chain(tt(cur[:, 1, :], cur[:, 1, :], cur[:, 0, :], ALU.mult))
                for lo, hi, init in ((0, CTX, 0.0), (LAT0, PADTOK, vb[:, STATE + 8 * d + j:STATE + 8 * d + j + 1])):
                    a, bb, o = cur[:, 2, lo:hi], cur[:, 1, lo:hi], cur[:, 0, lo:hi]
                    if d:
                        a, bb, o = a[:, ::-1], bb[:, ::-1], o[:, ::-1]
                    chain(dve.tensor_tensor_scan(o, a, bb, init, ALU.mult, ALU.add))
                edge = cur[:, 0, CTX - 1:CTX] if d == 0 else cur[:, 0, 0:1]
                chain(dve.tensor_copy(st[:, 8 * d + j:8 * d + j + 1], edge))
                if d == 1:
                    fwd = lru[:, (m - 1) % 3]
                    if j == 0:
                        dve.wait_ge(filled, done("hT", KT - 1))
                    for lo, hi, s in PSEGS:
                        ins = tt(y[:, j, lo:hi], fwd[:, 0, lo + s:hi + s], cur[:, 0, lo + s:hi + s], ALU.add)
                        if lo == 0:
                            chain(ins)
                        else:
                            ins.then_inc(lru_done, 1)

            def head_norm(w):
                cur = work[:, w % 2]
                is_k = w >= 3
                tile = w - 3 if is_k else w
                if is_k:
                    chain(dve.tensor_copy(cur[:, :, NOPE:QK], ckv[:, tile, None, KVL:CK].to_broadcast([P, H, ROPE])))
                dve.wait_ge(work_ready, w)
                chain(tt(sq, cur, cur, ALU.mult))
                dve.tensor_reduce(ssh[:, w, :], sq, AX.X, ALU.add).then_inc(work_sq, 1)
                dve.wait_ge(work_root, w + 1)
                chain(dve.reciprocal(rsh[:, w, :], rsh[:, w, :]))
                chain(tt(cur, cur, rsh[:, w, :, None].to_broadcast([P, H, QK]), ALU.mult))
                last = tt(cur, cur, qk_g[:, int(is_k), None, :].to_broadcast([P, H, QK]), ALU.mult)
                if tile in (1, 2):
                    chain(last)
                    pair = cur[:, :, NOPE:QK].rearrange("p h (i two) -> p h i two", two=2)
                    x1, x2 = pair[:, :, :, 0], pair[:, :, :, 1]
                    tab = const[:, K_ROPE + 32 * (tile - 1):K_ROPE + 32 * tile]
                    co = tab[:, None, 0:16].to_broadcast([P, H, 16])
                    si = tab[:, None, 16:32].to_broadcast([P, H, 16])
                    for k, (a, b2) in enumerate(((x1, co), (x2, si), (x1, si), (x2, co))):
                        chain(tt(rt[:, k], a, b2, ALU.mult))
                    chain(tt(x1, rt[:, 0], rt[:, 1], ALU.subtract))
                    last = tt(x2, rt[:, 2], rt[:, 3], ALU.add)
                last.then_inc(work_ready, 1)

            def diag(row, c, hf, half):
                for b4 in range(4):
                    f = 4 * hf + b4
                    ins = ts(scratch[:, P * b4:P * b4 + P], ident, mcol[:, row + f, c:c + 1], ALU.mult, half, ALU.mult)
                    if b4 < 3:
                        chain(ins)
                ins.then_inc(diag_ready, 1)

            def first_max(one, v, m):
                chain(tt(one, v, m.to_broadcast([P, NT, 4]), ALU.is_equal))
                chain(tt(one, one, const[:, None, K_FIRST:K_FIRST + 4].to_broadcast([P, NT, 4]), ALU.mult))
                chain(dve.tensor_reduce(gz, one, AX.X, ALU.max))
                chain(tt(one, one, gz.to_broadcast([P, NT, 4]), ALU.is_equal))

            def route():
                gl = lg[:, :, 0:NG]
                chain(dve.tensor_reduce(gm, gl, AX.X, ALU.max))
                first_max(g1h, gl, gm)
                chain(tt(gsh, gl, gm.to_broadcast([P, NT, 4]), ALU.subtract))
                el = lg[:, :, NG:NR].rearrange("p t (g n) -> p t n g", g=NG)
                ep = eprod.rearrange("p t (n g) -> p t n g", g=NG)
                chain(tt(ep, el, g1h[:, :, None, :].to_broadcast([P, NT, EG, NG]), ALU.mult))
                chain(dve.tensor_reduce(ein, ep, AX.X, ALU.add))
                chain(dve.tensor_reduce(m1, ein, AX.X, ALU.max))
                first_max(o1, ein, m1)
                chain(stt(t4, o1, -1e30, ein, ALU.mult, ALU.add))
                chain(dve.tensor_reduce(m2, t4, AX.X, ALU.max))
                first_max(o2, t4, m2)
                tt(e21, m2, m1, ALU.subtract).then_inc(sel_ready, 1)
                dve.wait_ge(h2T_ready, KT + 1)
                chain(dve.tensor_reduce(gz, gsh, AX.X, ALU.add))
                chain(dve.reciprocal(gw, gz))
                chain(ts(gz, e21, 1.0, ALU.add))
                chain(dve.reciprocal(w1c, gz))
                chain(tt(w2c, w1c, e21, ALU.mult))
                chain(tt(w1c, w1c, gw, ALU.mult))
                chain(tt(w2c, w2c, gw, ALU.mult))
                chain(tt(wsel, o1, w1c.to_broadcast([P, NT, 4]), ALU.mult))
                chain(tt(t4, o2, w2c.to_broadcast([P, NT, 4]), ALU.mult))
                chain(tt(wsel, wsel, t4, ALU.add))
                chain(tt(ssel, o1, o2, ALU.add))
                sh = [P, NT, NG, EG]
                cv = comb.rearrange("p t (g n) -> p t g n", g=NG)
                sv = sel.rearrange("p t (g n) -> p t g n", g=NG)
                chain(tt(cv, g1h[:, :, :, None].to_broadcast(sh), wsel[:, :, None, :].to_broadcast(sh), ALU.mult))
                tt(sv, g1h[:, :, :, None].to_broadcast(sh), ssel[:, :, None, :].to_broadcast(sh), ALU.mult).then_inc(sel_ready, 1)

            dve.wait_ge(const_in, 16)
            dve.wait_ge(zeroed, 5)
            dve.wait_ge(row_in, 16 * 8)
            dve.wait_ge(x_in, 32)

            for n, (kind, which, who) in enumerate(plan):
                b = banks[n % 8]
                if who == "dve":
                    dve.wait_ge(filled, n + 1)
                if kind == "vec":
                    if which == 0:
                        dve.tensor_copy(va, b[:, 0:NVA]).then_inc(freed["dve"], 1)
                    else:
                        dve.tensor_copy(vb, b[:, 0:NVB]).then_inc(freed["dve"], 1)
                        dve.wait_ge(freed["dve"], 2)
                        ts(lam[:, 5, :], vb[:, LAM:LAM + 16], -1.0, ALU.mult).then_inc(cols_ready, 1)
                        dve.wait_ge(cols_ready, 1)
                        tt(lam[:, 0, :], vb[:, LAM:LAM + 16], lam[:, 5, :], ALU.max).then_inc(lru_ez, 1)
                        dve.wait_ge(tanhc_ready, 1)
                        chain(stt(tanh_c, tanh_c, 1.0, va[:, CVEC:CVEC + 2 * KT].rearrange("p (a b) -> p a b", a=2), ALU.add, ALU.mult))
                        ts(silu_c.rearrange("p f c -> p c f"), tanh_c, 0.5, ALU.mult).then_inc(silu_ready, 1)
                        norm_x(0, 1)
                        softplus_cols()
                elif kind == "mod":
                    c4 = 4 * which
                    pv = b[:, 0:8].rearrange("p (j c) -> p j c", c=2)
                    for c in range(2):
                        ins = tt(mcol[:, c4:c4 + 4, c], pv[:, :, c], va[:, BMOD + c4:BMOD + c4 + 4], ALU.add)
                        if c == 0:
                            chain(ins)
                        else:
                            ins.then_inc(freed["dve"], 1)
                    if which in (3, 9):
                        dve.wait_ge(freed["dve"], emptied_by[n][1])
                        row, nrm, out = (SC1, N1, scale1) if which == 3 else (SC2, N2, scale2)
                        chain(stt(out[:, :, 0], mcol[:, row:row + KT, 0], 1.0, va[:, nrm:nrm + KT], ALU.add, ALU.mult))
                        ins = stt(out[:, :, 1], mcol[:, row:row + KT, 1], 1.0, va[:, nrm:nrm + KT], ALU.add, ALU.mult)
                        if which == 3:
                            chain(ins)
                        else:
                            ins.then_inc(scale2_ready, 1)
                elif kind == "hT":
                    f = which
                    for c, lo, hi in SEGS:
                        ins = ts(hT[:, f, lo:hi], b[:, lo:hi], scale1[:, f, c:c + 1], ALU.mult, mcol[:, SH1 + f, c:c + 1], ALU.add)
                        ins.then_inc(hT_ready if c == 0 else freed["dve"], 1)
                elif kind == "xrnn":
                    j = which
                    dve.wait_ge(xpad_ready, j + 1)
                    dve.wait_ge(freed["act"], emptied_by[n][1])
                    src = xpad[j % 2]
                    w = [va[:, CONVW + 8 * k + j:CONVW + 8 * k + j + 1] for k in range(4)]
                    chain(ts(xc[:, j, :], src[:, 0:PADTOK], w[0], ALU.mult, va[:, CONVB + j:CONVB + j + 1], ALU.add))
                    for k in range(1, 4):
                        ins = stt(xc[:, j, :], src[:, k:k + PADTOK], w[k], xc[:, j, :], ALU.mult, ALU.add)
                        if k < 3:
                            chain(ins)
                    ins.then_inc(conv_done, 1)
                elif kind == "qlat":
                    t = which
                    dve.wait_ge(root, 2 + t)
                    chain(dve.reciprocal(rs[:, 3 + t:4 + t], rs[:, 3 + t:4 + t]))
                    stt(qln[:, t, :], b[:, 0:QL], rs[:, 3 + t:4 + t], qan, ALU.mult, ALU.mult).then_inc(freed["dve"], 1)
                elif kind == "kvlat":
                    t = which
                    dve.wait_ge(root, 5 + t)
                    chain(dve.reciprocal(rs[:, 6 + t:7 + t], rs[:, 6 + t:7 + t]))
                    chain(stt(ckv[:, t, 0:KVL], b[:, 0:KVL], rs[:, 6 + t:7 + t], kvan, ALU.mult, ALU.mult))
                    dve.tensor_copy(ckv[:, t, KVL:CK], b[:, KVL:CK]).then_inc(freed["dve"], 1)
                elif kind == "lru" and which[1] == 1:
                    m = which[0]
                    cur = lru[:, m % 3]
                    dve.wait_ge(lru_ez, 2 + m)
                    dve.wait_ge(lru_q, m)
                    chain(tt(lru_sq, cur[:, 2, :], cur[:, 2, :], ALU.mult))
                    stt(cur[:, 0, :], lru_sq, 1.0, cur[:, 0, :], ALU.add, ALU.mult).then_inc(lru_q, 1)
                    if m >= 1:
                        lru_finish(m - 1)
                elif kind == "qlT" and which == 0:
                    lru_finish(15)
                elif (kind == "uq" and which[1] == 1) or kind == "uk":
                    w = which[0] if kind == "uq" else which + 3
                    dve.wait_ge(freed["act"], emptied_by[n][1])
                    if w == 0:
                        dve.wait_ge(cache_in, 32)
                        dve.wait_ge(*out_of("kvlat", NT - 1))
                    head_norm(w)
                elif kind == "grnn":
                    dve.wait_ge(freed["act"], emptied_by[n][1])
                    tt(y[:, which, :], y[:, which, :], gtmp[:, which % 2, :], ALU.mult).then_inc(y_ready, 1)
                elif kind == "score":
                    i = which
                    nk = CTX if UNITS[i][1] == 0 else NTOK
                    dve.wait_ge(filled, n + 1)
                    chain(dve.tensor_reduce(rmax[:, i:i + 1], b[:, 0:nk], AX.X, ALU.max))
                    ts(rmax[:, i:i + 1], rmax[:, i:i + 1], -QK ** -0.5, ALU.mult).then_inc(nmax_ready, 1)
                    dve.wait_ge(freed["act"], emptied_by[n][1])
                    chain(dve.reciprocal(rsum[:, i:i + 1], rsum[:, i:i + 1]))
                    ts(prob[:, i % 3, 0:nk], prob[:, i % 3, 0:nk], rsum[:, i:i + 1], ALU.mult).then_inc(prob_ready, 1)
                elif kind == "pv":
                    h, q = UNITS[which]
                    lo = 64 * (h % 2)
                    dve.tensor_copy(yatt[lo:lo + 64, h // 2, q * P:(q + 1) * P], b[lo:lo + 64, 0:P]).then_inc(freed["dve"], 1)
                elif kind in ("gb1", "gb2"):
                    c, hf = which
                    if n and plan[n - 1][0] == kind:
                        dve.wait_ge(filled, n)
                    else:
                        dve.wait_ge(filled, n)
                    if kind == "gb1":
                        diag(G1, c, hf, 0.5)
                    else:
                        diag(G2, c, hf, 1.0)
                elif kind == "ornn":
                    if which == 0:
                        dve.wait_ge(filled, done("score", len(UNITS) - 1))
                    dve.wait_ge(*out_of("gate", which))
                    stt(merged[:, which, :], gbuf[:, which, :], 1.0, b[:, 0:NTOK], ALU.add, ALU.mult).then_inc(freed["dve"], 1)
                elif kind == "omla":
                    dve.wait_ge(*out_of("gate", 8 + which))
                    stt(gbuf[:, which, :], gbuf[:, which, :], 1.0, b[:, 0:NTOK], ALU.add, ALU.mult).then_inc(freed["dve"], 1)
                    dve.wait_ge(freed["dve"], emptied_by[n][1])
                    tt(merged[:, which, :], merged[:, which, :], gbuf[:, which, :], ALU.add).then_inc(merged_ready, 1)
                elif kind == "mix":
                    hf, t = which
                    dve.wait_ge(*out_of("gb1", (1, 1)))
                    if which == (0, 0):
                        dve.wait_ge(filled, done("gb1", (1, 1)))
                    seg = slice(512 * hf, 512 * hf + 512)
                    dve.wait_ge(x_ready, 3 * hf + t)
                    tt(scratch, b[:, :], bc[:, min(t, 1), seg], ALU.mult).then_inc(freed["dve"], 1)
                    dve.wait_ge(freed["dve"], emptied_by[n][1])
                    tt(x[:, t, seg], x[:, t, seg], scratch, ALU.add).then_inc(x_ready, 1)
                    if which == (1, NT - 1):
                        norm_x(9, 8)
                elif kind == "logit":
                    dve.memset(acc, 0.0).then_inc(acc_step, 1)
                    tt(lg, b[:, 0:NT * NR].rearrange("p (t n) -> p t n", n=NR), router_b[:, None, :].to_broadcast([P, NT, NR]), ALU.add)\
                        .then_inc(freed["dve"], 1)
                    dve.wait_ge(freed["dve"], emptied_by[n][1])
                    route()
                elif kind == "pos":
                    cnt = b[:, 64:64 + NE]
                    chain(dve.tensor_reduce(cmax, cnt, AX.X, ALU.max))
                    pb = b[:, 0:NT * NE].rearrange("p (t n) -> p t n", n=NE)
                    chain(stt(posm, pb, 1.0, sel, ALU.add, ALU.mult))
                    chain(ts(posm, posm, -1.0, ALU.add))
                    chain(ts(rcount, const[:, K_THR:K_THR + ROUNDS], cmax, ALU.is_lt))
                    chain(dve.tensor_reduce(nrf, rcount, AX.X, ALU.add))
                    dve.tensor_copy(nri, nrf).then_inc(freed["dve"], 1)
                    dve.wait_ge(freed["dve"], emptied_by[n][1])

            dve.sem_inc(he_ready, CREDIT)
            rounds = dve.value_load(nri[0:1, :], min_val=1, max_val=ROUNDS)
            with dve.Fori(0, rounds) as r:
                with dve.Fori(0, PAIRS) as i:
                    k = r * PAIRS + i
                    for u in range(2):
                        dve.wait_ge(swt_done[u], k + CREDIT)
                        dve.tensor_copy(pcur[:, u, :], posm[:, :, bass.ds(2 * i + u, 1)].rearrange("p t e -> p (t e)")).then_inc(pos_cur, 1)
                        dve.tensor_copy(ccur[:, u, :], comb[:, :, bass.ds(2 * i + u, 1)].rearrange("p t e -> p (t e)")).then_inc(pos_cur, 1)
                        dve.wait_ge(pos_cur, 4 * k + 2 * u + 2)
                        for t in range(NT):
                            ts(S[u][:, t, :], iota, pcur[:, u, t:t + 1], ALU.is_equal).then_inc(S_ready, 1)
                        for t in range(NT):
                            ts(SW[u][:, t, :], iota, pcur[:, u, t:t + 1], ALU.is_equal, ccur[:, u, t:t + 1], ALU.mult).then_inc(S_ready, 1)
                    for u in range(2):
                        dve.wait_ge(scattered[u], k + CREDIT)
                        dve.wait_ge(swt_done[u], k + 1 + CREDIT)
                        dve.tensor_copy(SWT[u], banks[6 + u][0:T, 0:NTOK]).then_inc(swt_ready, 1)
                    for u in range(2):
                        dve.wait_ge(sil_ready, 2 * k + u + 1)
                        dve.wait_ge(e_used[4 + u], k + CREDIT)
                        tt(heT[u], sil[u], banks[3][:, 0:HB * T].rearrange("p (f t) -> p f t", t=T), ALU.mult).then_inc(he_ready, 1)
                    for u in range(2):
                        for s in range(6):
                            t, hf = s // 2, s % 2
                            m = 2 + 6 * u + s
                            if s < 5:
                                dve.wait_ge(sc_done, 10 * k + 5 * u + s + 1)
                            else:
                                dve.wait_ge(scattered[u], k + 1 + CREDIT)
                            dve.wait_ge(acc_step, 12 * k + 1 if u == 0 else 12 * k + s + 2)
                            part = acc[:, t, 512 * hf:512 * hf + 512]
                            tt(part, part, banks[6 + m % 2][:, :], ALU.add).then_inc(acc_step, 1)
                dve.wait_ge(S_ready, (r + 1) * PAIRS * 12)
                dve.tensor_scalar(posm, posm, -float(T), None, ALU.add).then_inc(pos_round, 1)
                dve.wait_ge(pos_round, r + 1)
            dve.wait_ge(acc_step, rounds * (12 * PAIRS) + 1)
            for t in range(NT):
                chain(tt(acc[:, t, :], acc[:, t, :], bc[:, min(t, 1), :], ALU.mult))
                tt(x[:, t, :], x[:, t, :], acc[:, t, :], ALU.add).then_inc(final, 1)

        @block.tensor
        def _(pe):
            va_row, vb_row = mem[0:NVA, at_qln:at_qln + P], mem[0:NVB, at_qln + P:at_qln + 2 * P]

            def weights(key):
                n = chunk_no[key]
                extra = sum(1 for k in chunks[:n + 1] if k[0] == "ukv" and chunk_no[k] % RING == n % RING)
                pe.wait_ge(loaded[n % RING], 16 * (n // RING + 1 + extra))
                return chunk_ap(key)

            pe.wait_ge(const_in, 16)
            pe.wait_ge(vec_in, 16 * 11)
            pe.wait_ge(zeroed, 5)
            for n, (kind, which, who) in enumerate(plan):
                b = banks[n % 8]
                if n >= 8:
                    w, c = emptied_by[n - 8]
                    pe.wait_ge(freed[w], c)
                mm = None
                if kind == "vec":
                    src, rows = (va_row, NVA) if which == 0 else (vb_row, NVB)
                    mm = pe.transpose(b[:, 0:rows], src, ident[0:rows, 0:rows])
                elif kind == "mod":
                    if which == 0:
                        pe.wait_ge(silu_ready, 1)
                    w = weights(("mod", which))
                    for jb in range(4):
                        for f in range(KT):
                            mm = pe.matmul(b[:, 2 * jb:2 * jb + 2], w[:, f, P * jb:P * jb + P], silu_c[:, f, :],
                                           start=(f == 0), stop=(f == KT - 1))
                elif kind in ("hT", "h2T"):
                    pe.wait_ge(xs_ready, NT if kind == "hT" else 2 * NT)
                    for t in range(NT):
                        mm = pe.transpose(b[:, t * P:t * P + P], xs[:, t, which * P:which * P + P], ident)
                elif kind in ("xrnn", "grnn", "gate", "ornn"):
                    if kind == "xrnn" and which == 0:
                        pe.wait_ge(hT_ready, KT)
                        pe.wait_ge(*out_of("hT", KT - 1))
                    if kind == "ornn" and which == 0:
                        pe.wait_ge(y_ready, KT)
                    w = weights((kind, which // 4))
                    src = y if kind == "ornn" else hT
                    for f in range(KT):
                        mm = pe.matmul(b[:, 0:NTOK], w[:, f, P * (which % 4):P * (which % 4) + P], src[:, f, :],
                                       start=(f == 0), stop=(f == KT - 1))
                elif kind in ("qlat", "kvlat"):
                    w = weights((kind, 0))
                    width = QL if kind == "qlat" else CK
                    for f in range(KT):
                        mm = pe.matmul(b[:, 0:width], hT[:, f, which * P:which * P + P], w[:, f, :], start=(f == 0), stop=(f == KT - 1))
                elif kind == "lru":
                    m, s = which
                    if m == 0 and s == 0:
                        pe.wait_ge(lruw_in, 16 * 8)
                        pe.wait_ge(conv_done, KT)
                    j, d = m // 2, m % 2
                    mm = pe.matmul(b[:, 0:PADTOK], lruw[:, 4 * j + 2 * d + s, :], xc[:, j, :], start=True, stop=True)
                elif kind == "qlT":
                    pe.wait_ge(*out_of("qlat", NT - 1))
                    for t in range(NT):
                        mm = pe.transpose(b[:, t * P:t * P + P], qln[:, t, which * P:which * P + P], ident)
                elif kind == "ckvT":
                    pe.wait_ge(*out_of("kvlat", NT - 1))
                    pe.wait_ge(cache_in, 32)
                    for t in range(4):
                        mm = pe.transpose(b[:, t * P:t * P + P], ckv[:, t, which * P:which * P + P], ident)
                elif kind == "uq":
                    t, hf = which
                    pe.wait_ge(*out_of("qlT", 2))
                    w = weights(("uq", 0))
                    for f in range(3):
                        mm = pe.matmul(b[:, 0:4 * QK], qlT[:, f, t * P:t * P + P], w[:, f, 4 * QK * hf:4 * QK * (hf + 1)],
                                       start=(f == 0), stop=(f == 2))
                elif kind in ("uk", "uv"):
                    pe.wait_ge(*out_of("ckvT", 1))
                    w = weights(("ukv", 0))
                    for f in range(2):
                        mm = pe.matmul(b[:, :], ckvT[:, f, which * P:which * P + P], w[:, f + (2 if kind == "uv" else 0), :],
                                       start=(f == 0), stop=(f == 1))
                elif kind == "qkT":
                    wi, hf = which
                    pe.wait_ge(work_ready, wi + 1)
                    for h4 in range(4):
                        mm = pe.transpose(b[0:QK, h4 * P:h4 * P + P], work[:, wi % 2, 4 * hf + h4, :], ident)
                elif kind == "score":
                    h, q = UNITS[which]
                    pe.wait_ge(*out_of("qkT", (6, 1)))
                    lo, hi = (0, P) if q == 0 else (P, 4 * P)
                    mm = pe.matmul(b[:, 0:hi - lo], qT[0:QK, h, q * P:q * P + P], kT[0:QK, h, lo:hi], start=True, stop=True)
                elif kind == "pT":
                    q = UNITS[which][1]
                    pe.wait_ge(prob_ready, which + 1)
                    for t in range(1 if q == 0 else 3):
                        mm = pe.transpose(b[:, t * P:t * P + P], prob[:, which % 3, t * P:t * P + P], ident)
                elif kind == "pv":
                    h, q = UNITS[which]
                    pe.wait_ge(*out_of("pT", which))
                    lo = 64 * (h % 2)
                    tiles = [0] if q == 0 else [1, 2, 3]
                    for z, t in enumerate(tiles):
                        mm = pe.matmul(b[lo:lo + 64, 0:P], values[:, t, V * h:V * h + V], pT[:, which % 2, z * P:z * P + P],
                                       start=(z == 0), stop=(z == len(tiles) - 1))
                elif kind in ("gb1", "gb2"):
                    c, hf = which
                    pe.wait_ge(diag_ready, (4 if kind == "gb2" else 0) + 2 * c + hf + 1)
                    mm = pe.matmul(b[:, :], ones, scratch, start=True, stop=True)
                elif kind == "omla":
                    if which == 0:
                        pe.wait_ge(*out_of("pv", len(UNITS) - 1))
                    w = weights(("omla", 0))
                    for f in range(4):
                        mm = pe.matmul(b[:, 0:NTOK], w[:, f, which * P:which * P + P], yatt[:, f, :], start=(f == 0), stop=(f == 3))
                elif kind == "mix":
                    hf, t = which
                    pe.wait_ge(merged_ready, KT)
                    w = weights(("wout", hf))
                    for f in range(KT):
                        mm = pe.matmul(b[:, :], merged[:, f, t * P:t * P + P], w[:, f, :], start=(f == 0), stop=(f == KT - 1))
                elif kind == "state":
                    pe.wait_ge(lru_done, 8)
                    mm = pe.transpose(b[0:16, 0:P], st, ident)
                elif kind == "logit":
                    pe.wait_ge(*out_of("h2T", KT - 1))
                    pe.wait_ge(h2T_ready, KT)
                    for t in range(NT):
                        for f in range(KT):
                            mm = pe.matmul(b[:, NR * t:NR * t + NR], hT[:, f, t * P:t * P + P], router_w[:, f, :],
                                           start=(f == 0), stop=(f == KT - 1))
                elif kind == "h2tok":
                    t, hf = which
                    for f4 in range(4):
                        mm = pe.transpose(b[:, f4 * P:f4 * P + P], hT[:, 4 * hf + f4, t * P:t * P + P], ident)
                elif kind == "pos":
                    pe.wait_ge(sel_ready, 2)
                    for t in range(NT):
                        for t2 in range(t + 1):
                            pe.matmul(b[:, NE * t:NE * t + NE], upper if t2 == t else ones, sel[:, t2, :],
                                      start=(t2 == 0), stop=(t2 == t))
                    for t2 in range(NT):
                        mm = pe.matmul(b[:, 64:64 + NE], ones, sel[:, t2, :], start=(t2 == 0), stop=(t2 == NT - 1))
                mm.then_inc(filled, 1)

            for w in ("act", "dve"):
                pe.wait_ge(freed[w], count[w])
            for s in e_used + swt_done + scattered:
                pe.sem_inc(s, CREDIT)
            pe.wait_ge(*out_of("pos", 0))
            rounds = pe.value_load(nri[0:1, :], min_val=1, max_val=ROUNDS)
            ew = [view(slot_at[expert_slots[j]], KT, HID) for j in range(4)] + \
                 [view(slot_at[expert_slots[j]], HB, D) for j in (4, 5)]
            with pe.Fori(0, rounds) as r:
                with pe.Fori(0, PAIRS) as i:
                    k = r * PAIRS + i
                    for u in range(2):
                        pe.wait_ge(S_ready, 12 * k + 6 * u + 6)
                        pe.wait_ge(xe_ready, 4 * k + 2 * u + CREDIT)
                        for f in range(KT):
                            for t in range(NT):
                                mm = pe.matmul(banks[f // 4][:, T * (f % 4):T * (f % 4) + T], h2[:, t, f * P:f * P + P], S[u][:, t, :],
                                               start=(t == 0), stop=(t == NT - 1))
                            if f % 4 == 3:
                                mm.then_inc(gathered, 1)
                    for u in range(2):
                        if u == 0:
                            pe.wait_ge(acc_step, 12 * k + 1)
                        for t in range(NT):
                            mm = pe.transpose(banks[6 + u][0:T, t * P:t * P + P], SW[u][:, t, :], ident)
                        mm.then_inc(swt_done[u], 1)
                    for u in range(2):
                        pe.wait_ge(xe_ready, 4 * k + 2 * u + 2 + CREDIT)
                        pe.wait_ge(he_ready, 2 * k + u + CREDIT)
                        for s in range(2):
                            j = 2 * u + s
                            pe.wait_ge(e_loaded[j], 16 * k + 16)
                            for m in range(HB):
                                for f in range(KT):
                                    mm = pe.matmul(banks[2 + s][:, T * m:T * m + T], ew[j][:, f, m * P:m * P + P], xeT[u][:, f, :],
                                                   start=(f == 0), stop=(f == KT - 1))
                            mm.then_inc(e_used[j], 1)
                    for u in range(2):
                        pe.wait_ge(he_ready, 2 * k + u + 1 + CREDIT)
                        pe.wait_ge(e_loaded[4 + u], 16 * k + 16)
                        pe.wait_ge(ye_ready, 4 * k + 2 * u + CREDIT)
                        for hf in range(2):
                            for m in range(HB):
                                mm = pe.matmul(banks[4 + hf][0:T, :], heT[u][:, m, :], ew[4 + u][:, m, 512 * hf:512 * hf + 512],
                                               start=(m == 0), stop=(m == HB - 1))
                            mm.then_inc(y_done if hf == 0 else e_used[4 + u], 1)
                    for u in range(2):
                        pe.wait_ge(ye_ready, 4 * k + 2 * u + 2 + CREDIT)
                        for s in range(6):
                            t, hf = s // 2, s % 2
                            m = 2 + 6 * u + s
                            if m < 4:
                                pe.wait_ge(swt_ready, 2 * k + m - 1)
                            else:
                                pe.wait_ge(acc_step, 12 * k + m - 2)
                            mm = pe.matmul(banks[6 + m % 2][:, :], SWT[u][:, t * P:t * P + P], ye[u][:, 512 * hf:512 * hf + 512],
                                           start=True, stop=True)
                            mm.then_inc(sc_done if s < 5 else scattered[u], 1)


_NAMES = ['x_prompt', 'x_sample', 'cache_mla_ckv', 'cache_mla_krope', 'state_rglru', 'c', 'c_ctx', 'norm1_g', 'norm2_g',
          'w_mod', 'b_mod', 'w_in', 'conv_w', 'conv_b', 'lru_wa', 'lru_ba', 'lru_wx', 'lru_bx', 'lru_lam', 'q_a_norm',
          'kv_a_norm', 'w_uq', 'w_uk', 'w_uv', 'q_norm', 'k_norm', 'w_o_rnn', 'w_o_mla', 'w_out', 'router_wg', 'router_bg',
          'router_we', 'router_be', 'exp_w1', 'exp_w3', 'exp_w2']
_OUTS = [(1, CTX, D), (1, LAT, D), (1, 1, CTX, KVL), (1, 1, CTX, ROPE), (1, 1, 2, D)]


def shape_constants():
    import numpy as np
    k = np.zeros((P, NK), np.float32)
    k[:, K_ID:K_ID + P] = np.eye(P)
    k[:, K_UP:K_UP + P] = np.triu(np.ones((P, P)), 1)
    k[:, K_IOTA:K_IOTA + T] = np.arange(T)
    token = np.arange(LAT)
    inv = (10000.0 ** (-np.arange(0, 16, 2, dtype=np.float32) / 16)).astype(np.float32)
    ang = np.concatenate([(token // 64).astype(np.float32)[:, None] * inv, (token % 64).astype(np.float32)[:, None] * inv], -1)
    tab = np.concatenate([np.cos(ang), np.sin(ang)], -1).astype(np.float32)
    k[:, K_ROPE:K_ROPE + 32] = tab[:P]
    k[:, K_ROPE + 32:K_ROPE + 64] = tab[P:]
    k[:, K_FIRST:K_FIRST + 4] = [4, 3, 2, 1]
    k[:, K_THR:K_THR + ROUNDS] = T * np.arange(ROUNDS)
    return k


def kernel(**inputs):
    import numpy as _np
    import concourse.bacc as _bacc
    from concourse import mybir as _mybir
    from concourse.bass_utils import run_bass_kernel_spmd as _run

    nc = _bacc.Bacc("TRN2", target_bir_lowering=False, num_devices=1)
    arrays, io = {}, {}
    for name in _NAMES:
        arrays[f"in_{name}"] = _np.ascontiguousarray(inputs[name])
    arrays["in_consts"] = shape_constants()
    for key, a in arrays.items():
        io[key[3:]] = nc.dram_tensor(key, a.shape, _mybir.dt.from_np(a.dtype), kind="ExternalInput").ap()
    outs = [nc.dram_tensor(f"out_{i}", s, _mybir.dt.float32, kind="ExternalOutput").ap() for i, s in enumerate(_OUTS)]
    hybrid_step(nc, io, *outs)
    r = _run(nc, [arrays], core_ids=[0])
    return tuple(r.results[0][f"out_{i}"] for i in range(len(_OUTS)))
```

```python
from contextlib import ExitStack

import concourse.bass as bass
from concourse import mybir

ALU = mybir.AluOpType
ACT = mybir.ActivationFunctionType
AX = mybir.AxisListType
F32 = mybir.dt.float32
F32R = mybir.dt.float32r
I32 = mybir.dt.int32

P = 128
D = 1024
KT = D // P
CTX, LAT = 128, 256
NTOK = CTX + LAT
NT = NTOK // P
PADTOK = NTOK + 2
LAT0 = CTX + 2
H, NOPE, ROPE, QK, V = 8, 64, 32, 96, 64
QL, KVL = 384, 256
CK = KVL + ROPE
LRU_C = 8.0
EPS = 1e-6
NE, NG, EG, HID = 16, 4, 4, 512
NR = NG + NE
T = 96
ROUNDS = -(-NTOK // T)
CREDIT = 1
PAIRS = NE // 2
HB = HID // P
C_G, C_Q, C_KV, C_GATE = D, 2 * D, 2 * D + QL, 2 * D + QL + CK
BASE = 16512
PIECE = 2
PIECES = KT // PIECE
PRING = 4
SLOT = 4096
RING = 4
SEGS = ((0, 0, CTX), (1, CTX, NTOK))
PSEGS = ((0, CTX, 0), (CTX, NTOK, 2))

BMOD, N1, N2, CVEC, CONVW, CONVB, NVA = 0, 48, 56, 64, 80, 112, 120
BA, BX, LAM, STATE, NVB = 0, 16, 32, 48, 64
SH1, SC1, G1, SH2, SC2, G2 = (8 * i for i in range(6))
K_ID, K_UP, K_IOTA, K_ROPE, K_FIRST, K_THR, NK = 0, P, 2 * P, 2 * P + T, 2 * P + T + 64, 2 * P + T + 68, 2 * P + T + 68 + ROUNDS
UNITS = [(h, q) for h in range(H) for q in range(NT)]


def stream_plan():
    plan = [("mod", c) for c in range(4)]
    plan += [("xrnn", 0), ("xrnn", 1), ("qlat", 0), ("kvlat", 0)]
    plan += [("mod", c) for c in range(4, 12)]
    plan += [("uq", 0), ("ukv", 0), ("grnn", 0), ("grnn", 1)]
    plan += [("gate", 0), ("ornn", 0), ("gate", 1), ("ornn", 1), ("gate", 2), ("gate", 3), ("omla", 0)]
    plan += [("wout", 0), ("wout", 1)]
    return plan


def psum_plan():
    g = [("vec", 0, "dve"), ("vec", 1, "dve")]
    for c in range(4):
        g += [("mod", c, "act")] + ([("modT", c - 1, "dve")] if c else [])
    g += [("modT", 3, "dve")]
    g += [("hT", f, "dve") for f in range(KT)]
    g += [("xrnn", j, "act") for j in range(KT)]
    g += [("qlat", t, "dve") for t in range(NT)] + [("kvlat", t, "dve") for t in range(NT)]
    for n in range(16):
        g += [("lru", (n, s), "act") for s in range(2)]
        if n % 2 == 1:
            g += [("mod", 4 + n // 2, "act"), ("modT", 4 + n // 2, "dve")]
    g += [("qlT", f, "act") for f in range(3)] + [("ckvT", f, "act") for f in range(2)]
    for n in range(8):
        if n < 3:
            g += [("uq", (n, 0), "act"), ("uq", (n, 1), "act")]
        elif n < 7:
            g += [("uk", n - 3, "act"), ("uv", n - 3, "act")]
        if n >= 1:
            g += [("qkT", (n - 1, 0), "act"), ("qkT", (n - 1, 1), "act")]
    g += [("grnn", j, "act") for j in range(KT)]
    for i in range(len(UNITS) + 3):
        if i < len(UNITS):
            g += [("score", i, "act")]
        if 0 <= i - 2 < len(UNITS):
            g += [("pT", i - 2, "act")]
        if i >= 3:
            g += [("pv", i - 3, "dve")]
    g += [("gb1", (c, hf), "act") for c in range(2) for hf in range(2)]
    for c in range(2):
        g += [("gate", 4 * c + b, "act") for b in range(4)] + [("ornn", 4 * c + b, "dve") for b in range(4)]
    g += [("gate", 8 + b, "act") for b in range(8)] + [("omla", b, "dve") for b in range(8)]
    g += [("mix", (hf, t), "dve") for hf in range(2) for t in range(NT)]
    g += [("state", 0, "act")]
    g += [("h2T", f, "act") for f in range(KT)]
    g += [("logit", 0, "dve")]
    g += [("h2tok", (t, hf), "dve") for t in range(NT) for hf in range(2)]
    g += [("gb2", (c, hf), "act") for c in range(2) for hf in range(2)]
    g += [("pos", 0, "dve")]
    return g


def hybrid_step(nc, io, y_prompt, y_sample, new_ckv, new_krope, new_state):
    chunks = stream_plan()
    chunk_no = {key: n for n, key in enumerate(chunks)}
    plan = psum_plan()
    group_no = {(k, i): n for n, (k, i, _) in enumerate(plan)}
    emptied_by = []
    count = {"act": 0, "dve": 0}
    for _, _, who in plan:
        count[who] += 1
        emptied_by.append((who, count[who]))

    with ExitStack() as ctx:
        floats = 53200
        mem = nc.alloc_sbuf_tensor_at("mem", [P, floats], F32, offset=BASE)
        banks = [ctx.enter_context(nc.psum_tensor(f"bank{b}", [P, 512], F32)) for b in range(8)]

        def sem(name):
            return ctx.enter_context(nc.semaphore(name))

        top = [0]

        def take(n):
            at = top[0]
            top[0] += -(-n // 8) * 8
            assert top[0] <= floats, top[0]
            return at

        def view(at, *dims):
            n = 1
            for d in dims:
                n *= d
            ap = mem[:, at:at + n]
            if len(dims) == 2:
                ap = ap.rearrange("p (a b) -> p a b", a=dims[0])
            if len(dims) == 3:
                ap = ap.rearrange("p (a b c) -> p a b c", a=dims[0], b=dims[1])
            return ap

        ring_at = [take(SLOT) for _ in range(RING)]
        extra_at = top[0]
        at_q = take(H * NTOK)
        qT = view(at_q, H, NTOK)
        xpad = [view(at_q + 400 * b, 3 + PADTOK) for b in range(2)]
        values = view(take(4 * H * V), 4, H * V)
        at_work = take(2 * H * QK)
        work = view(at_work, 2, H, QK)
        yatt = view(at_work, 4, NTOK)
        mrow = [view(at_work + 512 * b, 512)[0:2] for b in range(2)]
        lru_at = take(9 * PADTOK)
        lru = view(lru_at, 3, 3, PADTOK)
        gtmp = view(lru_at, 2, NTOK)
        lru_sq = view(take(PADTOK), PADTOK)
        at_x = top[0]
        x = view(take(NT * D), NT, D)
        at_hT = take(KT * NTOK)
        hT = view(at_hT, KT, NTOK)
        at_xc = take(KT * PADTOK)
        xc = view(at_xc, KT, PADTOK)
        gbuf = view(at_xc, KT, NTOK)
        acc = view(at_xc, NT, D)
        at_y = take(KT * NTOK)
        xs = view(at_y, NT, D)
        y = view(at_y, KT, NTOK)
        at_kl = take(SLOT)
        kT = view(at_kl, H, 512)
        lruw = view(at_kl, 32, P)
        merged = view(at_kl, KT, NTOK)
        at_qln = take(NT * QL)
        qln = view(at_qln, NT, QL)
        prob = view(at_qln, 3, NTOK)
        ckv = view(take(4 * CK), 4, CK)
        at_qlT = take(3 * NTOK)
        qlT = view(at_qlT, 3, NTOK)
        pT = view(at_qlT, 2, NTOK)
        scratch = view(at_qlT, 512)
        ckvT = view(take(2 * 512), 2, 512)
        moe_end = top[0]
        bc = view(take(2 * D), 2, D)
        mcol = view(take(96), 48, 2)
        va = view(take(NVA), NVA)
        vb = view(take(NVB), NVB)
        silu_c = view(take(16), KT, 2)
        tanh_c = view(take(16), 2, KT)
        scale1 = view(take(16), KT, 2)
        scale2 = view(take(16), KT, 2)
        hbias = view(take(32), 32)
        lam = view(take(16 * 6), 6, 16)
        hc = view(take(16), 16)
        nhc = view(take(16), 16)
        const = view(take(NK), NK)
        ident = const[:, K_ID:K_ID + P]
        upper = const[:, K_UP:K_UP + P]
        iota = const[:, K_IOTA:K_IOTA + T]
        ones = view(take(P), P)
        qan = view(take(QL), QL)
        kvan = view(take(KVL), KVL)
        qk_g = view(take(2 * QK), 2, QK)
        router_b = view(take(NR), NR)
        router_w = view(take(KT * NR), KT, NR)
        ss = view(take(16), 16)
        rs = view(take(16), 16)
        ssh = view(take(56), 7, H)
        rsh = view(take(56), 7, H)
        rmax = view(take(24), 24)
        rsum = view(take(24), 24)
        eps = view(take(1), 1)
        st = view(take(16), 16)
        st_row = view(take(P), P)
        tmp_at = take(H * QK)
        sq = view(tmp_at, H, QK)
        rt = view(tmp_at, 4, H, ROPE // 2)
        at = [tmp_at]

        def small(*dims):
            n = 1
            for d in dims:
                n *= d
            at[0] += n
            assert at[0] <= tmp_at + H * QK
            return view(at[0] - n, *dims)

        lg = small(NT, NR)
        gm, gz, m1, m2, w1c, w2c, e21, gw = (small(NT, 1) for _ in range(8))
        gsh, g1h, ein, o1, o2, t4, wsel, ssel = (small(NT, EG) for _ in range(8))
        eprod, sel, comb, posm = (small(NT, NE) for _ in range(4))
        rcount = small(ROUNDS)
        cmax, nrf = small(1), small(1)
        nri = mem[:, at[0]:at[0] + 1].bitcast(I32)
        small(1)
        pcur, ccur = (small(2, NT) for _ in range(2))
        nf = len(chunks)
        spare = ring_at[nf % RING]
        raw_at = [extra_at, extra_at + SLOT, spare]
        late = [ring_at[(nf + i) % RING] for i in (1, 2, 3)]

        def rounded(name, at, *dims):
            n = 1
            for d in dims:
                n *= d
            full = nc.alloc_sbuf_tensor_at(name, [P, n], F32R, offset=BASE + 4 * at)
            ap = full[:, :]
            if len(dims) == 2:
                ap = ap.rearrange("p (a b) -> p a b", a=dims[0])
            return ap

        w_hi = [rounded(f"w_hi{i}", late[0] + 1024 * i, PIECE, HID) for i in range(PRING)]
        w_lo = [rounded(f"w_lo{i}", late[1] + 1024 * i, PIECE, HID) for i in range(PRING)]
        xe_hi = [rounded(f"xe_hi{u}", late[2] + KT * T * u, KT, T) for u in range(2)]
        xe_lo = [rounded(f"xe_lo{u}", late[2] + KT * T * (2 + u), KT, T) for u in range(2)]
        heT = [view(late[2] + KT * T * 4 + HB * T * u, HB, T) for u in range(2)]
        assert KT * T * 4 + 2 * HB * T <= SLOT
        h2_hi = rounded("h2_hi", at_y, NT, D)
        h2_lo = rounded("h2_lo", at_kl, NT, D)
        at = [at_qln]

        def after(n, end):
            start = at[0]
            at[0] += -(-n // 8) * 8
            assert at[0] <= end
            return start

        ye_hi = [rounded(f"ye_hi{u}", after(D, moe_end), D)[0:T] for u in range(2)]
        ye_lo = [rounded(f"ye_lo{u}", after(D, moe_end), D)[0:T] for u in range(2)]
        at = [extra_at + 2 * SLOT]
        S = [rounded(f"S{u}", after(NT * T, at_x), NT, T) for u in range(2)]
        SWT = [rounded(f"ST{u}", after(NTOK, at_x), NTOK)[0:T] for u in range(2)]
        wcur = [rounded(f"wcur{u}", after(2 * NT, at_x), NT, 2) for u in range(2)]
        comb2 = rounded("comb2", after(2 * NT * NE, at_x), NT * NE, 2)
        wslot = [view(after(1, at_x), 1)[0:T] for u in range(2)]
        row = [view(a, D)[0:T] for a in (at_hT, at_hT + D)]
        hid = [view(a, HID)[0:T] for a in (at_hT + 2 * D, at_hT + 2 * D + HID)]


        def chunk_ap(key):
            kind, _ = key
            at0 = ring_at[chunk_no[key] % RING]
            if kind in ("mod", "xrnn", "grnn", "gate", "ornn", "wout"):
                return view(at0, KT, 512)
            if kind == "qlat":
                return view(at0, KT, QL)
            if kind == "kvlat":
                return view(at0, KT, CK)
            if kind == "uq":
                return view(at0, 3, H * QK)
            if kind == "ukv":
                return view(at0, 4, 512)
            return view(at0, 4, D)

        reader = {"qlat": ("qlat", NT), "kvlat": ("kvlat", NT), "ukv": ("uv", 4), "omla": ("omla", 8)}
        chunk_end = []
        for kind, c in chunks:
            if kind == "mod":
                last = (kind, c)
            elif kind == "uq":
                last = (kind, (NT - 1, 1))
            elif kind == "wout":
                last = ("mix", (c, NT - 1))
            elif kind in reader:
                last = (reader[kind][0], reader[kind][1] - 1)
            else:
                last = (kind, 4 * c + 3)
            chunk_end.append(group_no[last] + 1)

        def done(kind, which):
            return group_no[(kind, which)] + 1

        def out_of(kind, which):
            who, c = emptied_by[group_no[(kind, which)]]
            return freed[who], c

        filled = sem("psum_filled")
        freed = {"act": sem("psum_freed_by_act"), "dve": sem("psum_freed_by_dve")}
        loaded = [sem(f"ring{s}_loaded") for s in range(RING)]
        const_in, x_in, vec_in, row_in, cache_in, lruw_in = (sem(n) for n in (
            "const_in", "x_in", "vec_in", "row_in", "cache_in", "lruw_in"))
        zeroed, dve_chain, act_chain = sem("zeroed"), sem("dve_chain"), sem("act_chain")
        sumsq, root, xs_ready = sem("sumsq"), sem("root"), sem("xs_ready")
        cols_ready, tanhc_ready, silu_ready, hT_ready = (sem(n) for n in (
            "cols_ready", "tanhc_ready", "silu_ready", "hT_ready"))
        xpad_ready, conv_done = sem("xpad_ready"), sem("conv_done")
        lru_cols, lru_exp, lru_ez, lru_q, lru_root, lru_done = (sem(n) for n in (
            "lru_cols", "lru_exp", "lru_ez", "lru_q", "lru_root", "lru_done"))
        y_ready, gelu_ready = sem("y_ready"), sem("gelu_ready")
        qlT_ready, kv_ready = sem("qlT_ready"), sem("kv_ready")
        work_raw, work_sq, work_root, work_ready = (sem(n) for n in ("work_raw", "work_sq", "work_root", "work_ready"))
        qkT_ready, nmax_ready, exp_ready, prob_ready, pT_ready, yatt_ready = (sem(n) for n in (
            "qkT_ready", "nmax_ready", "exp_ready", "prob_ready", "pT_ready", "yatt_ready"))
        diag_ready, bc_ready, gate_ready, merged_ready, x_ready = (sem(n) for n in (
            "diag_ready", "bc_ready", "gate_ready", "merged_ready", "x_ready"))
        scale2_ready, h2T_ready, sel_ready = (sem(n) for n in (
            "scale2_ready", "h2T_ready", "sel_ready"))
        final = sem("final")
        stored = sem("stored")
        e_loaded = [sem(f"{w}_loaded") for w in ("w1a", "w3a", "w1b", "w3b", "w2a", "w2b")]
        w2_used = [sem(f"{w}_used") for w in ("w2a", "w2b")]
        hi_ready, lo_ready, piece_used, xhi_ready, yhi_ready, h2hi_ready = (sem(n) for n in (
            "hi_ready", "lo_ready", "piece_used", "xhi_ready", "yhi_ready", "h2hi_ready"))
        S_ready, gathered, xe_ready, sil_ready, he_ready = (sem(n) for n in (
            "S_ready", "gathered", "xe_ready", "sil_ready", "he_ready"))
        g_out, t_done, h_done, ht_out = (sem(n) for n in ("rows_ready", "rows_turned", "hidden_turned", "heT_ready"))
        swt_done, scattered = ([sem(f"{n}{u}") for u in range(2)] for n in ("map_turned", "scattered"))
        y_done, ye_ready, sc_done, swt_ready, pos_cur, acc_step, pos_round = (sem(n) for n in (
            "y_done", "ye_ready", "sc_done", "swt_ready", "pos_cur", "acc_step", "pos_round"))

        block = ctx.enter_context(nc.Block())

        @block.sync
        def _(sp):
            w_in = io["w_in"][0].rearrange("(f p) n -> p f n", p=P)
            w_mod = io["w_mod"][0].rearrange("(f p) n -> p f n", p=P)
            o_rnn = io["w_o_rnn"][0].rearrange("(f p) n -> p f n", p=P)
            w_out = io["w_out"][0].rearrange("(f p) n -> p f n", p=P)
            sp.wait_ge(const_in, 16)
            sp.wait_ge(vec_in, 16 * 11)
            for n, (kind, c) in enumerate(chunks):
                if n >= RING:
                    sp.wait_ge(filled, chunk_end[n - RING])
                dst = chunk_ap((kind, c))
                if kind == "ukv":
                    sp.dma_start(dst[:, 0:2, :], io["w_uk"][0].rearrange("(f p) n -> p f n", p=P)).then_inc(loaded[n % RING], 16)
                    sp.dma_start(dst[:, 2:4, :], io["w_uv"][0].rearrange("(f p) n -> p f n", p=P)).then_inc(loaded[n % RING], 16)
                    continue
                src = {"mod": w_mod[:, :, c * 512:(c + 1) * 512],
                       "xrnn": w_in[:, :, (c % 2) * 512:(c % 2 + 1) * 512],
                       "grnn": w_in[:, :, C_G + (c % 2) * 512:C_G + (c % 2 + 1) * 512],
                       "qlat": w_in[:, :, C_Q:C_Q + QL],
                       "kvlat": w_in[:, :, C_KV:C_KV + CK],
                       "gate": w_in[:, :, C_GATE + (c % 4) * 512:C_GATE + (c % 4 + 1) * 512],
                       "uq": io["w_uq"][0].rearrange("(f p) n -> p f n", p=P),
                       "ornn": o_rnn[:, :, (c % 2) * 512:(c % 2 + 1) * 512],
                       "omla": io["w_o_mla"][0].rearrange("(f p) n -> p f n", p=P),
                       "wout": w_out[:, :, (c % 2) * 512:(c % 2 + 1) * 512]}[kind]
                sp.dma_start(dst, src).then_inc(loaded[n % RING], 16)

            def expert_chunk(j, e):
                dst = raw_at[j % 3]
                if j < 4:
                    src = (io["exp_w1"] if j % 2 == 0 else io["exp_w3"])[0, bass.ds(e + j // 2, 1)]
                    sp.dma_start(view(dst, KT, HID), src.rearrange("e (f p) n -> p (e f) n", p=P)).then_inc(e_loaded[j], 16)
                else:
                    src = io["exp_w2"][0, bass.ds(e + j - 4, 1)]
                    sp.dma_start(view(dst, HB, D), src.rearrange("e (f p) n -> p (e f) n", p=P)).then_inc(e_loaded[j], 16)

            def expert_pair(k, e):
                sp.wait_ge(lo_ready, 16 * k)
                expert_chunk(0, e)
                for j in (1, 2):
                    sp.wait_ge(w2_used[j - 1], k + CREDIT)
                    expert_chunk(j, e)
                for j in (3, 4, 5):
                    sp.wait_ge(lo_ready, 16 * k + 4 * (j - 2))
                    expert_chunk(j, e)

            sp.wait_ge(filled, chunk_end[chunk_no[("omla", 0)]])
            sp.wait_ge(filled, chunk_end[nf - RING])
            for j in range(6):
                if j >= 3:
                    sp.wait_ge(lo_ready, 4 * (j - 2))
                expert_chunk(j, 0)
            with sp.Fori(1, PAIRS) as i:
                expert_pair(i, 2 * i)
            sp.wait_ge(*out_of("pos", 0))
            rounds = sp.value_load(nri[0:1, :], min_val=1, max_val=ROUNDS)
            with sp.If(rounds > 1):
                with sp.Fori(1, rounds) as r:
                    with sp.Fori(0, PAIRS) as i:
                        expert_pair(r * PAIRS + i, 2 * i)

        @block.gpsimd
        def _(pool):
            pool.memset(ones, 1.0).then_inc(zeroed, 1)
            pool.memset(eps, EPS).then_inc(zeroed, 1)
            pool.memset(lruw, 0.0).then_inc(zeroed, 1)
            for b in range(2):
                pool.memset(xpad[b], 0.0).then_inc(zeroed, 1)
            pool.wait_ge(zeroed, 5)
            lv = lruw.rearrange("p (j k) m -> p j k m", k=4)
            for d in range(2):
                for s, name in enumerate(("lru_wa", "lru_wx")):
                    src = io[name][0, d].rearrange("(j h) k m -> h k j m", h=2)
                    for hh in range(2):
                        pool.dma_start(lv[64 * hh:64 * hh + 64, :, 2 * d + s, 64 * hh:64 * hh + 64], src[hh]).then_inc(lruw_in, 16)

            def spread(dst, name, n):
                src = io[name][0].rearrange("(a n) -> a n", a=1)
                pool.dma_start(dst, src.to_broadcast([P, n])).then_inc(row_in, 16)

            spread(qan, "q_a_norm", QL)
            spread(kvan, "kv_a_norm", KVL)
            spread(qk_g[:, 0, :], "q_norm", QK)
            spread(qk_g[:, 1, :], "k_norm", QK)
            spread(router_b[:, 0:NG], "router_bg", NG)
            spread(router_b[:, NG:NR], "router_be", NE)
            pool.dma_start(router_w[:, :, 0:NG], io["router_wg"][0].rearrange("(f p) n -> p f n", p=P)).then_inc(row_in, 16)
            pool.dma_start(router_w[:, :, NG:NR], io["router_we"][0].rearrange("(f p) n -> p f n", p=P)).then_inc(row_in, 16)

        @block.scalar
        def _(act):
            steps = [0]

            def chain(ins):
                steps[0] += 1
                ins.then_inc(act_chain, 1)
                act.wait_ge(act_chain, steps[0])

            def full(kind, which):
                act.wait_ge(filled, done(kind, which))

            act.dma_start(const, io["consts"]).then_inc(const_in, 16)
            va_row, vb_row = mem[0:NVA, at_qln:at_qln + P], mem[0:NVB, at_qln + P:at_qln + 2 * P]

            def rows(dst, lo, ap):
                src = ap.rearrange("(r n) -> r n", n=P)
                act.dma_start(dst[lo:lo + src.shape[0], :], src).then_inc(vec_in, 16)

            rows(va_row, BMOD, io["b_mod"][0])
            rows(va_row, N1, io["norm1_g"][0])
            rows(va_row, N2, io["norm2_g"][0])
            rows(va_row, CVEC, io["c_ctx"])
            rows(va_row, CVEC + KT, io["c"][0])
            rows(va_row, CONVW, io["conv_w"][0].rearrange("k n -> (k n)"))
            rows(va_row, CONVB, io["conv_b"][0])
            rows(vb_row, BA, io["lru_ba"][0].rearrange("d n -> (d n)"))
            rows(vb_row, BX, io["lru_bx"][0].rearrange("d n -> (d n)"))
            rows(vb_row, LAM, io["lru_lam"][0].rearrange("d n -> (d n)"))
            rows(vb_row, STATE, io["state_rglru"][0, 0].rearrange("d n -> (d n)"))
            act.dma_start(x[:, 0, :], io["x_prompt"][0]).then_inc(x_in, 16)
            act.dma_start(x[:, 1:3, :], io["x_sample"][0].rearrange("(t p) n -> p t n", p=P)).then_inc(x_in, 16)
            act.dma_start(ckv[:, 3, 0:KVL], io["cache_mla_ckv"][0, 0]).then_inc(cache_in, 16)
            act.dma_start(ckv[:, 3, KVL:CK], io["cache_mla_krope"][0, 0]).then_inc(cache_in, 16)

            act.wait_ge(zeroed, 5)
            act.wait_ge(x_in, 32)
            for t in range(NT):
                act.activation(xs[:, t, :], x[:, t, :], ACT.Square, accum_out=ss[:, t:t + 1]).then_inc(sumsq, 1)
            act.wait_ge(sumsq, NT)
            act.activation(rs[:, 0:NT], ss[:, 0:NT], ACT.Sqrt, scale=1.0 / D, bias=eps).then_inc(root, 1)
            act.wait_ge(cols_ready, 1)
            act.activation(tanh_c, va[:, CVEC:CVEC + 2 * KT].rearrange("p (a b) -> p a b", a=2), ACT.Tanh, scale=0.5).then_inc(tanhc_ready, 1)
            act.wait_ge(lru_ez, 1)
            act.activation(lam[:, 1, :], lam[:, 0, :], ACT.Exp, scale=-1.0).then_inc(lru_exp, 1)

            n_work = [0]
            for n, (kind, which, who) in enumerate(plan):
                b = banks[n % 8]
                if who == "act":
                    act.wait_ge(filled, n + 1)
                if kind == "mod":
                    if which >= 2:
                        act.wait_ge(filled, done("modT", which - 2))
                    act.activation(mrow[which % 2], b[0:2, :], ACT.Copy).then_inc(freed["act"], 1)
                if kind == "xrnn":
                    j = which
                    if j >= 2:
                        act.wait_ge(conv_done, j - 1)
                    act.activation(xpad[j % 2][:, 1:1 + CTX], b[:, 0:CTX], ACT.Copy).then_inc(xpad_ready, 1)
                    act.activation(xpad[j % 2][:, 1 + LAT0:1 + PADTOK], b[:, CTX:NTOK], ACT.Copy).then_inc(freed["act"], 1)
                elif kind in ("qlat", "kvlat"):
                    act.wait_ge(filled, n + 1)
                    width = QL if kind == "qlat" else KVL
                    col = (3 if kind == "qlat" else 6) + which
                    chain(act.activation(lru_sq[:, 0:width], b[:, 0:width], ACT.Square, accum_out=ss[:, col:col + 1]))
                    act.activation(rs[:, col:col + 1], ss[:, col:col + 1], ACT.Sqrt, scale=1.0 / width, bias=eps).then_inc(root, 1)
                elif kind == "lru":
                    m, s = which
                    d, j = m % 2, m // 2
                    cur = lru[:, m % 3]
                    if m == 0 and s == 0:
                        act.wait_ge(lru_cols, 1)
                        act.wait_ge(*out_of("kvlat", NT - 1))
                    if m >= 3 and s == 0:
                        act.wait_ge(lru_done, (m - 3) // 2 + 1)
                    bias = hbias[:, 16 * s + 8 * d + j:16 * s + 8 * d + j + 1]
                    act.activation(cur[:, s, :], b[:, 0:PADTOK], ACT.Tanh, scale=0.5, bias=bias).then_inc(freed["act"], 1)
                    if s == 1:
                        c = 8 * d + j
                        act.wait_ge(freed["act"], emptied_by[n][1])
                        chain(act.activation(cur[:, 2, :], cur[:, 0, :], ACT.Exp, scale=hc[:, c:c + 1], bias=hc[:, c:c + 1]))
                        act.activation(cur[:, 0, :], cur[:, 0, :], ACT.Tanh, scale=nhc[:, c:c + 1], bias=nhc[:, c:c + 1]).then_inc(lru_ez, 1)
                        if m >= 1:
                            act.wait_ge(lru_q, m)
                            prev = lru[:, (m - 1) % 3]
                            act.activation(prev[:, 0, :], prev[:, 0, :], ACT.Sqrt, scale=0.25).then_inc(lru_root, 1)
                elif kind == "qlT":
                    if which == 0:
                        act.wait_ge(lru_q, 16)
                        act.activation(lru[:, 15 % 3, 0, :], lru[:, 15 % 3, 0, :], ACT.Sqrt, scale=0.25).then_inc(lru_root, 1)
                    act.activation(qlT[:, which, :], b[:, 0:NTOK], ACT.Copy).then_inc(freed["act"], 1)
                elif kind == "ckvT":
                    act.activation(ckvT[:, which, :], b[:, :], ACT.Copy).then_inc(freed["act"], 1)
                elif kind == "uq":
                    t, hf = which
                    if t >= 2:
                        act.wait_ge(filled, done("qkT", (t - 2, 1)))
                    act.activation(work[:, t % 2, 4 * hf:4 * hf + 4, :], b[:, 0:4 * QK].rearrange("p (h d) -> p h d", d=QK),
                                   ACT.Copy).then_inc(freed["act"], 1)
                elif kind == "uk":
                    w = which + 3
                    act.wait_ge(filled, done("qkT", (w - 2, 1)))
                    act.activation(work[:, w % 2, :, 0:NOPE], b[:, :].rearrange("p (h d) -> p h d", d=NOPE),
                                   ACT.Copy).then_inc(freed["act"], 1)
                elif kind == "uv":
                    act.activation(values[:, which, :], b[:, :], ACT.Copy).then_inc(freed["act"], 1)
                if (kind == "uq" and which[1] == 1) or kind == "uk":
                    w = which[0] if kind == "uq" else which + 3
                    act.wait_ge(work_sq, w + 1)
                    act.activation(rsh[:, w, :], ssh[:, w, :], ACT.Sqrt, scale=1.0 / QK, bias=eps).then_inc(work_root, 1)
                elif kind == "qkT":
                    w, hf = which
                    src = b[0:QK, :].rearrange("p (h n) -> p h n", n=P)
                    if w == 0 and hf == 0:
                        act.wait_ge(conv_done, KT)
                    dst = qT[0:QK, 4 * hf:4 * hf + 4, w * P:(w + 1) * P] if w < 3 else \
                        kT[0:QK, 4 * hf:4 * hf + 4, (w - 3) * P:(w - 2) * P]
                    act.activation(dst, src, ACT.Copy).then_inc(freed["act"], 1)
                elif kind == "grnn":
                    if which >= 2:
                        act.wait_ge(y_ready, which - 1)
                    else:
                        act.wait_ge(lru_done, 8)
                    act.activation(gtmp[:, which % 2, :], b[:, 0:NTOK], ACT.Gelu_apprx_tanh).then_inc(freed["act"], 1)
                elif kind == "score":
                    i = which
                    nk = CTX if UNITS[i][1] == 0 else NTOK
                    act.wait_ge(nmax_ready, i + 1)
                    if i >= 3:
                        act.wait_ge(filled, done("pT", i - 3))
                    act.activation(prob[:, i % 3, 0:nk], b[:, 0:nk], ACT.Exp, scale=QK ** -0.5, bias=rmax[:, i:i + 1],
                                   accum_out=rsum[:, i:i + 1]).then_inc(freed["act"], 1)
                elif kind == "pT":
                    i = which
                    nk = CTX if UNITS[i][1] == 0 else NTOK
                    if i >= 2:
                        act.wait_ge(filled, done("pv", i - 2))
                    act.activation(pT[:, i % 2, 0:nk], b[:, 0:nk], ACT.Copy).then_inc(freed["act"], 1)
                elif kind in ("gb1", "gb2"):
                    c, hf = which
                    if kind == "gb2" and which == (0, 0):
                        act.wait_ge(x_ready, 6)
                    act.activation(bc[:, c, 512 * hf:512 * hf + 512], b[:, :], ACT.Copy).then_inc(freed["act"], 1)
                elif kind == "gate":
                    if which == 0:
                        act.wait_ge(filled, done("lru", (15, 1)))
                        act.wait_ge(lru_done, 8)
                    if which >= 8:
                        act.wait_ge(*out_of("ornn", which - 8))
                    act.activation(gbuf[:, which % 8, :], b[:, 0:NTOK], ACT.Tanh, scale=0.5).then_inc(freed["act"], 1)
                elif kind == "state":
                    act.activation(st_row[0:16, :], b[0:16, 0:P], ACT.Copy).then_inc(freed["act"], 1)
                    act.wait_ge(freed["act"], emptied_by[n][1])
                    act.dma_start(new_state[0, 0].rearrange("d (j p) -> (d j) p", p=P), st_row[0:16, :]).then_inc(stored, 16)
                elif kind == "h2T":
                    f = which
                    if f == 0:
                        act.wait_ge(scale2_ready, 1)
                    act.activation(hT[:, f, 0:CTX], b[:, 0:CTX], ACT.Identity, scale=scale2[:, f, 0:1], bias=mcol[:, SH2 + f, 0:1])\
                       .then_inc(h2T_ready, 1)
                    act.activation(hT[:, f, CTX:NTOK], b[:, CTX:NTOK], ACT.Identity, scale=scale2[:, f, 1:2], bias=mcol[:, SH2 + f, 1:2])\
                       .then_inc(freed["act"], 1)
                elif kind == "h2tok":
                    t, hf = which
                    act.wait_ge(filled, n + 1)
                    act.activation(h2_hi[:, t, 512 * hf:512 * hf + 512], b[:, :], ACT.Copy).then_inc(h2hi_ready, 1)
                elif kind == "mix" and which == (1, NT - 1):
                    act.wait_ge(x_ready, 6)
                    act.wait_ge(filled, done("ornn", 7))
                    for t in range(NT):
                        act.activation(xs[:, t, :], x[:, t, :], ACT.Square, accum_out=ss[:, 9 + t:10 + t]).then_inc(sumsq, 1)
                    act.wait_ge(sumsq, 2 * NT)
                    act.activation(rs[:, 9:12], ss[:, 9:12], ACT.Sqrt, scale=1.0 / D, bias=eps).then_inc(root, 1)
                if kind == "logit":
                    act.wait_ge(sel_ready, 1)
                    chain(act.activation(gsh, gsh, ACT.Exp))
                    act.activation(e21, e21, ACT.Exp).then_inc(h2T_ready, 1)
                if kind == "kvlat" and which == 0:
                    act.wait_ge(*out_of("kvlat", 0))
                    act.dma_start(new_ckv[0, 0], ckv[:, 0, 0:KVL]).then_inc(stored, 16)
                    act.dma_start(new_krope[0, 0], ckv[:, 0, KVL:CK]).then_inc(stored, 16)

            act.wait_ge(stored, 16 * 3)
            for s in (ye_ready, yhi_ready):
                act.sem_inc(s, CREDIT)
            act.wait_ge(*out_of("pos", 0))
            rounds = act.value_load(nri[0:1, :], min_val=1, max_val=ROUNDS)
            with act.Fori(0, rounds) as r:
                with act.Fori(0, PAIRS) as i:
                    k = r * PAIRS + i

                    def split_hi(j):
                        act.wait_ge(e_loaded[j], 16 * k + 16)
                        raw = view(raw_at[j % 3], KT, HID)
                        for q in range(PIECES):
                            p = PIECES * j + q
                            act.wait_ge(piece_used, 16 * k + p + 1)
                            act.activation(w_hi[p % PRING], raw[:, PIECE * q:PIECE * q + PIECE, :], ACT.Copy).then_inc(hi_ready, 1)

                    split_hi(0)
                    for u in range(2):
                        act.wait_ge(t_done, 4 * k + 2 * u + CREDIT)
                        for hf in range(2):
                            act.wait_ge(gathered, 4 * k + 2 * u + hf + 1)
                            act.activation(row[u][:, 512 * hf:512 * hf + 512], banks[2 * u + hf][0:T, :], ACT.Copy).then_inc(g_out, 1)
                    for u in range(2):
                        act.wait_ge(piece_used, 16 * k + PRING)
                        for hf in range(2):
                            act.wait_ge(t_done, 4 * k + 2 * u + hf + 1 + CREDIT)
                            act.activation(xe_hi[u][:, 4 * hf:4 * hf + 4, :], banks[2 * u + hf][:, 0:4 * T].rearrange("p (f t) -> p f t", t=T),
                                           ACT.Copy).then_inc(xhi_ready, 1)
                    split_hi(1)
                    for u in range(2):
                        if u == 1:
                            split_hi(2)
                            split_hi(3)
                        act.wait_ge(piece_used, 16 * k + 8 * u + 4 + PRING)
                        act.wait_ge(h_done, 2 * k + CREDIT)
                        act.activation(hid[u], banks[4 + 2 * u][0:T, :], ACT.Silu).then_inc(sil_ready, 1)
                    for u in range(2):
                        act.wait_ge(w2_used[u], k + CREDIT)
                        act.wait_ge(h_done, 2 * k + u + 1 + CREDIT)
                        act.activation(heT[u], banks[4 + 2 * u][:, 0:HB * T].rearrange("p (f t) -> p f t", t=T), ACT.Copy).then_inc(ht_out, 1)
                    for u in range(2):
                        act.wait_ge(scattered[u], k + CREDIT)
                        act.wait_ge(swt_ready, 4 * k + 2 * u + 2)
                        for hf in range(2):
                            if hf == 0:
                                act.wait_ge(y_done, 2 * k + u + 1)
                            else:
                                act.wait_ge(w2_used[u], k + 1 + CREDIT)
                            act.activation(ye_hi[u][:, 512 * hf:512 * hf + 512], banks[2 * u + hf][0:T, :], ACT.Copy, scale=wslot[u])\
                               .then_inc(yhi_ready, 1)
            for t in range(NT):
                act.wait_ge(final, t + 1)
                dst = y_prompt[0] if t == 0 else y_sample[0, (t - 1) * P:t * P]
                act.dma_start(dst, x[:, t, :]).then_inc(stored, 16)
            act.wait_ge(stored, 16 * 6)

        @block.vector
        def _(dve):
            steps = [0]

            def chain(ins):
                steps[0] += 1
                ins.then_inc(dve_chain, 1)
                dve.wait_ge(dve_chain, steps[0])

            def tt(out, a, b, op, **kw):
                return dve.tensor_tensor(out, a, b, op, **kw)

            def ts(out, a, s1, op0, s2=None, op1=None):
                if op1 is None:
                    return dve.tensor_scalar(out, a, s1, None, op0)
                return dve.tensor_scalar(out, a, s1, s2, op0, op1)

            def stt(out, a, s, b, op0, op1):
                return dve.scalar_tensor_tensor(out=out, in0=a, scalar=s, in1=b, op0=op0, op1=op1)

            def norm_x(col, n_root):
                dve.wait_ge(root, n_root)
                chain(dve.reciprocal(rs[:, col:col + NT], rs[:, col:col + NT]))
                for t in range(NT):
                    ts(xs[:, t, :], x[:, t, :], rs[:, col + t:col + t + 1], ALU.mult).then_inc(xs_ready, 1)

            def softplus_cols():
                dve.wait_ge(lru_exp, 1)
                z, w, w2, acc16, t16 = lam[:, 1, :], lam[:, 2, :], lam[:, 3, :], lam[:, 4, :], lam[:, 5, :]
                chain(ts(t16, z, 2.0, ALU.add))
                chain(dve.reciprocal(t16, t16))
                chain(tt(w, z, t16, ALU.mult))
                chain(tt(w2, w, w, ALU.mult))
                chain(ts(acc16, w2, 1.0 / 17, ALU.mult, 1.0 / 15, ALU.add))
                for odd in (13, 11, 9, 7, 5, 3, 1):
                    chain(tt(acc16, acc16, w2, ALU.mult))
                    chain(ts(acc16, acc16, 1.0 / odd, ALU.add))
                chain(tt(acc16, acc16, w, ALU.mult))
                chain(ts(t16, vb[:, LAM:LAM + 16], -1.0, ALU.mult, 0.0, ALU.max))
                chain(stt(acc16, acc16, 2.0, t16, ALU.mult, ALU.add))
                chain(ts(hbias, vb[:, BA:BA + 32], 0.5, ALU.mult))
                chain(ts(nhc, acc16, LRU_C / 2, ALU.mult))
                ts(hc, acc16, -LRU_C / 2, ALU.mult).then_inc(lru_cols, 1)

            def lru_finish(m):
                d, j = m % 2, m // 2
                cur = lru[:, m % 3]
                chain(stt(cur[:, 1, :], cur[:, 1, :], 1.0, xc[:, j, :], ALU.add, ALU.mult))
                dve.wait_ge(lru_root, m + 1)
                chain(tt(cur[:, 1, :], cur[:, 1, :], cur[:, 0, :], ALU.mult))
                for lo, hi, init in ((0, CTX, 0.0), (LAT0, PADTOK, vb[:, STATE + 8 * d + j:STATE + 8 * d + j + 1])):
                    a, bb, o = cur[:, 2, lo:hi], cur[:, 1, lo:hi], cur[:, 0, lo:hi]
                    if d:
                        a, bb, o = a[:, ::-1], bb[:, ::-1], o[:, ::-1]
                    chain(dve.tensor_tensor_scan(o, a, bb, init, ALU.mult, ALU.add))
                edge = cur[:, 0, CTX - 1:CTX] if d == 0 else cur[:, 0, 0:1]
                chain(dve.tensor_copy(st[:, 8 * d + j:8 * d + j + 1], edge))
                if d == 1:
                    fwd = lru[:, (m - 1) % 3]
                    if j == 0:
                        dve.wait_ge(filled, done("hT", KT - 1))
                    for lo, hi, s in PSEGS:
                        ins = tt(y[:, j, lo:hi], fwd[:, 0, lo + s:hi + s], cur[:, 0, lo + s:hi + s], ALU.add)
                        if lo == 0:
                            chain(ins)
                        else:
                            ins.then_inc(lru_done, 1)

            def head_norm(w):
                cur = work[:, w % 2]
                is_k = w >= 3
                tile = w - 3 if is_k else w
                if is_k:
                    chain(dve.tensor_copy(cur[:, :, NOPE:QK], ckv[:, tile, None, KVL:CK].to_broadcast([P, H, ROPE])))
                dve.wait_ge(work_ready, w)
                chain(tt(sq, cur, cur, ALU.mult))
                dve.tensor_reduce(ssh[:, w, :], sq, AX.X, ALU.add).then_inc(work_sq, 1)
                dve.wait_ge(work_root, w + 1)
                chain(dve.reciprocal(rsh[:, w, :], rsh[:, w, :]))
                chain(tt(cur, cur, rsh[:, w, :, None].to_broadcast([P, H, QK]), ALU.mult))
                last = tt(cur, cur, qk_g[:, int(is_k), None, :].to_broadcast([P, H, QK]), ALU.mult)
                if tile in (1, 2):
                    chain(last)
                    pair = cur[:, :, NOPE:QK].rearrange("p h (i two) -> p h i two", two=2)
                    x1, x2 = pair[:, :, :, 0], pair[:, :, :, 1]
                    tab = const[:, K_ROPE + 32 * (tile - 1):K_ROPE + 32 * tile]
                    co = tab[:, None, 0:16].to_broadcast([P, H, 16])
                    si = tab[:, None, 16:32].to_broadcast([P, H, 16])
                    for k, (a, b2) in enumerate(((x1, co), (x2, si), (x1, si), (x2, co))):
                        chain(tt(rt[:, k], a, b2, ALU.mult))
                    chain(tt(x1, rt[:, 0], rt[:, 1], ALU.subtract))
                    last = tt(x2, rt[:, 2], rt[:, 3], ALU.add)
                last.then_inc(work_ready, 1)

            def diag(row, c, hf, half):
                for b4 in range(4):
                    f = 4 * hf + b4
                    ins = ts(scratch[:, P * b4:P * b4 + P], ident, mcol[:, row + f, c:c + 1], ALU.mult, half, ALU.mult)
                    if b4 < 3:
                        chain(ins)
                ins.then_inc(diag_ready, 1)

            def first_max(one, v, m):
                chain(tt(one, v, m.to_broadcast([P, NT, 4]), ALU.is_equal))
                chain(tt(one, one, const[:, None, K_FIRST:K_FIRST + 4].to_broadcast([P, NT, 4]), ALU.mult))
                chain(dve.tensor_reduce(gz, one, AX.X, ALU.max))
                chain(tt(one, one, gz.to_broadcast([P, NT, 4]), ALU.is_equal))

            def route():
                gl = lg[:, :, 0:NG]
                chain(dve.tensor_reduce(gm, gl, AX.X, ALU.max))
                first_max(g1h, gl, gm)
                chain(tt(gsh, gl, gm.to_broadcast([P, NT, 4]), ALU.subtract))
                el = lg[:, :, NG:NR].rearrange("p t (g n) -> p t n g", g=NG)
                ep = eprod.rearrange("p t (n g) -> p t n g", g=NG)
                chain(tt(ep, el, g1h[:, :, None, :].to_broadcast([P, NT, EG, NG]), ALU.mult))
                chain(dve.tensor_reduce(ein, ep, AX.X, ALU.add))
                chain(dve.tensor_reduce(m1, ein, AX.X, ALU.max))
                first_max(o1, ein, m1)
                chain(stt(t4, o1, -1e30, ein, ALU.mult, ALU.add))
                chain(dve.tensor_reduce(m2, t4, AX.X, ALU.max))
                first_max(o2, t4, m2)
                tt(e21, m2, m1, ALU.subtract).then_inc(sel_ready, 1)
                dve.wait_ge(h2T_ready, KT + 1)
                chain(dve.tensor_reduce(gz, gsh, AX.X, ALU.add))
                chain(dve.reciprocal(gw, gz))
                chain(ts(gz, e21, 1.0, ALU.add))
                chain(dve.reciprocal(w1c, gz))
                chain(tt(w2c, w1c, e21, ALU.mult))
                chain(tt(w1c, w1c, gw, ALU.mult))
                chain(tt(w2c, w2c, gw, ALU.mult))
                chain(tt(wsel, o1, w1c.to_broadcast([P, NT, 4]), ALU.mult))
                chain(tt(t4, o2, w2c.to_broadcast([P, NT, 4]), ALU.mult))
                chain(tt(wsel, wsel, t4, ALU.add))
                chain(tt(ssel, o1, o2, ALU.add))
                sh = [P, NT, NG, EG]
                cv = comb.rearrange("p t (g n) -> p t g n", g=NG)
                sv = sel.rearrange("p t (g n) -> p t g n", g=NG)
                chain(tt(cv, g1h[:, :, :, None].to_broadcast(sh), wsel[:, :, None, :].to_broadcast(sh), ALU.mult))
                tt(sv, g1h[:, :, :, None].to_broadcast(sh), ssel[:, :, None, :].to_broadcast(sh), ALU.mult).then_inc(sel_ready, 1)

            dve.wait_ge(const_in, 16)
            dve.wait_ge(zeroed, 5)
            dve.wait_ge(x_in, 32)

            for n, (kind, which, who) in enumerate(plan):
                b = banks[n % 8]
                if who == "dve":
                    dve.wait_ge(filled, n + 1)
                if kind == "vec":
                    if which == 0:
                        dve.tensor_copy(va, b[:, 0:NVA]).then_inc(freed["dve"], 1)
                    else:
                        dve.tensor_copy(vb, b[:, 0:NVB]).then_inc(freed["dve"], 1)
                        dve.wait_ge(freed["dve"], 2)
                        ts(lam[:, 5, :], vb[:, LAM:LAM + 16], -1.0, ALU.mult).then_inc(cols_ready, 1)
                        dve.wait_ge(cols_ready, 1)
                        tt(lam[:, 0, :], vb[:, LAM:LAM + 16], lam[:, 5, :], ALU.max).then_inc(lru_ez, 1)
                        dve.wait_ge(tanhc_ready, 1)
                        chain(stt(tanh_c, tanh_c, 1.0, va[:, CVEC:CVEC + 2 * KT].rearrange("p (a b) -> p a b", a=2), ALU.add, ALU.mult))
                        ts(silu_c.rearrange("p f c -> p c f"), tanh_c, 0.5, ALU.mult).then_inc(silu_ready, 1)
                        norm_x(0, 1)
                        softplus_cols()
                elif kind == "modT":
                    c4 = 4 * which
                    pv = b[:, 0:8].rearrange("p (j c) -> p j c", c=2)
                    for c in range(2):
                        ins = tt(mcol[:, c4:c4 + 4, c], pv[:, :, c], va[:, BMOD + c4:BMOD + c4 + 4], ALU.add)
                        if c == 0:
                            chain(ins)
                        else:
                            ins.then_inc(freed["dve"], 1)
                    if which in (3, 9):
                        dve.wait_ge(freed["dve"], emptied_by[n][1])
                        row, nrm, out = (SC1, N1, scale1) if which == 3 else (SC2, N2, scale2)
                        chain(stt(out[:, :, 0], mcol[:, row:row + KT, 0], 1.0, va[:, nrm:nrm + KT], ALU.add, ALU.mult))
                        ins = stt(out[:, :, 1], mcol[:, row:row + KT, 1], 1.0, va[:, nrm:nrm + KT], ALU.add, ALU.mult)
                        if which == 3:
                            chain(ins)
                        else:
                            ins.then_inc(scale2_ready, 1)
                elif kind == "hT":
                    f = which
                    for c, lo, hi in SEGS:
                        ins = ts(hT[:, f, lo:hi], b[:, lo:hi], scale1[:, f, c:c + 1], ALU.mult, mcol[:, SH1 + f, c:c + 1], ALU.add)
                        ins.then_inc(hT_ready if c == 0 else freed["dve"], 1)
                elif kind == "xrnn":
                    j = which
                    dve.wait_ge(xpad_ready, j + 1)
                    dve.wait_ge(freed["act"], emptied_by[n][1])
                    src = xpad[j % 2]
                    w = [va[:, CONVW + 8 * k + j:CONVW + 8 * k + j + 1] for k in range(4)]
                    chain(ts(xc[:, j, :], src[:, 0:PADTOK], w[0], ALU.mult, va[:, CONVB + j:CONVB + j + 1], ALU.add))
                    for k in range(1, 4):
                        ins = stt(xc[:, j, :], src[:, k:k + PADTOK], w[k], xc[:, j, :], ALU.mult, ALU.add)
                        if k < 3:
                            chain(ins)
                    ins.then_inc(conv_done, 1)
                elif kind == "qlat":
                    t = which
                    if t == 0:
                        dve.wait_ge(row_in, 16 * 8)
                    dve.wait_ge(root, 2 + t)
                    chain(dve.reciprocal(rs[:, 3 + t:4 + t], rs[:, 3 + t:4 + t]))
                    stt(qln[:, t, :], b[:, 0:QL], rs[:, 3 + t:4 + t], qan, ALU.mult, ALU.mult).then_inc(freed["dve"], 1)
                elif kind == "kvlat":
                    t = which
                    dve.wait_ge(root, 5 + t)
                    chain(dve.reciprocal(rs[:, 6 + t:7 + t], rs[:, 6 + t:7 + t]))
                    chain(stt(ckv[:, t, 0:KVL], b[:, 0:KVL], rs[:, 6 + t:7 + t], kvan, ALU.mult, ALU.mult))
                    dve.tensor_copy(ckv[:, t, KVL:CK], b[:, KVL:CK]).then_inc(freed["dve"], 1)
                elif kind == "lru" and which[1] == 1:
                    m = which[0]
                    cur = lru[:, m % 3]
                    dve.wait_ge(lru_ez, 2 + m)
                    dve.wait_ge(lru_q, m)
                    chain(tt(lru_sq, cur[:, 2, :], cur[:, 2, :], ALU.mult))
                    stt(cur[:, 0, :], lru_sq, 1.0, cur[:, 0, :], ALU.add, ALU.mult).then_inc(lru_q, 1)
                    if m >= 1:
                        lru_finish(m - 1)
                elif kind == "qlT" and which == 0:
                    lru_finish(15)
                elif (kind == "uq" and which[1] == 1) or kind == "uk":
                    w = which[0] if kind == "uq" else which + 3
                    dve.wait_ge(freed["act"], emptied_by[n][1])
                    if w == 0:
                        dve.wait_ge(cache_in, 32)
                        dve.wait_ge(*out_of("kvlat", NT - 1))
                    head_norm(w)
                elif kind == "grnn":
                    dve.wait_ge(freed["act"], emptied_by[n][1])
                    tt(y[:, which, :], y[:, which, :], gtmp[:, which % 2, :], ALU.mult).then_inc(y_ready, 1)
                elif kind == "score":
                    i = which
                    nk = CTX if UNITS[i][1] == 0 else NTOK
                    dve.wait_ge(filled, n + 1)
                    chain(dve.tensor_reduce(rmax[:, i:i + 1], b[:, 0:nk], AX.X, ALU.max))
                    ts(rmax[:, i:i + 1], rmax[:, i:i + 1], -QK ** -0.5, ALU.mult).then_inc(nmax_ready, 1)
                    dve.wait_ge(freed["act"], emptied_by[n][1])
                    chain(dve.reciprocal(rsum[:, i:i + 1], rsum[:, i:i + 1]))
                    ts(prob[:, i % 3, 0:nk], prob[:, i % 3, 0:nk], rsum[:, i:i + 1], ALU.mult).then_inc(prob_ready, 1)
                elif kind == "pv":
                    h, q = UNITS[which]
                    lo = 64 * (h % 2)
                    dve.tensor_copy(yatt[lo:lo + 64, h // 2, q * P:(q + 1) * P], b[lo:lo + 64, 0:P]).then_inc(freed["dve"], 1)
                elif kind in ("gb1", "gb2"):
                    c, hf = which
                    if n and plan[n - 1][0] == kind:
                        dve.wait_ge(filled, n)
                    else:
                        dve.wait_ge(filled, n)
                    if kind == "gb1":
                        diag(G1, c, hf, 0.5)
                    else:
                        diag(G2, c, hf, 1.0)
                elif kind == "ornn":
                    if which == 0:
                        dve.wait_ge(filled, done("score", len(UNITS) - 1))
                    dve.wait_ge(*out_of("gate", which))
                    stt(merged[:, which, :], gbuf[:, which, :], 1.0, b[:, 0:NTOK], ALU.add, ALU.mult).then_inc(freed["dve"], 1)
                elif kind == "omla":
                    dve.wait_ge(*out_of("gate", 8 + which))
                    stt(gbuf[:, which, :], gbuf[:, which, :], 1.0, b[:, 0:NTOK], ALU.add, ALU.mult).then_inc(freed["dve"], 1)
                    dve.wait_ge(freed["dve"], emptied_by[n][1])
                    tt(merged[:, which, :], merged[:, which, :], gbuf[:, which, :], ALU.add).then_inc(merged_ready, 1)
                elif kind == "mix":
                    hf, t = which
                    dve.wait_ge(*out_of("gb1", (1, 1)))
                    if which == (0, 0):
                        dve.wait_ge(filled, done("gb1", (1, 1)))
                    seg = slice(512 * hf, 512 * hf + 512)
                    dve.wait_ge(x_ready, 3 * hf + t)
                    tt(scratch, b[:, :], bc[:, min(t, 1), seg], ALU.mult).then_inc(freed["dve"], 1)
                    dve.wait_ge(freed["dve"], emptied_by[n][1])
                    tt(x[:, t, seg], x[:, t, seg], scratch, ALU.add).then_inc(x_ready, 1)
                    if which == (1, NT - 1):
                        norm_x(9, 8)
                elif kind == "logit":
                    dve.memset(acc, 0.0).then_inc(acc_step, 1)
                    tt(lg, b[:, 0:NT * NR].rearrange("p (t n) -> p t n", n=NR), router_b[:, None, :].to_broadcast([P, NT, NR]), ALU.add)\
                        .then_inc(freed["dve"], 1)
                    dve.wait_ge(freed["dve"], emptied_by[n][1])
                    route()
                elif kind == "h2tok":
                    t, hf = which
                    seg = slice(512 * hf, 512 * hf + 512)
                    dve.wait_ge(h2hi_ready, 2 * t + hf + 1)
                    tt(h2_lo[:, t, seg], b[:, :], h2_hi[:, t, seg].bitcast(F32), ALU.subtract).then_inc(freed["dve"], 1)
                elif kind == "pos":
                    cnt = b[:, 64:64 + NE]
                    chain(dve.tensor_reduce(cmax, cnt, AX.X, ALU.max))
                    pb = b[:, 0:NT * NE].rearrange("p (t n) -> p t n", n=NE)
                    chain(stt(posm, pb, 1.0, sel, ALU.add, ALU.mult))
                    chain(ts(posm, posm, -1.0, ALU.add))
                    cf = comb.rearrange("p t n -> p (t n)")
                    chain(dve.tensor_copy(comb2[:, :, 0], cf))
                    chain(tt(comb2[:, :, 1], cf, comb2[:, :, 0].bitcast(F32), ALU.subtract))
                    chain(ts(rcount, const[:, K_THR:K_THR + ROUNDS], cmax, ALU.is_lt))
                    chain(dve.tensor_reduce(nrf, rcount, AX.X, ALU.add))
                    dve.tensor_copy(nri, nrf).then_inc(freed["dve"], 1)
                    dve.wait_ge(freed["dve"], emptied_by[n][1])

            rounds = dve.value_load(nri[0:1, :], min_val=1, max_val=ROUNDS)
            with dve.Fori(0, rounds) as r:
                with dve.Fori(0, PAIRS) as i:
                    k = r * PAIRS + i

                    def split_lo(j):
                        raw = view(raw_at[j % 3], KT, HID)
                        for q in range(PIECES):
                            p = PIECES * j + q
                            dve.wait_ge(hi_ready, 16 * k + p + 1)
                            tt(w_lo[p % PRING], raw[:, PIECE * q:PIECE * q + PIECE, :], w_hi[p % PRING].bitcast(F32), ALU.subtract)\
                                .then_inc(lo_ready, 1)

                    for u in range(2):
                        dve.wait_ge(swt_done[u], k + CREDIT)
                        dve.tensor_copy(pcur[:, u, :], posm[:, :, bass.ds(2 * i + u, 1)].rearrange("p t e -> p (t e)")).then_inc(pos_cur, 1)
                        c2 = comb2.rearrange("p (t n) two -> p t n two", t=NT)
                        dve.tensor_copy(wcur[u], c2[:, :, bass.ds(2 * i + u, 1), :].rearrange("p t e two -> p (t e) two")).then_inc(pos_cur, 1)
                        dve.wait_ge(pos_cur, 4 * k + 2 * u + 2)
                        for t in range(NT):
                            ts(S[u][:, t, :], iota, pcur[:, u, t:t + 1], ALU.is_equal).then_inc(S_ready, 1)
                    split_lo(0)
                    for u in range(2):
                        dve.wait_ge(scattered[u], k + CREDIT)
                        dve.wait_ge(swt_done[u], k + 1 + CREDIT)
                        dve.tensor_copy(SWT[u], banks[6 + u][0:T, 0:NTOK]).then_inc(swt_ready, 1)
                        dve.wait_ge(yhi_ready, 4 * k + CREDIT)
                        dve.wait_ge(ye_ready, 4 * k + CREDIT)
                        dve.tensor_reduce(wslot[u], banks[6 + u][0:T, NTOK:NTOK + 2], AX.X, ALU.add).then_inc(swt_ready, 1)
                    for u in range(2):
                        for hf in range(2):
                            seg = slice(4 * hf, 4 * hf + 4)
                            dve.wait_ge(xhi_ready, 4 * k + 2 * u + hf + 1)
                            tt(xe_lo[u][:, seg, :], banks[2 * u + hf][:, 0:4 * T].rearrange("p (f t) -> p f t", t=T),
                               xe_hi[u][:, seg, :].bitcast(F32), ALU.subtract).then_inc(xe_ready, 1)
                    split_lo(1)
                    split_lo(2)
                    for u in range(2):
                        if u == 1:
                            split_lo(3)
                        dve.wait_ge(sil_ready, 2 * k + u + 1)
                        dve.wait_ge(piece_used, 16 * k + 8 * u + 8 + PRING)
                        tt(hid[u], hid[u], banks[5 + 2 * u][0:T, :], ALU.mult).then_inc(he_ready, 1)
                    for u in range(2):
                        for hf in range(2):
                            seg = slice(512 * hf, 512 * hf + 512)
                            dve.wait_ge(yhi_ready, 4 * k + 2 * u + hf + 1 + CREDIT)
                            stt(ye_lo[u][:, seg], banks[2 * u + hf][0:T, :], wslot[u], ye_hi[u][:, seg].bitcast(F32), ALU.mult, ALU.subtract)\
                                .then_inc(ye_ready, 1)
                    for u in range(2):
                        for s in range(6):
                            t, hf = s // 2, s % 2
                            m = 6 * u + s
                            if s < 5:
                                dve.wait_ge(sc_done, 10 * k + 5 * u + s + 1)
                            else:
                                dve.wait_ge(scattered[u], k + 1 + CREDIT)
                            dve.wait_ge(acc_step, 12 * k + 1 if u == 0 else 12 * k + s + 2)
                            part = acc[:, t, 512 * hf:512 * hf + 512]
                            tt(part, part, banks[4 + m % 4][:, :], ALU.add).then_inc(acc_step, 1)
                dve.wait_ge(S_ready, (r + 1) * PAIRS * 6)
                dve.tensor_scalar(posm, posm, -float(T), None, ALU.add).then_inc(pos_round, 1)
                dve.wait_ge(pos_round, r + 1)
            dve.wait_ge(acc_step, rounds * (12 * PAIRS) + 1)
            for t in range(NT):
                chain(tt(acc[:, t, :], acc[:, t, :], bc[:, min(t, 1), :], ALU.mult))
                tt(x[:, t, :], x[:, t, :], acc[:, t, :], ALU.add).then_inc(final, 1)

        @block.tensor
        def _(pe):
            va_row, vb_row = mem[0:NVA, at_qln:at_qln + P], mem[0:NVB, at_qln + P:at_qln + 2 * P]

            def weights(key):
                n = chunk_no[key]
                extra = sum(1 for k in chunks[:n + 1] if k[0] == "ukv" and chunk_no[k] % RING == n % RING)
                pe.wait_ge(loaded[n % RING], 16 * (n // RING + 1 + extra))
                return chunk_ap(key)

            pe.wait_ge(const_in, 16)
            pe.wait_ge(vec_in, 16 * 11)
            pe.wait_ge(zeroed, 5)
            for n, (kind, which, who) in enumerate(plan):
                b = banks[n % 8]
                if n >= 8:
                    w, c = emptied_by[n - 8]
                    pe.wait_ge(freed[w], c)
                mm = None
                if kind == "vec":
                    src, rows = (va_row, NVA) if which == 0 else (vb_row, NVB)
                    mm = pe.transpose(b[:, 0:rows], src, ident[0:rows, 0:rows])
                elif kind == "mod":
                    if which == 0:
                        pe.wait_ge(silu_ready, 1)
                    w = weights(("mod", which))
                    for f in range(KT):
                        mm = pe.matmul(b[0:2, :], silu_c[:, f, :], w[:, f, :], start=(f == 0), stop=(f == KT - 1))
                elif kind == "modT":
                    pe.wait_ge(*out_of("mod", which))
                    for jb in range(4):
                        mm = pe.transpose(b[:, 2 * jb:2 * jb + 2], mrow[which % 2][:, P * jb:P * jb + P], ident[0:2, 0:2])
                elif kind in ("hT", "h2T"):
                    pe.wait_ge(xs_ready, NT if kind == "hT" else 2 * NT)
                    for t in range(NT):
                        mm = pe.transpose(b[:, t * P:t * P + P], xs[:, t, which * P:which * P + P], ident)
                elif kind in ("xrnn", "grnn", "gate", "ornn"):
                    if kind == "xrnn" and which == 0:
                        pe.wait_ge(hT_ready, KT)
                        pe.wait_ge(*out_of("hT", KT - 1))
                    if kind == "ornn" and which == 0:
                        pe.wait_ge(y_ready, KT)
                    w = weights((kind, which // 4))
                    src = y if kind == "ornn" else hT
                    for f in range(KT):
                        mm = pe.matmul(b[:, 0:NTOK], w[:, f, P * (which % 4):P * (which % 4) + P], src[:, f, :],
                                       start=(f == 0), stop=(f == KT - 1))
                elif kind in ("qlat", "kvlat"):
                    w = weights((kind, 0))
                    width = QL if kind == "qlat" else CK
                    for f in range(KT):
                        mm = pe.matmul(b[:, 0:width], hT[:, f, which * P:which * P + P], w[:, f, :], start=(f == 0), stop=(f == KT - 1))
                elif kind == "lru":
                    m, s = which
                    if m == 0 and s == 0:
                        pe.wait_ge(lruw_in, 16 * 8)
                        pe.wait_ge(conv_done, KT)
                    j, d = m // 2, m % 2
                    mm = pe.matmul(b[:, 0:PADTOK], lruw[:, 4 * j + 2 * d + s, :], xc[:, j, :], start=True, stop=True)
                elif kind == "qlT":
                    pe.wait_ge(*out_of("qlat", NT - 1))
                    for t in range(NT):
                        mm = pe.transpose(b[:, t * P:t * P + P], qln[:, t, which * P:which * P + P], ident)
                elif kind == "ckvT":
                    pe.wait_ge(*out_of("kvlat", NT - 1))
                    pe.wait_ge(cache_in, 32)
                    for t in range(4):
                        mm = pe.transpose(b[:, t * P:t * P + P], ckv[:, t, which * P:which * P + P], ident)
                elif kind == "uq":
                    t, hf = which
                    pe.wait_ge(*out_of("qlT", 2))
                    w = weights(("uq", 0))
                    for f in range(3):
                        mm = pe.matmul(b[:, 0:4 * QK], qlT[:, f, t * P:t * P + P], w[:, f, 4 * QK * hf:4 * QK * (hf + 1)],
                                       start=(f == 0), stop=(f == 2))
                elif kind in ("uk", "uv"):
                    pe.wait_ge(*out_of("ckvT", 1))
                    w = weights(("ukv", 0))
                    for f in range(2):
                        mm = pe.matmul(b[:, :], ckvT[:, f, which * P:which * P + P], w[:, f + (2 if kind == "uv" else 0), :],
                                       start=(f == 0), stop=(f == 1))
                elif kind == "qkT":
                    wi, hf = which
                    pe.wait_ge(work_ready, wi + 1)
                    for h4 in range(4):
                        mm = pe.transpose(b[0:QK, h4 * P:h4 * P + P], work[:, wi % 2, 4 * hf + h4, :], ident)
                elif kind == "score":
                    h, q = UNITS[which]
                    pe.wait_ge(*out_of("qkT", (6, 1)))
                    lo, hi = (0, P) if q == 0 else (P, 4 * P)
                    mm = pe.matmul(b[:, 0:hi - lo], qT[0:QK, h, q * P:q * P + P], kT[0:QK, h, lo:hi], start=True, stop=True)
                elif kind == "pT":
                    q = UNITS[which][1]
                    pe.wait_ge(prob_ready, which + 1)
                    for t in range(1 if q == 0 else 3):
                        mm = pe.transpose(b[:, t * P:t * P + P], prob[:, which % 3, t * P:t * P + P], ident)
                elif kind == "pv":
                    h, q = UNITS[which]
                    pe.wait_ge(*out_of("pT", which))
                    lo = 64 * (h % 2)
                    tiles = [0] if q == 0 else [1, 2, 3]
                    for z, t in enumerate(tiles):
                        mm = pe.matmul(b[lo:lo + 64, 0:P], values[:, t, V * h:V * h + V], pT[:, which % 2, z * P:z * P + P],
                                       start=(z == 0), stop=(z == len(tiles) - 1))
                elif kind in ("gb1", "gb2"):
                    c, hf = which
                    pe.wait_ge(diag_ready, (4 if kind == "gb2" else 0) + 2 * c + hf + 1)
                    mm = pe.matmul(b[:, :], ones, scratch, start=True, stop=True)
                elif kind == "omla":
                    if which == 0:
                        pe.wait_ge(*out_of("pv", len(UNITS) - 1))
                    w = weights(("omla", 0))
                    for f in range(4):
                        mm = pe.matmul(b[:, 0:NTOK], w[:, f, which * P:which * P + P], yatt[:, f, :], start=(f == 0), stop=(f == 3))
                elif kind == "mix":
                    hf, t = which
                    pe.wait_ge(merged_ready, KT)
                    w = weights(("wout", hf))
                    for f in range(KT):
                        mm = pe.matmul(b[:, :], merged[:, f, t * P:t * P + P], w[:, f, :], start=(f == 0), stop=(f == KT - 1))
                elif kind == "state":
                    pe.wait_ge(lru_done, 8)
                    mm = pe.transpose(b[0:16, 0:P], st, ident)
                elif kind == "logit":
                    pe.wait_ge(*out_of("h2T", KT - 1))
                    pe.wait_ge(h2T_ready, KT)
                    pe.wait_ge(row_in, 16 * 8)
                    for t in range(NT):
                        for f in range(KT):
                            mm = pe.matmul(b[:, NR * t:NR * t + NR], hT[:, f, t * P:t * P + P], router_w[:, f, :],
                                           start=(f == 0), stop=(f == KT - 1))
                elif kind == "h2tok":
                    t, hf = which
                    for f4 in range(4):
                        mm = pe.transpose(b[:, f4 * P:f4 * P + P], hT[:, 4 * hf + f4, t * P:t * P + P], ident)
                elif kind == "pos":
                    pe.wait_ge(sel_ready, 2)
                    for t in range(NT):
                        for t2 in range(t + 1):
                            pe.matmul(b[:, NE * t:NE * t + NE], upper if t2 == t else ones, sel[:, t2, :],
                                      start=(t2 == 0), stop=(t2 == t))
                    for t2 in range(NT):
                        mm = pe.matmul(b[:, 64:64 + NE], ones, sel[:, t2, :], start=(t2 == 0), stop=(t2 == NT - 1))
                mm.then_inc(filled, 1)

            for w in ("act", "dve"):
                pe.wait_ge(freed[w], count[w])
            for s in [*w2_used, *swt_done, *scattered, h_done, t_done]:
                pe.sem_inc(s, CREDIT)
            pe.sem_inc(piece_used, PRING)
            pe.wait_ge(*out_of("pos", 0))
            rounds = pe.value_load(nri[0:1, :], min_val=1, max_val=ROUNDS)
            w2 = [view(raw_at[j % 3], HB, D) for j in (4, 5)]
            with pe.Fori(0, rounds) as r:
                with pe.Fori(0, PAIRS) as i:
                    k = r * PAIRS + i
                    pe.wait_ge(ye_ready, 4 * k + CREDIT)
                    for u in range(2):
                        pe.wait_ge(S_ready, 6 * k + 3 * u + 3)
                        for hf in range(2):
                            seg = slice(512 * hf, 512 * hf + 512)
                            for t in range(NT):
                                pe.matmul(banks[2 * u + hf][0:T, :], S[u][:, t, :], h2_hi[:, t, seg], start=(t == 0), stop=False)
                                mm = pe.matmul(banks[2 * u + hf][0:T, :], S[u][:, t, :], h2_lo[:, t, seg], start=False, stop=(t == NT - 1))
                            mm.then_inc(gathered, 1)
                    pe.wait_ge(acc_step, 12 * k + 1)
                    for u in range(2):
                        for t in range(NT):
                            pe.transpose(banks[6 + u][0:T, t * P:t * P + P], S[u][:, t, :].bitcast(F32), ident)
                        for t in range(NT):
                            mm = pe.matmul(banks[6 + u][0:T, NTOK:NTOK + 2], S[u][:, t, :], wcur[u][:, t, :], start=(t == 0), stop=(t == NT - 1))
                        mm.then_inc(swt_done[u], 1)
                    for u in range(2):
                        for hf in range(2):
                            pe.wait_ge(g_out, 4 * k + 2 * u + hf + 1)
                            for f in range(4):
                                mm = pe.transpose(banks[2 * u + hf][:, T * f:T * f + T], row[u][:, (4 * hf + f) * P:(4 * hf + f + 1) * P],
                                                  ident[0:T, 0:T])
                            mm.then_inc(t_done, 1)
                    for u in range(2):
                        pe.wait_ge(xe_ready, 4 * k + 2 * u + 2)
                        if u == 1:
                            pe.wait_ge(swt_ready, 4 * k + 4)
                        for s in range(2):
                            out = banks[4 + 2 * u + s][0:T, :]
                            for q in range(PIECES):
                                p = PIECES * (2 * u + s) + q
                                pe.wait_ge(lo_ready, 16 * k + p + 1)
                                for z in range(PIECE):
                                    f = PIECE * q + z
                                    hi, lo = w_hi[p % PRING][:, z, :], w_lo[p % PRING][:, z, :]
                                    pe.matmul(out, xe_hi[u][:, f, :], hi, start=(f == 0), stop=False)
                                    pe.matmul(out, xe_hi[u][:, f, :], lo, start=False, stop=False)
                                    mm = pe.matmul(out, xe_lo[u][:, f, :], hi, start=False, stop=(f == KT - 1))
                                mm.then_inc(piece_used, 1)
                    for u in range(2):
                        pe.wait_ge(he_ready, 2 * k + u + 1)
                        for f in range(HB):
                            mm = pe.transpose(banks[4 + 2 * u][:, T * f:T * f + T], hid[u][:, f * P:f * P + P], ident[0:T, 0:T])
                        mm.then_inc(h_done, 1)
                        pe.wait_ge(ht_out, 2 * k + u + 1)
                        pe.wait_ge(e_loaded[4 + u], 16 * k + 16)
                        for hf in range(2):
                            for m in range(HB):
                                mm = pe.matmul(banks[2 * u + hf][0:T, :], heT[u][:, m, :], w2[u][:, m, 512 * hf:512 * hf + 512],
                                               start=(m == 0), stop=(m == HB - 1))
                            mm.then_inc(y_done if hf == 0 else w2_used[u], 1)
                    for u in range(2):
                        pe.wait_ge(ye_ready, 4 * k + 2 * u + 2 + CREDIT)
                        for s in range(6):
                            t, hf = s // 2, s % 2
                            m = 6 * u + s
                            seg = slice(512 * hf, 512 * hf + 512)
                            if m >= 4:
                                pe.wait_ge(acc_step, 12 * k + m - 2)
                            pe.matmul(banks[4 + m % 4][:, :], SWT[u][:, t * P:t * P + P], ye_hi[u][:, seg], start=True, stop=False)
                            mm = pe.matmul(banks[4 + m % 4][:, :], SWT[u][:, t * P:t * P + P], ye_lo[u][:, seg], start=False, stop=True)
                            mm.then_inc(sc_done if s < 5 else scattered[u], 1)


_NAMES = ['x_prompt', 'x_sample', 'cache_mla_ckv', 'cache_mla_krope', 'state_rglru', 'c', 'c_ctx', 'norm1_g', 'norm2_g',
          'w_mod', 'b_mod', 'w_in', 'conv_w', 'conv_b', 'lru_wa', 'lru_ba', 'lru_wx', 'lru_bx', 'lru_lam', 'q_a_norm',
          'kv_a_norm', 'w_uq', 'w_uk', 'w_uv', 'q_norm', 'k_norm', 'w_o_rnn', 'w_o_mla', 'w_out', 'router_wg', 'router_bg',
          'router_we', 'router_be', 'exp_w1', 'exp_w3', 'exp_w2']
_OUTS = [(1, CTX, D), (1, LAT, D), (1, 1, CTX, KVL), (1, 1, CTX, ROPE), (1, 1, 2, D)]


def shape_constants():
    import numpy as np
    k = np.zeros((P, NK), np.float32)
    k[:, K_ID:K_ID + P] = np.eye(P)
    k[:, K_UP:K_UP + P] = np.triu(np.ones((P, P)), 1)
    k[:, K_IOTA:K_IOTA + T] = np.arange(T)
    token = np.arange(LAT)
    inv = (10000.0 ** (-np.arange(0, 16, 2, dtype=np.float32) / 16)).astype(np.float32)
    ang = np.concatenate([(token // 64).astype(np.float32)[:, None] * inv, (token % 64).astype(np.float32)[:, None] * inv], -1)
    tab = np.concatenate([np.cos(ang), np.sin(ang)], -1).astype(np.float32)
    k[:, K_ROPE:K_ROPE + 32] = tab[:P]
    k[:, K_ROPE + 32:K_ROPE + 64] = tab[P:]
    k[:, K_FIRST:K_FIRST + 4] = [4, 3, 2, 1]
    k[:, K_THR:K_THR + ROUNDS] = T * np.arange(ROUNDS)
    return k


def kernel(**inputs):
    import numpy as _np
    import concourse.bacc as _bacc
    from concourse import mybir as _mybir
    from concourse.bass_utils import run_bass_kernel_spmd as _run

    nc = _bacc.Bacc("TRN2", target_bir_lowering=False, num_devices=1)
    arrays, io = {}, {}
    for name in _NAMES:
        arrays[f"in_{name}"] = _np.ascontiguousarray(inputs[name])
    arrays["in_consts"] = shape_constants()
    for key, a in arrays.items():
        io[key[3:]] = nc.dram_tensor(key, a.shape, _mybir.dt.from_np(a.dtype), kind="ExternalInput").ap()
    outs = [nc.dram_tensor(f"out_{i}", s, _mybir.dt.float32, kind="ExternalOutput").ap() for i, s in enumerate(_OUTS)]
    hybrid_step(nc, io, *outs)
    r = _run(nc, [arrays], core_ids=[0])
    return tuple(r.results[0][f"out_{i}"] for i in range(len(_OUTS)))
```

```python
from contextlib import ExitStack

import concourse.bass as bass
from concourse import mybir

ALU = mybir.AluOpType
ACT = mybir.ActivationFunctionType
AX = mybir.AxisListType
F32 = mybir.dt.float32
F32R = mybir.dt.float32r
I32 = mybir.dt.int32

P = 128
D = 1024
KT = D // P
CTX, LAT = 128, 256
NTOK = CTX + LAT
NT = NTOK // P
PADTOK = NTOK + 2
LAT0 = CTX + 2
H, NOPE, ROPE, QK, V = 8, 64, 32, 96, 64
QL, KVL = 384, 256
CK = KVL + ROPE
LRU_C = 8.0
EPS = 1e-6
NE, NG, EG, HID = 16, 4, 4, 512
NR = NG + NE
T = 96
ROUNDS = -(-NTOK // T)
CREDIT = 1
PAIRS = NE // 2
HB = HID // P
C_G, C_Q, C_KV, C_GATE = D, 2 * D, 2 * D + QL, 2 * D + QL + CK
BASE = 16512
PIECE = 2
PIECES = KT // PIECE
ALLP = 6 * PIECES
PRING = 4
SLOT = 4096
RING = 4
SEGS = ((0, 0, CTX), (1, CTX, NTOK))
PSEGS = ((0, CTX, 0), (CTX, NTOK, 2))

BMOD, N1, N2, CVEC, CONVW, CONVB, NVA = 0, 48, 56, 64, 80, 112, 120
BA, BX, LAM, STATE, NVB = 0, 16, 32, 48, 64
SH1, SC1, G1, SH2, SC2, G2 = (8 * i for i in range(6))
K_ID, K_UP, K_IOTA, K_ROPE, K_FIRST, K_THR, NK = 0, P, 2 * P, 2 * P + T, 2 * P + T + 64, 2 * P + T + 68, 2 * P + T + 68 + ROUNDS
SETS, BATCH = 8, 4
UNITS = [(h, q) for h in range(H) for q in range(NT)]


def stream_plan():
    plan = [("mod", c) for c in range(4)]
    plan += [("xrnn", 0), ("xrnn", 1), ("qlat", 0), ("kvlat", 0)]
    plan += [("mod", c) for c in range(4, 12)]
    plan += [("uq", 0), ("ukv", 0), ("grnn", 0), ("grnn", 1)]
    plan += [("gate", 0), ("gate", 1), ("ornn", 0), ("ornn", 1), ("gate", 2), ("gate", 3), ("omla", 0)]
    plan += [("wout", 0), ("wout", 1)]
    return plan


def psum_plan():
    g = [("vec", 0, "dve"), ("vec", 1, "dve")]
    for c in range(4):
        g += [("mod", c, "act")] + ([("modT", c - 1, "dve")] if c else [])
    g += [("modT", 3, "dve")]
    g += [("hT", f, "dve") for f in range(KT)]
    g += [("xrnn", j, "act") for j in range(KT)]
    g += [("qlat", t, "dve") for t in range(NT)] + [("kvlat", t, "dve") for t in range(NT)]
    for n in range(16):
        g += [("lru", (n, s), "act") for s in range(2)]
        if n % 2 == 1:
            g += [("mod", 4 + n // 2, "act"), ("modT", 4 + n // 2, "dve")]
    g += [("qlT", f, "act") for f in range(3)] + [("ckvT", f, "act") for f in range(2)]
    for n in range(8):
        if n < 3:
            g += [("uq", (n, 0), "act"), ("uq", (n, 1), "act")]
        elif n < 7:
            g += [("uk", n - 3, "act"), ("uv", n - 3, "act")]
        if n >= 1:
            g += [("qkT", (n - 1, 0), "act"), ("qkT", (n - 1, 1), "act")]
        g += [("grnn", n, "act")]
    g += [("state", 0, "act")] + [("gb1", (c, hf), "act") for c in range(2) for hf in range(2)]
    for i in range(len(UNITS) + 3):
        if i < len(UNITS):
            g += [("score", i, "act")]
        if 0 <= i - 2 < len(UNITS):
            g += [("pT", i - 2, "act")]
        if i >= 3:
            g += [("pv", i - 3, "dve")]
        if i % 3 == 2 and i // 3 < 8:
            g += [("gate", i // 3, "act")]
    for c in range(2):
        g += [("ornn", 4 * c + b, "dve") for b in range(4)]
    g += [("gate", 8 + b, "act") for b in range(8)] + [("omla", b, "dve") for b in range(8)]
    h2T, h2tok = ([[(kind, (t, 0), who0), (kind, (t, 1), "dve")] for t in range(NT)] for kind, who0 in (("h2T", "act"), ("h2tok", "dve")))
    g += [("mix", (0, 0), "dve"), ("mix", (1, 0), "dve"), ("mix", (0, 1), "dve")] + [("gb2", (0, hf), "act") for hf in range(2)]
    g += [("mix", (1, 1), "dve")] + h2T[0] + [("mix", (2, 0), "dve")] + h2tok[0] + [("lgT", 0, "dve"), ("mix", (2, 1), "dve")]
    g += h2T[1] + [("gb2", (1, hf), "act") for hf in range(2)]
    g += h2T[2] + h2tok[1] + [("lgT", 1, "dve"), ("lgT", 2, "dve"), ("logit", 0, "dve")] + h2tok[2]
    g += [("pos", 0, "dve")]
    return g


def split_plan():
    spread = lambda name, groups: [((name, q), g) for q, g in enumerate(groups)]
    plan = spread("y", [("score", i) for i in (0, 2, 4, 6)]) + spread(("ornn", 0), [("score", i) for i in (9, 12, 15, 18)])
    plan += spread("hT", [("ornn", b) for b in range(4)]) + spread(("ornn", 1), [("ornn", b) for b in range(4)])
    plan += spread("yatt", [("ornn", b) for b in range(4, 8)]) + spread(("gate", 2), [("ornn", b) for b in range(4, 8)])
    plan += spread(("gate", 3), [("gate", b) for b in range(8, 12)]) + spread(("omla", 0), [("gate", b) for b in range(12, 16)])
    plan += spread(("wout", 0), [("omla", b) for b in range(3, 7)]) + spread(("wout", 1), [("mix", (1, 0))] * 4)
    return plan


MIX = [(0, 0), (1, 0), (0, 1), (1, 1), (2, 0), (2, 1)]
SPLIT_SLOTS = {("ornn", 0): (2, 3), ("ornn", 1): (0, 1), ("gate", 2): (2, 3), ("gate", 3): (0, 1),
               ("omla", 0): (2, 3), ("wout", 0): (0, 1), ("wout", 1): (2, 3)}


def hybrid_step(nc, io, y_prompt, y_sample, new_ckv, new_krope, new_state):
    chunks = stream_plan()
    chunk_no = {key: n for n, key in enumerate(chunks)}
    plan = psum_plan()
    group_no = {(k, i): n for n, (k, i, _) in enumerate(plan)}
    emptied_by = []
    count = {"act": 0, "dve": 0}
    for _, _, who in plan:
        count[who] += 1
        emptied_by.append((who, count[who]))

    with ExitStack() as ctx:
        floats = 53200
        mem = nc.alloc_sbuf_tensor_at("mem", [P, floats], F32, offset=BASE)
        banks = [ctx.enter_context(nc.psum_tensor(f"bank{b}", [P, 512], F32)) for b in range(8)]

        def sem(name):
            return ctx.enter_context(nc.semaphore(name))

        top = [0]

        def take(n):
            at = top[0]
            top[0] += -(-n // 8) * 8
            assert top[0] <= floats, top[0]
            return at

        def view(at, *dims):
            n = 1
            for d in dims:
                n *= d
            ap = mem[:, at:at + n]
            if len(dims) == 2:
                ap = ap.rearrange("p (a b) -> p a b", a=dims[0])
            if len(dims) == 3:
                ap = ap.rearrange("p (a b c) -> p a b c", a=dims[0], b=dims[1])
            return ap

        ring_at = [take(SLOT) for _ in range(RING)]
        extra_at = top[0]
        at_q = take(H * NTOK)
        qT = view(at_q, H, NTOK)
        xpad = [view(at_q + 400 * b, 3 + PADTOK) for b in range(2)]
        values = view(take(4 * H * V), 4, H * V)
        at_work = take(2 * H * QK)
        work = view(at_work, 2, H, QK)
        yatt = view(at_work, 4, NTOK)
        gtmp = view(take(2 * NTOK), 2, NTOK)
        maps_room = 2 * (NT * T + NTOK) + 2 * NT * (NE + 2) + 32
        high_at = at_work + 2 * H * QK
        take(max(SETS * 3 * PADTOK + PADTOK, 2 * SLOT + maps_room, high_at + KT * NTOK - at_q) - (top[0] - at_q))
        lru = view(at_q, SETS, 3, PADTOK)
        lru_sq = view(at_q + SETS * 3 * PADTOK, PADTOK)
        at_x = top[0]
        x = view(take(NT * D), NT, D)
        at_hT = take(KT * NTOK)
        hT = view(at_hT, KT, NTOK)
        at_xc = take(KT * PADTOK)
        xc = view(at_xc, KT, PADTOK)
        gbuf = view(at_xc, KT, NTOK)
        at_y = take(KT * NTOK)
        xs = view(at_y, NT, D)
        y = view(at_y, KT, NTOK)
        at_kl = take(SLOT)
        kT = view(at_kl, H, 512)
        lruw = view(at_kl, 32, P)
        merged = view(at_kl, KT, NTOK)
        acc = view(at_kl, NT, D)
        at_qln = take(NT * QL)
        qln = view(at_qln, NT, QL)
        prob = view(at_qln, 3, NTOK)
        ckv = view(take(4 * CK), 4, CK)
        at_qlT = take(3 * NTOK)
        qlT = view(at_qlT, 3, NTOK)
        pT = view(at_qlT, 2, NTOK)
        mrow = [view(at_qlT + 512 * b, 512)[0:2] for b in range(2)]
        scratch = [view(at_qlT + 512 * b, 512) for b in range(2)]
        lgT = view(at_qln, NTOK)[0:NR]
        at_ckvT = take(2 * 512)
        ckvT = view(at_ckvT, 2, 512)
        diagonal = [view(at_ckvT + 512 * b, 4, P) for b in range(2)]
        moe_end = top[0]
        bc = view(take(2 * D), 2, D)
        mcol = view(take(96), 48, 2)
        va = view(take(NVA), NVA)
        vb = view(take(NVB), NVB)
        silu_c = view(take(16), KT, 2)
        tanh_c = view(take(16), 2, KT)
        scale1 = view(take(16), KT, 2)
        scale2 = view(take(16), KT, 2)
        hbias = view(take(32), 32)
        lam = view(take(16 * 6), 6, 16)
        hc = view(take(16), 16)
        nhc = view(take(16), 16)
        const = view(take(NK), NK)
        ident = const[:, K_ID:K_ID + P]
        upper = const[:, K_UP:K_UP + P]
        iota = const[:, K_IOTA:K_IOTA + T]
        ones = view(take(P), P)
        exact_at = [take(P), take(P), take(NT * NE)]
        qan = view(take(QL), QL)
        kvan = view(take(KVL), KVL)
        qk_g = view(take(2 * QK), 2, QK)
        router_b = view(take(NR), NR)
        router_w = view(take(KT * NR), KT, NR)
        ss = view(take(16), 16)
        rs = view(take(16), 16)
        ssh = view(take(56), 7, H)
        rsh = view(take(56), 7, H)
        rmax = view(take(24), 24)
        rsum = view(take(24), 24)
        eps = view(take(1), 1)
        st = view(take(16), 16)
        st_row = view(take(P), P)
        tmp_at = take(H * QK)
        sq = view(tmp_at, H, QK)
        rt = view(tmp_at, 4, H, ROPE // 2)
        at = [tmp_at]

        def small(*dims):
            n = 1
            for d in dims:
                n *= d
            at[0] += n
            assert at[0] <= tmp_at + H * QK
            return view(at[0] - n, *dims)

        lg = small(NT, NR)
        gm, gz, m1, m2, w1c, w2c, e21, gw = (small(NT, 1) for _ in range(8))
        gsh, g1h, ein, o1, o2, t4, wsel, ssel = (small(NT, EG) for _ in range(8))
        eprod, comb = (small(NT, NE) for _ in range(2))
        posm = small(NT, NE + 2)
        rcount = small(ROUNDS)
        cmax, nrf = small(1), small(1)
        nri = mem[:, at[0]:at[0] + 1].bitcast(I32)
        small(1)
        pcur, ccur = (small(2, NT) for _ in range(2))
        nf = len(chunks)
        spare = ring_at[0]
        raw_at = [extra_at, extra_at + SLOT, spare]
        late = ring_at[1:]

        def rounded(name, at, *dims):
            n = 1
            for d in dims:
                n *= d
            full = nc.alloc_sbuf_tensor_at(name, [P, n], F32R, offset=BASE + 4 * at)
            ap = full[:, :]
            if len(dims) == 2:
                ap = ap.rearrange("p (a b) -> p a b", a=dims[0])
            return ap

        ring_r = [[rounded(f"ring_r{b}_{q}", ring_at[b] + SLOT // 4 * q, SLOT // 4) for q in range(4)] for b in range(RING)]

        def blocks_r(name, at, blocks):
            return [rounded(f"{name}{q}", at + 2 * NTOK * q, 2, NTOK) for q in range(blocks // 2)]

        y_hi, y_lo = blocks_r("y_hi", high_at, KT), blocks_r("y_lo", at_y, KT)
        hT_hi, hT_lo = blocks_r("hT_hi", at_q, KT), blocks_r("hT_lo", at_hT, KT)
        yatt_hi, yatt_lo = blocks_r("yatt_hi", at_q + H * NTOK, 4), blocks_r("yatt_lo", at_work, 4)
        merged_hi, merged_lo = blocks_r("merged_hi", high_at, KT), blocks_r("merged_lo", at_kl, KT)
        splits = split_plan()
        beside = {}
        for kind, which, _ in plan:
            beside[(kind, which)] = [n for n, (_, g) in enumerate(splits) if g == (kind, which)]
        split_order = [n for kind, which, _ in plan for n in beside[(kind, which)]]

        def hi_by(name):
            return "pool" if name in ("y", ("ornn", 0)) else "act"

        def lo_by(name):
            return "pool" if name in SPLIT_SLOTS or name == "y" else "dve"

        hi_count, lo_count = {}, {}
        for n in split_order:
            (name, q), _ = splits[n]
            hi_count[(name, q)] = 1 + sum(hi_by(other[0]) == hi_by(name) for other in hi_count)
            lo_count[(name, q)] = 1 + sum(lo_by(other[0]) == lo_by(name) for other in lo_count)

        def split_parts(name, q):
            if name in SPLIT_SLOTS:
                lo_slot, hi_slot = SPLIT_SLOTS[name]
                return view(ring_at[lo_slot] + SLOT // 4 * q, SLOT // 4), ring_r[hi_slot][q], ring_r[lo_slot][q]
            whole, hi, lo = {"y": (y, y_hi, y_lo), "hT": (hT, hT_hi, hT_lo), "yatt": (yatt, yatt_hi, yatt_lo)}[name]
            if name == "yatt":
                return whole[:, q, :], hi[q // 2][:, q % 2, :], lo[q // 2][:, q % 2, :]
            return whole[:, 2 * q:2 * q + 2, :], hi[q], lo[q]

        ones_r, upper_r, sel = (rounded(n, a, *d) for n, a, d in zip(("ones_r", "upper_r", "sel"), exact_at, ((P,), (P,), (NT, NE))))

        def piece_of(p):
            j, q = p // PIECES, p % PIECES
            if j < 4:
                return view(raw_at[j % 3], KT, HID)[:, PIECE * q:PIECE * q + PIECE, :]
            hf, m2 = q // 2, q % 2
            return view(raw_at[j % 3], HB, D)[:, 2 * m2:2 * m2 + 2, 512 * hf:512 * hf + 512]

        w_hi = [rounded(f"w_hi{i}", late[0] + 1024 * i, PIECE, HID) for i in range(PRING)]
        w_lo = [rounded(f"w_lo{i}", late[1] + 1024 * i, PIECE, HID) for i in range(PRING)]
        xe_hi = [rounded(f"xe_hi{u}", late[2] + KT * T * u, KT, T) for u in range(2)]
        xe_lo = [rounded(f"xe_lo{u}", late[2] + KT * T * (2 + u), KT, T) for u in range(2)]
        assert KT * T * 4 <= SLOT
        h2_hi = rounded("h2_hi", at_y, NT, D)
        h2_lo = rounded("h2_lo", at_xc, NT, D)
        at = [0]

        def after(n, end):
            start = at[0]
            at[0] += -(-n // 8) * 8
            assert at[0] <= end
            return start

        at[0] = at_kl + NT * D
        he_hi = [rounded(f"he_hi{u}", after(HB * T, at_qln), HB, T) for u in range(2)]
        at[0] = late[2] + KT * T * 4
        he_lo = [rounded(f"he_lo{u}", after(HB * T, late[2] + SLOT), HB, T) for u in range(2)]
        at[0] = at_qln
        ye_hi = [rounded(f"ye_hi{u}", after(D, moe_end), D)[0:T] for u in range(2)]
        ye_lo = [rounded(f"ye_lo{u}", after(D, moe_end), D)[0:T] for u in range(2)]
        at[0] = extra_at + 2 * SLOT
        S = [rounded(f"S{u}", after(NT * T, at_x), NT, T) for u in range(2)]
        SWT = [rounded(f"ST{u}", after(NTOK, at_x), NTOK)[0:T] for u in range(2)]
        wcur = [rounded(f"wcur{u}", after(2 * NT, at_x), NT, 2) for u in range(2)]
        comb2 = rounded("comb2", after(2 * NT * (NE + 2), at_x), NT * (NE + 2), 2)
        comb2 = comb2.rearrange("p (t n) two -> p t n two", t=NT)
        wslot = [view(after(1, at_x), 1)[0:T] for u in range(2)]
        row = [view(a, D)[0:T] for a in (at_hT, at_hT + D)]
        hid = [view(a, HID)[0:T] for a in (at_hT + 2 * D, at_hT + 2 * D + HID)]


        def slot_of(key):
            return SPLIT_SLOTS[key][0] if key in SPLIT_SLOTS else chunk_no[key] % RING

        def chunk_ap(key):
            kind, _ = key
            at0 = ring_at[slot_of(key)]
            if kind in ("mod", "xrnn", "grnn", "gate", "ornn", "wout"):
                return view(at0, KT, 512)
            if kind == "qlat":
                return view(at0, KT, QL)
            if kind == "kvlat":
                return view(at0, KT, CK)
            if kind == "uq":
                return view(at0, 3, H * QK)
            if kind == "ukv":
                return view(at0, 4, 512)
            return view(at0, 4, D)

        reader = {"qlat": ("qlat", NT), "kvlat": ("kvlat", NT), "ukv": ("uv", 4), "omla": ("omla", 8)}
        chunk_end = []
        for kind, c in chunks:
            if kind == "mod":
                last = (kind, c)
            elif kind == "uq":
                last = (kind, (NT - 1, 1))
            elif kind == "wout":
                last = ("mix", (NT - 1, c))
            elif kind in reader:
                last = (reader[kind][0], reader[kind][1] - 1)
            else:
                last = (kind, 4 * c + 3)
            chunk_end.append(group_no[last] + 1)

        def slot_free(slot, n):
            before = [m for m in range(n) if slot in (slot_of(chunks[m]), SPLIT_SLOTS.get(chunks[m], (0, -1))[1])]
            return chunk_end[before[-1]] if before else None

        def loads(n):
            return sum(2 if k[0] == "ukv" else 1 for k in chunks[:n + 1] if slot_of(k) == slot_of(chunks[n]))

        def done(kind, which):
            return group_no[(kind, which)] + 1

        def out_of(kind, which):
            who, c = emptied_by[group_no[(kind, which)]]
            return freed[who], c

        filled = sem("psum_filled")
        freed = {"act": sem("psum_freed_by_act"), "dve": sem("psum_freed_by_dve")}
        hi_made = {by: sem(f"high_parts_by_{by}") for by in ("act", "pool")}
        lo_made = {by: sem(f"low_parts_by_{by}") for by in ("dve", "pool")}
        merged_raw, merged_hi_ready = sem("merged_raw"), sem("merged_hi_ready")
        loaded = [sem(f"ring{s}_loaded") for s in range(RING)]
        const_in, x_in, vec_in, row_in, cache_in, lruw_in = (sem(n) for n in (
            "const_in", "x_in", "vec_in", "row_in", "cache_in", "lruw_in"))
        zeroed, dve_chain, act_chain = sem("zeroed"), sem("dve_chain"), sem("act_chain")
        sumsq, root, xs_ready = sem("sumsq"), sem("root"), sem("xs_ready")
        cols_ready, tanhc_ready, silu_ready, hT_ready = (sem(n) for n in (
            "cols_ready", "tanhc_ready", "silu_ready", "hT_ready"))
        xpad_ready, conv_done = sem("xpad_ready"), sem("conv_done")
        lru_cols, lru_exp, lru_ez, lru_q, lru_root, lru_done = (sem(n) for n in (
            "lru_cols", "lru_exp", "lru_ez", "lru_q", "lru_root", "lru_done"))
        y_ready, gelu_ready = sem("y_ready"), sem("gelu_ready")
        qlT_ready, kv_ready = sem("qlT_ready"), sem("kv_ready")
        work_raw, work_sq, work_root, work_ready = (sem(n) for n in ("work_raw", "work_sq", "work_root", "work_ready"))
        qkT_ready, nmax_ready, exp_ready, prob_ready, pT_ready, yatt_ready = (sem(n) for n in (
            "qkT_ready", "nmax_ready", "exp_ready", "prob_ready", "pT_ready", "yatt_ready"))
        diag_ready, bc_ready, gate_ready, merged_ready, x_ready = (sem(n) for n in (
            "diag_ready", "bc_ready", "gate_ready", "merged_ready", "x_ready"))
        scale2_ready, h2T_low, h2T_high, sel_ready, exact_ready, route_exp = (sem(n) for n in (
            "scale2_ready", "h2T_low_ready", "h2T_high_ready", "sel_ready", "exact_ready", "route_exp"))
        final = sem("final")
        stored = sem("stored")
        e_loaded = [sem(f"{w}_loaded") for w in ("w1a", "w3a", "w1b", "w3b", "w2a", "w2b")]
        hi_ready, lo_ready, piece_used, xhi_ready, yhi_ready, h2hi_ready = (sem(n) for n in (
            "hi_ready", "lo_ready", "piece_used", "xhi_ready", "yhi_ready", "h2hi_ready"))
        S_ready, gathered, xe_ready, sil_ready, he_ready = (sem(n) for n in (
            "S_ready", "gathered", "xe_ready", "sil_ready", "he_ready"))
        g_out, t_done, h_done, ht_out = (sem(n) for n in ("rows_ready", "rows_turned", "hidden_turned", "heT_ready"))
        swt_done = [sem(f"map_turned{u}") for u in range(2)]
        ye_ready, sc_done, swt_ready, pos_cur, acc_step, pos_round = (sem(n) for n in (
            "ye_ready", "scattered", "swt_ready", "pos_cur", "acc_step", "pos_round"))
        hehi_ready = sem("hehi_ready")

        block = ctx.enter_context(nc.Block())

        @block.sync
        def _(sp):
            w_in = io["w_in"][0].rearrange("(f p) n -> p f n", p=P)
            w_mod = io["w_mod"][0].rearrange("(f p) n -> p f n", p=P)
            o_rnn = io["w_o_rnn"][0].rearrange("(f p) n -> p f n", p=P)
            w_out = io["w_out"][0].rearrange("(f p) n -> p f n", p=P)
            for n, (kind, c) in enumerate(chunks):
                slot = slot_of((kind, c))
                if slot_free(slot, n) is not None:
                    sp.wait_ge(filled, slot_free(slot, n))
                if n == 1:
                    sp.wait_ge(const_in, 16)
                    sp.wait_ge(vec_in, 16 * 11)
                if n == 2:
                    sp.dma_start(x[:, 0, :], io["x_prompt"][0]).then_inc(x_in, 16)
                    sp.dma_start(x[:, 1:3, :], io["x_sample"][0].rearrange("(t p) n -> p t n", p=P)).then_inc(x_in, 16)
                dst = chunk_ap((kind, c))
                if kind == "ukv":
                    sp.dma_start(dst[:, 0:2, :], io["w_uk"][0].rearrange("(f p) n -> p f n", p=P)).then_inc(loaded[slot], 16)
                    sp.dma_start(dst[:, 2:4, :], io["w_uv"][0].rearrange("(f p) n -> p f n", p=P)).then_inc(loaded[slot], 16)
                    continue
                src = {"mod": w_mod[:, :, c * 512:(c + 1) * 512],
                       "xrnn": w_in[:, :, (c % 2) * 512:(c % 2 + 1) * 512],
                       "grnn": w_in[:, :, C_G + (c % 2) * 512:C_G + (c % 2 + 1) * 512],
                       "qlat": w_in[:, :, C_Q:C_Q + QL],
                       "kvlat": w_in[:, :, C_KV:C_KV + CK],
                       "gate": w_in[:, :, C_GATE + (c % 4) * 512:C_GATE + (c % 4 + 1) * 512],
                       "uq": io["w_uq"][0].rearrange("(f p) n -> p f n", p=P),
                       "ornn": o_rnn[:, :, (c % 2) * 512:(c % 2 + 1) * 512],
                       "omla": io["w_o_mla"][0].rearrange("(f p) n -> p f n", p=P),
                       "wout": w_out[:, :, (c % 2) * 512:(c % 2 + 1) * 512]}[kind]
                sp.dma_start(dst, src).then_inc(loaded[slot], 16)

            def expert_chunk(j, e):
                dst = raw_at[j % 3]
                if j < 4:
                    src = (io["exp_w1"] if j % 2 == 0 else io["exp_w3"])[0, bass.ds(e + j // 2, 1)]
                    sp.dma_start(view(dst, KT, HID), src.rearrange("e (f p) n -> p (e f) n", p=P)).then_inc(e_loaded[j], 16)
                else:
                    src = io["exp_w2"][0, bass.ds(e + j - 4, 1)]
                    sp.dma_start(view(dst, HB, D), src.rearrange("e (f p) n -> p (e f) n", p=P)).then_inc(e_loaded[j], 16)

            def expert_pair(k, e):
                for j in range(6):
                    sp.wait_ge(lo_ready, ALLP * k + PIECES * (j - 2))
                    expert_chunk(j, e)

            sp.wait_ge(filled, chunk_end[chunk_no[("omla", 0)]])
            for j in range(6):
                if j == 1:
                    sp.wait_ge(filled, chunk_end[nf - 1])
                if j >= 3:
                    sp.wait_ge(lo_ready, PIECES * (j - 2))
                expert_chunk(j, 0)
            with sp.Fori(1, PAIRS) as i:
                expert_pair(i, 2 * i)
            sp.wait_ge(*out_of("pos", 0))
            rounds = sp.value_load(nri[0:1, :], min_val=1, max_val=ROUNDS)
            with sp.If(rounds > 1):
                with sp.Fori(1, rounds) as r:
                    with sp.Fori(0, PAIRS) as i:
                        expert_pair(r * PAIRS + i, 2 * i)

        @block.gpsimd
        def _(pool):
            pool.memset(ones, 1.0).then_inc(zeroed, 1)
            pool.memset(eps, EPS).then_inc(zeroed, 1)
            pool.memset(lruw, 0.0).then_inc(zeroed, 1)
            for b in range(2):
                pool.memset(xpad[b], 0.0).then_inc(zeroed, 1)
            pool.wait_ge(zeroed, 5)
            lv = lruw.rearrange("p (j k) m -> p j k m", k=4)
            for d in range(2):
                for s, name in enumerate(("lru_wa", "lru_wx")):
                    src = io[name][0, d].rearrange("(j h) k m -> h k j m", h=2)
                    for hh in range(2):
                        pool.dma_start(lv[64 * hh:64 * hh + 64, :, 2 * d + s, 64 * hh:64 * hh + 64], src[hh]).then_inc(lruw_in, 16)

            def spread(dst, name, n):
                src = io[name][0].rearrange("(a n) -> a n", a=1)
                pool.dma_start(dst, src.to_broadcast([P, n])).then_inc(row_in, 16)

            spread(qan, "q_a_norm", QL)
            spread(kvan, "kv_a_norm", KVL)
            spread(qk_g[:, 0, :], "q_norm", QK)
            spread(qk_g[:, 1, :], "k_norm", QK)
            spread(router_b[:, 0:NG], "router_bg", NG)
            spread(router_b[:, NG:NR], "router_be", NE)
            pool.dma_start(router_w[:, :, 0:NG], io["router_wg"][0].rearrange("(f p) n -> p f n", p=P)).then_inc(row_in, 16)
            pool.dma_start(router_w[:, :, NG:NR], io["router_we"][0].rearrange("(f p) n -> p f n", p=P)).then_inc(row_in, 16)

            for n in split_order:
                name, q = splits[n][0]
                if lo_by(name) != "pool":
                    continue
                whole, hi, lo = split_parts(name, q)
                if hi_by(name) == "pool":
                    if name == "y":
                        pool.wait_ge(y_ready, KT)
                    else:
                        pool.wait_ge(loaded[slot_of(name)], 16 * loads(chunk_no[name]))
                        pool.wait_ge(filled, slot_free(SPLIT_SLOTS[name][1], chunk_no[name]))
                    pool.tensor_copy(hi, whole).then_inc(hi_made["pool"], 1)
                pool.wait_ge(hi_made[hi_by(name)], hi_count[(name, q)])
                pool.tensor_tensor(lo, whole, hi.bitcast(F32), ALU.subtract).then_inc(lo_made["pool"], 1)
            pool.wait_ge(filled, done("mix", (NT - 1, 1)))
            pool.memset(acc, 0.0).then_inc(acc_step, 1)

        @block.scalar
        def _(act):
            steps = [0]

            def chain(ins):
                steps[0] += 1
                ins.then_inc(act_chain, 1)
                act.wait_ge(act_chain, steps[0])

            def full(kind, which):
                act.wait_ge(filled, done(kind, which))

            act.dma_start(const, io["consts"]).then_inc(const_in, 16)
            va_row, vb_row = mem[0:NVA, at_qln:at_qln + P], mem[0:NVB, at_qln + P:at_qln + 2 * P]

            def rows(dst, lo, ap):
                src = ap.rearrange("(r n) -> r n", n=P)
                act.dma_start(dst[lo:lo + src.shape[0], :], src).then_inc(vec_in, 16)

            rows(va_row, BMOD, io["b_mod"][0])
            rows(va_row, N1, io["norm1_g"][0])
            rows(va_row, N2, io["norm2_g"][0])
            rows(va_row, CVEC, io["c_ctx"])
            rows(va_row, CVEC + KT, io["c"][0])
            rows(va_row, CONVW, io["conv_w"][0].rearrange("k n -> (k n)"))
            rows(va_row, CONVB, io["conv_b"][0])
            rows(vb_row, BA, io["lru_ba"][0].rearrange("d n -> (d n)"))
            rows(vb_row, BX, io["lru_bx"][0].rearrange("d n -> (d n)"))
            rows(vb_row, LAM, io["lru_lam"][0].rearrange("d n -> (d n)"))
            rows(vb_row, STATE, io["state_rglru"][0, 0].rearrange("d n -> (d n)"))
            act.dma_start(ckv[:, 3, 0:KVL], io["cache_mla_ckv"][0, 0]).then_inc(cache_in, 16)
            act.dma_start(ckv[:, 3, KVL:CK], io["cache_mla_krope"][0, 0]).then_inc(cache_in, 16)

            act.wait_ge(zeroed, 5)
            act.wait_ge(cols_ready, 1)
            act.activation(tanh_c, va[:, CVEC:CVEC + 2 * KT].rearrange("p (a b) -> p a b", a=2), ACT.Tanh, scale=0.5).then_inc(tanhc_ready, 1)
            act.wait_ge(lru_ez, 1)
            act.activation(lam[:, 1, :], lam[:, 0, :], ACT.Exp, scale=-1.0).then_inc(lru_exp, 1)
            act.wait_ge(x_in, 32)
            for t in range(NT):
                act.activation(xs[:, t, :], x[:, t, :], ACT.Square, accum_out=ss[:, t:t + 1]).then_inc(sumsq, 1)
            act.wait_ge(sumsq, NT)
            act.activation(rs[:, 0:NT], ss[:, 0:NT], ACT.Sqrt, scale=1.0 / D, bias=eps).then_inc(root, 1)

            n_work = [0]
            for n, (kind, which, who) in enumerate(plan):
                b = banks[n % 8]
                for m in beside[(kind, which)]:
                    name, q = splits[m][0]
                    if hi_by(name) != "act":
                        continue
                    whole, hi, _ = split_parts(name, q)
                    if name in SPLIT_SLOTS:
                        act.wait_ge(loaded[slot_of(name)], 16 * loads(chunk_no[name]))
                        act.wait_ge(filled, slot_free(SPLIT_SLOTS[name][1], chunk_no[name]))
                    elif name == "hT":
                        act.wait_ge(filled, done("score", len(UNITS) - 1))
                    else:
                        act.wait_ge(*out_of("pv", len(UNITS) - 1))
                    act.activation(hi, whole, ACT.Copy).then_inc(hi_made["act"], 1)
                if who == "act":
                    act.wait_ge(filled, n + 1)
                if kind == "mod":
                    if which >= 2:
                        act.wait_ge(filled, done("modT", which - 2))
                    act.activation(mrow[which % 2], b[0:2, :], ACT.Copy).then_inc(freed["act"], 1)
                if kind == "xrnn":
                    j = which
                    if j >= 2:
                        act.wait_ge(conv_done, j - 1)
                    act.activation(xpad[j % 2][:, 1:1 + CTX], b[:, 0:CTX], ACT.Copy).then_inc(xpad_ready, 1)
                    act.activation(xpad[j % 2][:, 1 + LAT0:1 + PADTOK], b[:, CTX:NTOK], ACT.Copy).then_inc(freed["act"], 1)
                elif kind in ("qlat", "kvlat"):
                    act.wait_ge(filled, n + 1)
                    width = QL if kind == "qlat" else KVL
                    col = (3 if kind == "qlat" else 6) + which
                    chain(act.activation(lru_sq[:, 0:width], b[:, 0:width], ACT.Square, accum_out=ss[:, col:col + 1]))
                    act.activation(rs[:, col:col + 1], ss[:, col:col + 1], ACT.Sqrt, scale=1.0 / width, bias=eps).then_inc(root, 1)
                elif kind == "lru":
                    m, s = which
                    d, j = m % 2, m // 2
                    cur = lru[:, m % SETS]
                    if m == 0 and s == 0:
                        act.wait_ge(lru_cols, 1)
                        act.wait_ge(*out_of("kvlat", NT - 1))
                    if m >= SETS and s == 0:
                        act.wait_ge(lru_done, (m - SETS) // 2 + 1)
                    bias = hbias[:, 16 * s + 8 * d + j:16 * s + 8 * d + j + 1]
                    act.activation(cur[:, s, :], b[:, 0:PADTOK], ACT.Tanh, scale=0.5, bias=bias).then_inc(freed["act"], 1)
                    if s == 1:
                        c = 8 * d + j
                        act.wait_ge(freed["act"], emptied_by[n][1])
                        chain(act.activation(cur[:, 2, :], cur[:, 0, :], ACT.Exp, scale=hc[:, c:c + 1], bias=hc[:, c:c + 1]))
                        act.activation(cur[:, 0, :], cur[:, 0, :], ACT.Tanh, scale=nhc[:, c:c + 1], bias=nhc[:, c:c + 1]).then_inc(lru_ez, 1)
                        if m % BATCH == BATCH - 1:
                            for mb in range(m - BATCH + 1, m + 1):
                                act.wait_ge(lru_q, mb + 1)
                                root_of = lru[:, mb % SETS, 0, :]
                                act.activation(root_of, root_of, ACT.Sqrt, scale=0.25).then_inc(lru_root, 1)
                elif kind == "qlT":
                    act.activation(qlT[:, which, :], b[:, 0:NTOK], ACT.Copy).then_inc(freed["act"], 1)
                elif kind == "ckvT":
                    act.activation(ckvT[:, which, :], b[:, :], ACT.Copy).then_inc(freed["act"], 1)
                elif kind == "uq":
                    t, hf = which
                    if which == (0, 0):
                        act.wait_ge(lru_done, 8)
                    if t >= 2:
                        act.wait_ge(filled, done("qkT", (t - 2, 1)))
                    act.activation(work[:, t % 2, 4 * hf:4 * hf + 4, :], b[:, 0:4 * QK].rearrange("p (h d) -> p h d", d=QK),
                                   ACT.Copy).then_inc(freed["act"], 1)
                elif kind == "uk":
                    w = which + 3
                    act.wait_ge(filled, done("qkT", (w - 2, 1)))
                    act.activation(work[:, w % 2, :, 0:NOPE], b[:, :].rearrange("p (h d) -> p h d", d=NOPE),
                                   ACT.Copy).then_inc(freed["act"], 1)
                elif kind == "uv":
                    act.activation(values[:, which, :], b[:, :], ACT.Copy).then_inc(freed["act"], 1)
                if (kind == "uq" and which[1] == 1) or kind == "uk":
                    w = which[0] if kind == "uq" else which + 3
                    act.wait_ge(work_sq, w + 1)
                    act.activation(rsh[:, w, :], ssh[:, w, :], ACT.Sqrt, scale=1.0 / QK, bias=eps).then_inc(work_root, 1)
                elif kind == "qkT":
                    w, hf = which
                    src = b[0:QK, :].rearrange("p (h n) -> p h n", n=P)
                    dst = qT[0:QK, 4 * hf:4 * hf + 4, w * P:(w + 1) * P] if w < 3 else \
                        kT[0:QK, 4 * hf:4 * hf + 4, (w - 3) * P:(w - 2) * P]
                    act.activation(dst, src, ACT.Copy).then_inc(freed["act"], 1)
                elif kind == "grnn":
                    if which >= 2:
                        act.wait_ge(y_ready, which - 1)
                    else:
                        act.wait_ge(lru_done, 8)
                    act.activation(gtmp[:, which % 2, :], b[:, 0:NTOK], ACT.Gelu_apprx_tanh).then_inc(freed["act"], 1)
                elif kind == "score":
                    i = which
                    nk = CTX if UNITS[i][1] == 0 else NTOK
                    act.wait_ge(nmax_ready, i + 1)
                    if i >= 3:
                        act.wait_ge(filled, done("pT", i - 3))
                    act.activation(prob[:, i % 3, 0:nk], b[:, 0:nk], ACT.Exp, scale=QK ** -0.5, bias=rmax[:, i:i + 1],
                                   accum_out=rsum[:, i:i + 1]).then_inc(freed["act"], 1)
                elif kind == "pT":
                    i = which
                    nk = CTX if UNITS[i][1] == 0 else NTOK
                    if i >= 2:
                        act.wait_ge(filled, done("pv", i - 2))
                    act.activation(pT[:, i % 2, 0:nk], b[:, 0:nk], ACT.Copy).then_inc(freed["act"], 1)
                elif kind in ("gb1", "gb2"):
                    c, hf = which
                    if kind == "gb2":
                        act.wait_ge(*out_of("mix", (2 * c, 1)))
                    act.activation(bc[:, c, 512 * hf:512 * hf + 512], b[:, :], ACT.Copy, scale=0.5 if kind == "gb1" else 1.0)\
                       .then_inc(freed["act"], 1)
                elif kind == "gate":
                    if which == 0:
                        act.wait_ge(filled, done("lru", (15, 1)))
                        act.wait_ge(lru_done, 8)
                    if which >= 8:
                        act.wait_ge(*out_of("ornn", which - 8))
                    act.activation(gbuf[:, which % 8, :], b[:, 0:NTOK], ACT.Tanh, scale=0.5).then_inc(freed["act"], 1)
                elif kind == "state":
                    act.activation(st_row[0:16, :], b[0:16, 0:P], ACT.Copy).then_inc(freed["act"], 1)
                    act.wait_ge(freed["act"], emptied_by[n][1])
                    act.dma_start(new_state[0, 0].rearrange("d (j p) -> (d j) p", p=P), st_row[0:16, :]).then_inc(stored, 16)
                elif kind == "h2T" and which[1] == 0:
                    t = which[0]
                    if t == 0:
                        act.wait_ge(scale2_ready, 1)
                    for f in range(4):
                        act.activation(hT[:, f, t * P:t * P + P], b[:, f * P:f * P + P], ACT.Identity, scale=scale2[:, f, min(t, 1):min(t, 1) + 1],
                                       bias=mcol[:, SH2 + f, min(t, 1):min(t, 1) + 1]).then_inc(h2T_low if f < 3 else freed["act"], 1)
                elif kind == "h2tok":
                    t, hf = which
                    act.wait_ge(filled, n + 1)
                    act.activation(h2_hi[:, t, 512 * hf:512 * hf + 512], b[:, :], ACT.Copy).then_inc(h2hi_ready, 1)
                    if which == (NT - 1, 1):
                        act.wait_ge(sel_ready, 1)
                        chain(act.activation(gsh, gsh, ACT.Exp))
                        act.activation(e21, e21, ACT.Exp).then_inc(route_exp, 1)
                elif kind == "omla":
                    act.wait_ge(merged_raw, which + 1)
                    act.activation(merged_hi[which // 2][:, which % 2, :], merged[:, which, :], ACT.Copy).then_inc(merged_hi_ready, 1)
                elif kind == "mix" and which[1] == 1:
                    t = which[0]
                    act.wait_ge(x_ready, MIX.index(which) + 1)
                    act.wait_ge(filled, done("ornn", 7))
                    act.activation(xs[:, t, :], x[:, t, :], ACT.Square, accum_out=ss[:, 9 + t:10 + t]).then_inc(sumsq, 1)
                    act.wait_ge(sumsq, NT + t + 1)
                    act.activation(rs[:, 9 + t:10 + t], ss[:, 9 + t:10 + t], ACT.Sqrt, scale=1.0 / D, bias=eps).then_inc(root, 1)
                if kind == "kvlat" and which == 0:
                    act.wait_ge(*out_of("kvlat", 0))
                    act.dma_start(new_ckv[0, 0], ckv[:, 0, 0:KVL]).then_inc(stored, 16)
                    act.dma_start(new_krope[0, 0], ckv[:, 0, KVL:CK]).then_inc(stored, 16)

            act.wait_ge(stored, 16 * 3)
            for s in (ye_ready, yhi_ready):
                act.sem_inc(s, CREDIT)
            act.wait_ge(*out_of("pos", 0))
            rounds = act.value_load(nri[0:1, :], min_val=1, max_val=ROUNDS)
            with act.Fori(0, rounds) as r:
                with act.Fori(0, PAIRS) as i:
                    k = r * PAIRS + i

                    def split_hi(first, end):
                        for p in range(first, end):
                            if p % PIECES == 0:
                                act.wait_ge(e_loaded[p // PIECES], 16 * k + 16)
                            act.wait_ge(piece_used, ALLP * k + p + 1)
                            act.activation(w_hi[p % PRING], piece_of(p), ACT.Copy).then_inc(hi_ready, 1)

                    def silu(u):
                        act.wait_ge(piece_used, ALLP * k + 8 * u + 4 + PRING)
                        act.wait_ge(h_done, 2 * k + CREDIT)
                        act.activation(hid[u], banks[4 + 2 * u][0:T, :], ACT.Silu).then_inc(sil_ready, 1)

                    def hidden_hi(u):
                        act.wait_ge(h_done, 2 * k + u + 1 + CREDIT)
                        act.activation(he_hi[u], banks[4 + 2 * u][:, 0:HB * T].rearrange("p (f t) -> p f t", t=T), ACT.Copy).then_inc(hehi_ready, 1)

                    def output_hi(u, hf):
                        act.wait_ge(sc_done, 6 * k + CREDIT)
                        act.wait_ge(swt_ready, 4 * k + 2 * u + 2)
                        act.wait_ge(piece_used, ALLP * k + 16 + 4 * u + 2 * hf + 2 + PRING)
                        act.activation(ye_hi[u][:, 512 * hf:512 * hf + 512], banks[2 * u + hf][0:T, :], ACT.Copy, scale=wslot[u])\
                           .then_inc(yhi_ready, 1)

                    split_hi(0, 4)
                    for u in range(2):
                        act.wait_ge(t_done, 4 * k + 2 * u + CREDIT)
                        for hf in range(2):
                            act.wait_ge(gathered, 4 * k + 2 * u + hf + 1)
                            act.activation(row[u][:, 512 * hf:512 * hf + 512], banks[2 * u + hf][0:T, :], ACT.Copy).then_inc(g_out, 1)
                    for u in range(2):
                        for hf in range(2):
                            act.wait_ge(t_done, 4 * k + 2 * u + hf + 1 + CREDIT)
                            act.activation(xe_hi[u][:, 4 * hf:4 * hf + 4, :], banks[2 * u + hf][:, 0:4 * T].rearrange("p (f t) -> p f t", t=T),
                                           ACT.Copy).then_inc(xhi_ready, 1)
                    split_hi(4, 8)
                    silu(0)
                    split_hi(8, 16)
                    hidden_hi(0)
                    silu(1)
                    split_hi(16, 22)
                    hidden_hi(1)
                    output_hi(0, 0)
                    split_hi(22, 24)
                    output_hi(0, 1)
                    output_hi(1, 0)
                    output_hi(1, 1)
            for t in range(NT):
                act.wait_ge(final, t + 1)
                dst = y_prompt[0] if t == 0 else y_sample[0, (t - 1) * P:t * P]
                act.dma_start(dst, x[:, t, :]).then_inc(stored, 16)
            act.wait_ge(stored, 16 * 6)

        @block.vector
        def _(dve):
            steps = [0]

            def chain(ins):
                steps[0] += 1
                ins.then_inc(dve_chain, 1)
                dve.wait_ge(dve_chain, steps[0])

            def tt(out, a, b, op, **kw):
                return dve.tensor_tensor(out, a, b, op, **kw)

            def ts(out, a, s1, op0, s2=None, op1=None):
                if op1 is None:
                    return dve.tensor_scalar(out, a, s1, None, op0)
                return dve.tensor_scalar(out, a, s1, s2, op0, op1)

            def stt(out, a, s, b, op0, op1):
                return dve.scalar_tensor_tensor(out=out, in0=a, scalar=s, in1=b, op0=op0, op1=op1)

            def norm_x(col, n_root, tiles):
                dve.wait_ge(root, n_root)
                cols = slice(col + tiles[0], col + tiles[-1] + 1)
                chain(dve.reciprocal(rs[:, cols], rs[:, cols]))
                for t in tiles:
                    ts(xs[:, t, :], x[:, t, :], rs[:, col + t:col + t + 1], ALU.mult).then_inc(xs_ready, 1)

            def softplus_cols():
                dve.wait_ge(lru_exp, 1)
                z, w, w2, acc16, t16 = lam[:, 1, :], lam[:, 2, :], lam[:, 3, :], lam[:, 4, :], lam[:, 5, :]
                chain(ts(t16, z, 2.0, ALU.add))
                chain(dve.reciprocal(t16, t16))
                chain(tt(w, z, t16, ALU.mult))
                chain(tt(w2, w, w, ALU.mult))
                chain(ts(acc16, w2, 1.0 / 17, ALU.mult, 1.0 / 15, ALU.add))
                for odd in (13, 11, 9, 7, 5, 3, 1):
                    chain(tt(acc16, acc16, w2, ALU.mult))
                    chain(ts(acc16, acc16, 1.0 / odd, ALU.add))
                chain(tt(acc16, acc16, w, ALU.mult))
                chain(ts(t16, vb[:, LAM:LAM + 16], -1.0, ALU.mult, 0.0, ALU.max))
                chain(stt(acc16, acc16, 2.0, t16, ALU.mult, ALU.add))
                chain(ts(hbias, vb[:, BA:BA + 32], 0.5, ALU.mult))
                chain(ts(nhc, acc16, LRU_C / 2, ALU.mult))
                ts(hc, acc16, -LRU_C / 2, ALU.mult).then_inc(lru_cols, 1)

            def lru_finish(m):
                d, j = m % 2, m // 2
                cur = lru[:, m % SETS]
                chain(stt(cur[:, 1, :], cur[:, 1, :], 1.0, xc[:, j, :], ALU.add, ALU.mult))
                dve.wait_ge(lru_root, m + 1)
                chain(tt(cur[:, 1, :], cur[:, 1, :], cur[:, 0, :], ALU.mult))
                for lo, hi, init in ((0, CTX, 0.0), (LAT0, PADTOK, vb[:, STATE + 8 * d + j:STATE + 8 * d + j + 1])):
                    a, bb, o = cur[:, 2, lo:hi], cur[:, 1, lo:hi], cur[:, 0, lo:hi]
                    if d:
                        a, bb, o = a[:, ::-1], bb[:, ::-1], o[:, ::-1]
                    chain(dve.tensor_tensor_scan(o, a, bb, init, ALU.mult, ALU.add))
                edge = cur[:, 0, CTX - 1:CTX] if d == 0 else cur[:, 0, 0:1]
                chain(dve.tensor_copy(st[:, 8 * d + j:8 * d + j + 1], edge))
                if d == 1:
                    fwd = lru[:, (m - 1) % SETS]
                    if j == 0:
                        dve.wait_ge(filled, done("hT", KT - 1))
                    for lo, hi, s in PSEGS:
                        ins = tt(y[:, j, lo:hi], fwd[:, 0, lo + s:hi + s], cur[:, 0, lo + s:hi + s], ALU.add)
                        if lo == 0:
                            chain(ins)
                        else:
                            ins.then_inc(lru_done, 1)

            def head_norm(w):
                cur = work[:, w % 2]
                is_k = w >= 3
                tile = w - 3 if is_k else w
                if is_k:
                    chain(dve.tensor_copy(cur[:, :, NOPE:QK], ckv[:, tile, None, KVL:CK].to_broadcast([P, H, ROPE])))
                dve.wait_ge(work_ready, w)
                chain(tt(sq, cur, cur, ALU.mult))
                dve.tensor_reduce(ssh[:, w, :], sq, AX.X, ALU.add).then_inc(work_sq, 1)
                dve.wait_ge(work_root, w + 1)
                chain(dve.reciprocal(rsh[:, w, :], rsh[:, w, :]))
                chain(tt(cur, cur, rsh[:, w, :, None].to_broadcast([P, H, QK]), ALU.mult))
                last = tt(cur, cur, qk_g[:, int(is_k), None, :].to_broadcast([P, H, QK]), ALU.mult)
                if tile in (1, 2):
                    chain(last)
                    pair = cur[:, :, NOPE:QK].rearrange("p h (i two) -> p h i two", two=2)
                    x1, x2 = pair[:, :, :, 0], pair[:, :, :, 1]
                    tab = const[:, K_ROPE + 32 * (tile - 1):K_ROPE + 32 * tile]
                    co = tab[:, None, 0:16].to_broadcast([P, H, 16])
                    si = tab[:, None, 16:32].to_broadcast([P, H, 16])
                    for k, (a, b2) in enumerate(((x1, co), (x2, si), (x1, si), (x2, co))):
                        chain(tt(rt[:, k], a, b2, ALU.mult))
                    chain(tt(x1, rt[:, 0], rt[:, 1], ALU.subtract))
                    last = tt(x2, rt[:, 2], rt[:, 3], ALU.add)
                last.then_inc(work_ready, 1)

            def diag(row, c, hf):
                at4 = mcol[:, row + 4 * hf:row + 4 * hf + 4, c:c + 1]
                tt(diagonal[hf], ident[:, None, :].to_broadcast([P, 4, P]), at4.to_broadcast([P, 4, P]), ALU.mult).then_inc(diag_ready, 1)

            def first_max(one, v, m):
                chain(tt(one, v, m.to_broadcast([P, NT, 4]), ALU.is_equal))
                chain(tt(one, one, const[:, None, K_FIRST:K_FIRST + 4].to_broadcast([P, NT, 4]), ALU.mult))
                chain(dve.tensor_reduce(gz, one, AX.X, ALU.max))
                chain(tt(one, one, gz.to_broadcast([P, NT, 4]), ALU.is_equal))

            def route():
                gl = lg[:, :, 0:NG]
                chain(dve.tensor_reduce(gm, gl, AX.X, ALU.max))
                first_max(g1h, gl, gm)
                chain(tt(gsh, gl, gm.to_broadcast([P, NT, 4]), ALU.subtract))
                el = lg[:, :, NG:NR].rearrange("p t (g n) -> p t n g", g=NG)
                ep = eprod.rearrange("p t (n g) -> p t n g", g=NG)
                chain(tt(ep, el, g1h[:, :, None, :].to_broadcast([P, NT, EG, NG]), ALU.mult))
                chain(dve.tensor_reduce(ein, ep, AX.X, ALU.add))
                chain(dve.tensor_reduce(m1, ein, AX.X, ALU.max))
                first_max(o1, ein, m1)
                chain(stt(t4, o1, -1e30, ein, ALU.mult, ALU.add))
                chain(dve.tensor_reduce(m2, t4, AX.X, ALU.max))
                first_max(o2, t4, m2)
                tt(e21, m2, m1, ALU.subtract).then_inc(sel_ready, 1)
                dve.wait_ge(route_exp, 1)
                chain(dve.tensor_reduce(gz, gsh, AX.X, ALU.add))
                chain(dve.reciprocal(gw, gz))
                chain(ts(gz, e21, 1.0, ALU.add))
                chain(dve.reciprocal(w1c, gz))
                chain(tt(w2c, w1c, e21, ALU.mult))
                chain(tt(w1c, w1c, gw, ALU.mult))
                chain(tt(w2c, w2c, gw, ALU.mult))
                chain(tt(wsel, o1, w1c.to_broadcast([P, NT, 4]), ALU.mult))
                chain(tt(t4, o2, w2c.to_broadcast([P, NT, 4]), ALU.mult))
                chain(tt(wsel, wsel, t4, ALU.add))
                chain(tt(ssel, o1, o2, ALU.add))
                sh = [P, NT, NG, EG]
                cv = comb.rearrange("p t (g n) -> p t g n", g=NG)
                sv = sel.rearrange("p t (g n) -> p t g n", g=NG)
                chain(tt(cv, g1h[:, :, :, None].to_broadcast(sh), wsel[:, :, None, :].to_broadcast(sh), ALU.mult))
                tt(sv, g1h[:, :, :, None].to_broadcast(sh), ssel[:, :, None, :].to_broadcast(sh), ALU.mult).then_inc(sel_ready, 1)
                chain(dve.memset(posm, 0.0))
                chain(dve.tensor_copy(comb2[:, :, 0:NE, 0], comb))
                chain(tt(comb2[:, :, 0:NE, 1], comb, comb2[:, :, 0:NE, 0].bitcast(F32), ALU.subtract))
                for part in range(2):
                    chain(dve.tensor_copy(comb2[:, :, NE:NE + 2, part], posm[:, :, NE:NE + 2]))

            dve.wait_ge(const_in, 16)
            dve.wait_ge(zeroed, 5)

            for n, (kind, which, who) in enumerate(plan):
                b = banks[n % 8]
                for m in beside[(kind, which)]:
                    piece = splits[m][0]
                    if lo_by(piece[0]) == "dve":
                        whole, hi, lo = split_parts(*piece)
                        dve.wait_ge(hi_made["act"], hi_count[piece])
                        tt(lo, whole, hi.bitcast(F32), ALU.subtract).then_inc(lo_made["dve"], 1)
                if kind == "mix" and which in ((1, 1), (2, 0)):
                    norm_x(9, 8 + which[0] - 1, [which[0] - 1])
                if who == "dve":
                    dve.wait_ge(filled, n + 1)
                if kind == "vec":
                    if which == 0:
                        dve.tensor_copy(va, b[:, 0:NVA]).then_inc(freed["dve"], 1)
                    else:
                        dve.tensor_copy(vb, b[:, 0:NVB]).then_inc(freed["dve"], 1)
                        dve.wait_ge(freed["dve"], 2)
                        ts(lam[:, 5, :], vb[:, LAM:LAM + 16], -1.0, ALU.mult).then_inc(cols_ready, 1)
                        dve.wait_ge(cols_ready, 1)
                        tt(lam[:, 0, :], vb[:, LAM:LAM + 16], lam[:, 5, :], ALU.max).then_inc(lru_ez, 1)
                        dve.wait_ge(tanhc_ready, 1)
                        chain(stt(tanh_c, tanh_c, 1.0, va[:, CVEC:CVEC + 2 * KT].rearrange("p (a b) -> p a b", a=2), ALU.add, ALU.mult))
                        ts(silu_c.rearrange("p f c -> p c f"), tanh_c, 0.5, ALU.mult).then_inc(silu_ready, 1)
                        dve.wait_ge(x_in, 32)
                        norm_x(0, 1, range(NT))
                        dve.tensor_copy(ones_r, ones).then_inc(exact_ready, 1)
                        dve.tensor_copy(upper_r, upper).then_inc(exact_ready, 1)
                        softplus_cols()
                elif kind == "modT":
                    c4 = 4 * which
                    pv = b[:, 0:8].rearrange("p (j c) -> p j c", c=2)
                    for c in range(2):
                        ins = tt(mcol[:, c4:c4 + 4, c], pv[:, :, c], va[:, BMOD + c4:BMOD + c4 + 4], ALU.add)
                        if c == 0:
                            chain(ins)
                        else:
                            ins.then_inc(freed["dve"], 1)
                    if which in (3, 9):
                        dve.wait_ge(freed["dve"], emptied_by[n][1])
                        row, nrm, out = (SC1, N1, scale1) if which == 3 else (SC2, N2, scale2)
                        chain(stt(out[:, :, 0], mcol[:, row:row + KT, 0], 1.0, va[:, nrm:nrm + KT], ALU.add, ALU.mult))
                        ins = stt(out[:, :, 1], mcol[:, row:row + KT, 1], 1.0, va[:, nrm:nrm + KT], ALU.add, ALU.mult)
                        if which == 3:
                            chain(ins)
                        else:
                            ins.then_inc(scale2_ready, 1)
                elif kind == "hT":
                    f = which
                    for c, lo, hi in SEGS:
                        ins = ts(hT[:, f, lo:hi], b[:, lo:hi], scale1[:, f, c:c + 1], ALU.mult, mcol[:, SH1 + f, c:c + 1], ALU.add)
                        ins.then_inc(hT_ready if c == 0 else freed["dve"], 1)
                elif kind == "xrnn":
                    j = which
                    dve.wait_ge(xpad_ready, j + 1)
                    dve.wait_ge(freed["act"], emptied_by[n][1])
                    src = xpad[j % 2]
                    w = [va[:, CONVW + 8 * k + j:CONVW + 8 * k + j + 1] for k in range(4)]
                    chain(ts(xc[:, j, :], src[:, 0:PADTOK], w[0], ALU.mult, va[:, CONVB + j:CONVB + j + 1], ALU.add))
                    for k in range(1, 4):
                        ins = stt(xc[:, j, :], src[:, k:k + PADTOK], w[k], xc[:, j, :], ALU.mult, ALU.add)
                        if k < 3:
                            chain(ins)
                    ins.then_inc(conv_done, 1)
                elif kind == "qlat":
                    t = which
                    if t == 0:
                        dve.wait_ge(row_in, 16 * 8)
                    dve.wait_ge(root, 2 + t)
                    chain(dve.reciprocal(rs[:, 3 + t:4 + t], rs[:, 3 + t:4 + t]))
                    stt(qln[:, t, :], b[:, 0:QL], rs[:, 3 + t:4 + t], qan, ALU.mult, ALU.mult).then_inc(freed["dve"], 1)
                elif kind == "kvlat":
                    t = which
                    dve.wait_ge(root, 5 + t)
                    chain(dve.reciprocal(rs[:, 6 + t:7 + t], rs[:, 6 + t:7 + t]))
                    chain(stt(ckv[:, t, 0:KVL], b[:, 0:KVL], rs[:, 6 + t:7 + t], kvan, ALU.mult, ALU.mult))
                    dve.tensor_copy(ckv[:, t, KVL:CK], b[:, KVL:CK]).then_inc(freed["dve"], 1)
                elif kind == "lru" and which[1] == 1:
                    m = which[0]
                    cur = lru[:, m % SETS]
                    dve.wait_ge(lru_ez, 2 + m)
                    dve.wait_ge(lru_q, m)
                    chain(tt(lru_sq, cur[:, 2, :], cur[:, 2, :], ALU.mult))
                    stt(cur[:, 0, :], lru_sq, 1.0, cur[:, 0, :], ALU.add, ALU.mult).then_inc(lru_q, 1)
                    if m % BATCH == BATCH - 1:
                        for mb in range(m - BATCH + 1, m + 1):
                            lru_finish(mb)
                elif (kind == "uq" and which[1] == 1) or kind == "uk":
                    w = which[0] if kind == "uq" else which + 3
                    dve.wait_ge(freed["act"], emptied_by[n][1])
                    if w == 0:
                        dve.wait_ge(cache_in, 32)
                        dve.wait_ge(*out_of("kvlat", NT - 1))
                    head_norm(w)
                elif kind == "grnn":
                    dve.wait_ge(freed["act"], emptied_by[n][1])
                    tt(y[:, which, :], y[:, which, :], gtmp[:, which % 2, :], ALU.mult).then_inc(y_ready, 1)
                elif kind == "score":
                    i = which
                    nk = CTX if UNITS[i][1] == 0 else NTOK
                    dve.wait_ge(filled, n + 1)
                    chain(dve.tensor_reduce(rmax[:, i:i + 1], b[:, 0:nk], AX.X, ALU.max))
                    ts(rmax[:, i:i + 1], rmax[:, i:i + 1], -QK ** -0.5, ALU.mult).then_inc(nmax_ready, 1)
                    dve.wait_ge(freed["act"], emptied_by[n][1])
                    chain(dve.reciprocal(rsum[:, i:i + 1], rsum[:, i:i + 1]))
                    ts(prob[:, i % 3, 0:nk], prob[:, i % 3, 0:nk], rsum[:, i:i + 1], ALU.mult).then_inc(prob_ready, 1)
                elif kind == "pv":
                    h, q = UNITS[which]
                    lo = 64 * (h % 2)
                    dve.tensor_copy(yatt[lo:lo + 64, h // 2, q * P:(q + 1) * P], b[lo:lo + 64, 0:P]).then_inc(freed["dve"], 1)
                elif kind == "gb1":
                    c, hf = which
                    dve.wait_ge(filled, done("gb1", (0, hf)) if c else done("uv", 3))
                    diag(G1, c, hf)
                elif kind == "ornn":
                    if which == 0:
                        dve.wait_ge(filled, done("score", len(UNITS) - 1))
                    dve.wait_ge(*out_of("gate", which))
                    stt(merged[:, which, :], gbuf[:, which, :], 1.0, b[:, 0:NTOK], ALU.add, ALU.mult).then_inc(freed["dve"], 1)
                elif kind == "omla":
                    dve.wait_ge(*out_of("gate", 8 + which))
                    stt(gbuf[:, which, :], gbuf[:, which, :], 1.0, b[:, 0:NTOK], ALU.add, ALU.mult).then_inc(freed["dve"], 1)
                    dve.wait_ge(freed["dve"], emptied_by[n][1])
                    tt(merged[:, which, :], merged[:, which, :], gbuf[:, which, :], ALU.add).then_inc(merged_raw, 1)
                    for done_f in ([which - 1] if which else []) + ([which] if which == KT - 1 else []):
                        dve.wait_ge(merged_hi_ready, done_f + 1)
                        tt(merged_lo[done_f // 2][:, done_f % 2, :], merged[:, done_f, :], merged_hi[done_f // 2][:, done_f % 2, :].bitcast(F32), ALU.subtract)\
                            .then_inc(merged_ready, 1)
                elif kind == "mix":
                    t, hf = which
                    if which == (0, 0):
                        dve.wait_ge(*out_of("gb1", (1, 1)))
                    seg = slice(512 * hf, 512 * hf + 512)
                    place = MIX.index(which)
                    if place >= 2:
                        dve.wait_ge(x_ready, place - 1)
                    tt(scratch[place % 2], b[:, :], bc[:, min(t, 1), seg], ALU.mult).then_inc(freed["dve"], 1)
                    dve.wait_ge(freed["dve"], emptied_by[n][1])
                    tt(x[:, t, seg], x[:, t, seg], scratch[place % 2], ALU.add).then_inc(x_ready, 1)
                    if which in ((0, 0), (1, 1)):
                        for half in range(2):
                            dve.wait_ge(filled, done("gb1", (1, half)) if t == 0 else done("gb2", (0, half)))
                            diag(G2, t, half)
                    if which == (2, 1):
                        norm_x(9, 8 + t, [t])
                elif kind == "h2T":
                    t, half = which
                    if half == 1:
                        for f4 in range(4):
                            f = 4 + f4
                            ts(hT[:, f, t * P:t * P + P], b[:, f4 * P:f4 * P + P], scale2[:, f, min(t, 1):min(t, 1) + 1], ALU.mult,
                               mcol[:, SH2 + f, min(t, 1):min(t, 1) + 1], ALU.add).then_inc(h2T_high if f4 < 3 else freed["dve"], 1)
                elif kind == "lgT":
                    dve.tensor_copy(lgT[:, which * P:which * P + P], b[0:NR, 0:P]).then_inc(freed["dve"], 1)
                elif kind == "logit":
                    tt(lg, b[:, 0:NT * NR].rearrange("p (t n) -> p t n", n=NR), router_b[:, None, :].to_broadcast([P, NT, NR]), ALU.add)\
                        .then_inc(freed["dve"], 1)
                    dve.wait_ge(freed["dve"], emptied_by[n][1])
                    route()
                elif kind == "h2tok":
                    t, hf = which
                    seg = slice(512 * hf, 512 * hf + 512)
                    dve.wait_ge(h2hi_ready, 2 * t + hf + 1)
                    tt(h2_lo[:, t, seg], b[:, :], h2_hi[:, t, seg].bitcast(F32), ALU.subtract).then_inc(freed["dve"], 1)
                elif kind == "pos":
                    cnt = b[:, 64:64 + NE]
                    chain(dve.tensor_reduce(cmax, cnt, AX.X, ALU.max))
                    pb = b[:, 0:NT * NE].rearrange("p (t n) -> p t n", n=NE)
                    chain(stt(posm[:, :, 0:NE], pb, 1.0, sel.bitcast(F32), ALU.add, ALU.mult))
                    chain(ts(posm, posm, -1.0, ALU.add))
                    chain(ts(rcount, const[:, K_THR:K_THR + ROUNDS], cmax, ALU.is_lt))
                    chain(dve.tensor_reduce(nrf, rcount, AX.X, ALU.add))
                    dve.tensor_copy(nri, nrf).then_inc(freed["dve"], 1)
                    dve.wait_ge(freed["dve"], emptied_by[n][1])

            rounds = dve.value_load(nri[0:1, :], min_val=1, max_val=ROUNDS)

            def maps(k, col, before):
                for u in range(2):
                    dve.wait_ge(swt_done[u], k + CREDIT)
                    dve.tensor_copy(pcur[:, u, :], posm[:, :, bass.ds(col + u, 1)].rearrange("p t e -> p (t e)")).then_inc(pos_cur, 1)
                    dve.tensor_copy(wcur[u], comb2[:, :, bass.ds(col + u, 1), :].rearrange("p t e two -> p (t e) two")).then_inc(pos_cur, 1)
                    dve.wait_ge(pos_cur, 4 * before + 2 * u + 2)
                    for t in range(NT):
                        ts(S[u][:, t, :], iota, pcur[:, u, t:t + 1], ALU.is_equal).then_inc(S_ready, 1)

            with dve.Fori(0, rounds) as r:
                maps(r * PAIRS, 0, r * (PAIRS + 1))
                with dve.Fori(0, PAIRS) as i:
                    k = r * PAIRS + i

                    def split_lo(first, end):
                        for p in range(first, end):
                            dve.wait_ge(hi_ready, ALLP * k + p + 1)
                            tt(w_lo[p % PRING], piece_of(p), w_hi[p % PRING].bitcast(F32), ALU.subtract).then_inc(lo_ready, 1)

                    def hidden(u):
                        dve.wait_ge(sil_ready, 2 * k + u + 1)
                        dve.wait_ge(piece_used, ALLP * k + 8 * u + 8 + PRING)
                        tt(hid[u], hid[u], banks[5 + 2 * u][0:T, :], ALU.mult).then_inc(he_ready, 1)

                    def hidden_lo(u):
                        dve.wait_ge(hehi_ready, 2 * k + u + 1)
                        tt(he_lo[u], banks[4 + 2 * u][:, 0:HB * T].rearrange("p (f t) -> p f t", t=T), he_hi[u].bitcast(F32),
                           ALU.subtract).then_inc(ht_out, 1)

                    split_lo(0, 4)
                    for u in range(2):
                        dve.wait_ge(sc_done, 6 * k + CREDIT)
                        dve.wait_ge(swt_done[u], k + 1 + CREDIT)
                        dve.tensor_copy(SWT[u], banks[6 + u][0:T, 0:NTOK]).then_inc(swt_ready, 1)
                        dve.wait_ge(yhi_ready, 4 * k + CREDIT)
                        dve.wait_ge(ye_ready, 4 * k + CREDIT)
                        dve.tensor_reduce(wslot[u], banks[6 + u][0:T, NTOK:NTOK + 2], AX.X, ALU.add).then_inc(swt_ready, 1)
                    for u in range(2):
                        for hf in range(2):
                            seg = slice(4 * hf, 4 * hf + 4)
                            dve.wait_ge(xhi_ready, 4 * k + 2 * u + hf + 1)
                            tt(xe_lo[u][:, seg, :], banks[2 * u + hf][:, 0:4 * T].rearrange("p (f t) -> p f t", t=T),
                               xe_hi[u][:, seg, :].bitcast(F32), ALU.subtract).then_inc(xe_ready, 1)
                    split_lo(4, 11)
                    hidden(0)
                    split_lo(11, 16)
                    hidden_lo(0)
                    split_lo(16, 19)
                    hidden(1)
                    split_lo(19, 22)
                    hidden_lo(1)
                    split_lo(22, 24)
                    maps(k + 1, 2 * i + 2, k + r + 1)
                    for u in range(2):
                        for hf in range(2):
                            seg = slice(512 * hf, 512 * hf + 512)
                            dve.wait_ge(yhi_ready, 4 * k + 2 * u + hf + 1 + CREDIT)
                            stt(ye_lo[u][:, seg], banks[2 * u + hf][0:T, :], wslot[u], ye_hi[u][:, seg].bitcast(F32), ALU.mult, ALU.subtract)\
                                .then_inc(ye_ready, 1)
                    dve.wait_ge(acc_step, 6 * k + 1)
                    for m in range(6):
                        hf, t = m // 3, m % 3
                        dve.wait_ge(sc_done, 6 * k + m + 1 + CREDIT)
                        part = acc[:, t, 512 * hf:512 * hf + 512]
                        tt(part, part, banks[4 + m % 4][:, :], ALU.add).then_inc(acc_step, 1)
                dve.wait_ge(S_ready, (r + 1) * (PAIRS + 1) * 6)
                dve.tensor_scalar(posm, posm, -float(T), None, ALU.add).then_inc(pos_round, 1)
                dve.wait_ge(pos_round, r + 1)
            dve.wait_ge(acc_step, rounds * (6 * PAIRS) + 1)
            for t in range(NT):
                chain(tt(acc[:, t, :], acc[:, t, :], bc[:, min(t, 1), :], ALU.mult))
                tt(x[:, t, :], x[:, t, :], acc[:, t, :], ALU.add).then_inc(final, 1)

        @block.tensor
        def _(pe):
            va_row, vb_row = mem[0:NVA, at_qln:at_qln + P], mem[0:NVB, at_qln + P:at_qln + 2 * P]

            def weights(key):
                pe.wait_ge(loaded[slot_of(key)], 16 * loads(chunk_no[key]))
                return chunk_ap(key)

            def split_weights(key, f, col, width):
                lo_slot, hi_slot = SPLIT_SLOTS[key]
                at_col = f * (D if key[0] == "omla" else 512) + col
                q, lo = at_col // (SLOT // 4), at_col % (SLOT // 4)
                return [ring_r[b][q][:, lo:lo + width] for b in (hi_slot, lo_slot)]

            def split_product(out, left, right, first, last):
                pe.matmul(out, left[0], right[0], start=first, stop=False)
                pe.matmul(out, left[0], right[1], start=False, stop=False)
                return pe.matmul(out, left[1], right[0], start=False, stop=last)

            pe.wait_ge(const_in, 16)
            pe.wait_ge(vec_in, 16 * 11)
            pe.wait_ge(zeroed, 5)
            for n, (kind, which, who) in enumerate(plan):
                b = banks[n % 8]
                if n >= 8:
                    w, c = emptied_by[n - 8]
                    pe.wait_ge(freed[w], c)
                mm = None
                if kind == "vec":
                    src, rows = (va_row, NVA) if which == 0 else (vb_row, NVB)
                    mm = pe.transpose(b[:, 0:rows], src, ident[0:rows, 0:rows])
                elif kind == "mod":
                    if which == 0:
                        pe.wait_ge(silu_ready, 1)
                    w = weights(("mod", which))
                    for f in range(KT):
                        mm = pe.matmul(b[0:2, :], silu_c[:, f, :], w[:, f, :], start=(f == 0), stop=(f == KT - 1))
                elif kind == "modT":
                    pe.wait_ge(*out_of("mod", which))
                    for jb in range(4):
                        mm = pe.transpose(b[:, 2 * jb:2 * jb + 2], mrow[which % 2][:, P * jb:P * jb + P], ident[0:2, 0:2])
                elif kind == "h2T":
                    t, half = which
                    pe.wait_ge(xs_ready, NT + t + 1)
                    for f4 in range(4):
                        f = 4 * half + f4
                        mm = pe.transpose(b[:, f4 * P:f4 * P + P], xs[:, t, f * P:f * P + P], ident)
                elif kind == "hT":
                    pe.wait_ge(xs_ready, NT)
                    for t in range(NT):
                        mm = pe.transpose(b[:, t * P:t * P + P], xs[:, t, which * P:which * P + P], ident)
                elif kind == "ornn" or (kind == "gate" and which >= 8) or kind == "omla":
                    name, src, blocks = {"ornn": ("y", (y_hi, y_lo), KT), "gate": ("hT", (hT_hi, hT_lo), KT),
                                         "omla": ("yatt", (yatt_hi, yatt_lo), 4)}[kind]
                    key = (kind, 0 if kind == "omla" else which // 4)
                    col = P * which if kind == "omla" else P * (which % 4)
                    for f in range(blocks):
                        for piece in ((key, 4 * f // blocks), (name, 4 * f // blocks)):
                            pe.wait_ge(lo_made[lo_by(piece[0])], lo_count[piece])
                        mm = split_product(b[:, 0:NTOK], split_weights(key, f, col, P), [part[f // 2][:, f % 2, :] for part in src],
                                           f == 0, f == blocks - 1)
                elif kind in ("xrnn", "grnn", "gate"):
                    if kind == "xrnn" and which == 0:
                        pe.wait_ge(hT_ready, KT)
                        pe.wait_ge(*out_of("hT", KT - 1))
                    w = weights((kind, which // 4))
                    for f in range(KT):
                        mm = pe.matmul(b[:, 0:NTOK], w[:, f, P * (which % 4):P * (which % 4) + P], hT[:, f, :],
                                       start=(f == 0), stop=(f == KT - 1))
                elif kind in ("qlat", "kvlat"):
                    w = weights((kind, 0))
                    width = QL if kind == "qlat" else CK
                    for f in range(KT):
                        mm = pe.matmul(b[:, 0:width], hT[:, f, which * P:which * P + P], w[:, f, :], start=(f == 0), stop=(f == KT - 1))
                elif kind == "lru":
                    m, s = which
                    if m == 0 and s == 0:
                        pe.wait_ge(lruw_in, 16 * 8)
                        pe.wait_ge(conv_done, KT)
                    j, d = m // 2, m % 2
                    mm = pe.matmul(b[:, 0:PADTOK], lruw[:, 4 * j + 2 * d + s, :], xc[:, j, :], start=True, stop=True)
                elif kind == "qlT":
                    pe.wait_ge(*out_of("qlat", NT - 1))
                    for t in range(NT):
                        mm = pe.transpose(b[:, t * P:t * P + P], qln[:, t, which * P:which * P + P], ident)
                elif kind == "ckvT":
                    pe.wait_ge(*out_of("kvlat", NT - 1))
                    pe.wait_ge(cache_in, 32)
                    for t in range(4):
                        mm = pe.transpose(b[:, t * P:t * P + P], ckv[:, t, which * P:which * P + P], ident)
                elif kind == "uq":
                    t, hf = which
                    pe.wait_ge(*out_of("qlT", 2))
                    w = weights(("uq", 0))
                    for f in range(3):
                        mm = pe.matmul(b[:, 0:4 * QK], qlT[:, f, t * P:t * P + P], w[:, f, 4 * QK * hf:4 * QK * (hf + 1)],
                                       start=(f == 0), stop=(f == 2))
                elif kind in ("uk", "uv"):
                    pe.wait_ge(*out_of("ckvT", 1))
                    w = weights(("ukv", 0))
                    for f in range(2):
                        mm = pe.matmul(b[:, :], ckvT[:, f, which * P:which * P + P], w[:, f + (2 if kind == "uv" else 0), :],
                                       start=(f == 0), stop=(f == 1))
                elif kind == "qkT":
                    wi, hf = which
                    pe.wait_ge(work_ready, wi + 1)
                    for h4 in range(4):
                        mm = pe.transpose(b[0:QK, h4 * P:h4 * P + P], work[:, wi % 2, 4 * hf + h4, :], ident)
                elif kind == "score":
                    h, q = UNITS[which]
                    pe.wait_ge(*out_of("qkT", (6, 1)))
                    lo, hi = (0, P) if q == 0 else (P, 4 * P)
                    mm = pe.matmul(b[:, 0:hi - lo], qT[0:QK, h, q * P:q * P + P], kT[0:QK, h, lo:hi], start=True, stop=True)
                elif kind == "pT":
                    q = UNITS[which][1]
                    pe.wait_ge(prob_ready, which + 1)
                    for t in range(1 if q == 0 else 3):
                        mm = pe.transpose(b[:, t * P:t * P + P], prob[:, which % 3, t * P:t * P + P], ident)
                elif kind == "pv":
                    h, q = UNITS[which]
                    pe.wait_ge(*out_of("pT", which))
                    lo = 64 * (h % 2)
                    tiles = [0] if q == 0 else [1, 2, 3]
                    for z, t in enumerate(tiles):
                        mm = pe.matmul(b[lo:lo + 64, 0:P], values[:, t, V * h:V * h + V], pT[:, which % 2, z * P:z * P + P],
                                       start=(z == 0), stop=(z == len(tiles) - 1))
                elif kind in ("gb1", "gb2"):
                    c, hf = which
                    pe.wait_ge(diag_ready, (4 if kind == "gb2" else 0) + 2 * c + hf + 1)
                    mm = pe.matmul(b[:, :], ones, diagonal[hf].rearrange("p a b -> p (a b)"), start=True, stop=True)
                elif kind == "mix":
                    t, hf = which
                    for f in range(KT):
                        pe.wait_ge(merged_ready, f + 1)
                        pe.wait_ge(lo_made["pool"], lo_count[(("wout", hf), f // 2)])
                        mm = split_product(b[:, :], [part[f // 2][:, f % 2, t * P:t * P + P] for part in (merged_hi, merged_lo)],
                                           split_weights(("wout", hf), f, 0, 512), f == 0, f == KT - 1)
                elif kind == "state":
                    pe.wait_ge(lru_done, 8)
                    mm = pe.transpose(b[0:16, 0:P], st, ident)
                elif kind in ("lgT", "h2tok"):
                    t = which if kind == "lgT" else which[0]
                    pe.wait_ge(*out_of("h2T", (t, 0)))
                    pe.wait_ge(*out_of("h2T", (t, 1)))
                    pe.wait_ge(h2T_low, 3 * (t + 1))
                    pe.wait_ge(h2T_high, 3 * (t + 1))
                    if kind == "lgT":
                        pe.wait_ge(row_in, 16 * 8)
                        for f in range(KT):
                            mm = pe.matmul(b[0:NR, 0:P], router_w[:, f, :], hT[:, f, t * P:t * P + P], start=(f == 0), stop=(f == KT - 1))
                    else:
                        for f4 in range(4):
                            mm = pe.transpose(b[:, f4 * P:f4 * P + P], hT[:, 4 * which[1] + f4, t * P:t * P + P], ident)
                elif kind == "logit":
                    pe.wait_ge(*out_of("lgT", NT - 1))
                    for t in range(NT):
                        mm = pe.transpose(b[:, NR * t:NR * t + NR], lgT[:, t * P:t * P + P], ident[0:NR, 0:NR])
                elif kind == "pos":
                    pe.wait_ge(exact_ready, 2)
                    pe.wait_ge(sel_ready, 2)
                    for t in range(NT):
                        for t2 in range(t + 1):
                            pe.matmul(b[:, NE * t:NE * t + NE], upper_r if t2 == t else ones_r, sel[:, t2, :],
                                      start=(t2 == 0), stop=(t2 == t))
                    for t2 in range(NT):
                        mm = pe.matmul(b[:, 64:64 + NE], ones_r, sel[:, t2, :], start=(t2 == 0), stop=(t2 == NT - 1))
                mm.then_inc(filled, 1)

            for w in ("act", "dve"):
                pe.wait_ge(freed[w], count[w])
            for s in [*swt_done, sc_done, h_done, t_done]:
                pe.sem_inc(s, CREDIT)
            pe.sem_inc(piece_used, PRING)
            pe.wait_ge(*out_of("pos", 0))
            rounds = pe.value_load(nri[0:1, :], min_val=1, max_val=ROUNDS)
            with pe.Fori(0, rounds) as r:
                with pe.Fori(0, PAIRS) as i:
                    k = r * PAIRS + i
                    pe.wait_ge(ye_ready, 4 * k + CREDIT)
                    for u in range(2):
                        pe.wait_ge(S_ready, 6 * (k + r) + 3 * u + 3)
                        for hf in range(2):
                            seg = slice(512 * hf, 512 * hf + 512)
                            for t in range(NT):
                                pe.matmul(banks[2 * u + hf][0:T, :], S[u][:, t, :], h2_hi[:, t, seg], start=(t == 0), stop=False)
                                mm = pe.matmul(banks[2 * u + hf][0:T, :], S[u][:, t, :], h2_lo[:, t, seg], start=False, stop=(t == NT - 1))
                            mm.then_inc(gathered, 1)
                    pe.wait_ge(acc_step, 6 * k + 1)
                    for u in range(2):
                        for t in range(NT):
                            pe.transpose(banks[6 + u][0:T, t * P:t * P + P], S[u][:, t, :].bitcast(F32), ident)
                        for t in range(NT):
                            mm = pe.matmul(banks[6 + u][0:T, NTOK:NTOK + 2], S[u][:, t, :], wcur[u][:, t, :], start=(t == 0), stop=(t == NT - 1))
                        mm.then_inc(swt_done[u], 1)
                    for u in range(2):
                        for hf in range(2):
                            pe.wait_ge(g_out, 4 * k + 2 * u + hf + 1)
                            for f in range(4):
                                mm = pe.transpose(banks[2 * u + hf][:, T * f:T * f + T], row[u][:, (4 * hf + f) * P:(4 * hf + f + 1) * P],
                                                  ident[0:T, 0:T])
                            mm.then_inc(t_done, 1)

                    def products(p, left_hi, left_lo):
                        pe.wait_ge(lo_ready, ALLP * k + p + 1)
                        j, q = p // PIECES, p % PIECES
                        out, blocks = (banks[4 + j], KT) if j < 4 else (banks[2 * (j - 4) + q // 2], HB)
                        out = out[0:T, :]
                        for z in range(PIECE):
                            f = (PIECE * q + z) % blocks
                            hi, lo = w_hi[p % PRING][:, z, :], w_lo[p % PRING][:, z, :]
                            pe.matmul(out, left_hi[:, f, :], hi, start=(f == 0), stop=False)
                            pe.matmul(out, left_hi[:, f, :], lo, start=False, stop=False)
                            mm = pe.matmul(out, left_lo[:, f, :], hi, start=False, stop=(f == blocks - 1))
                        mm.then_inc(piece_used, 1)

                    def turn_hidden(u):
                        pe.wait_ge(he_ready, 2 * k + u + 1)
                        for f in range(HB):
                            mm = pe.transpose(banks[4 + 2 * u][:, T * f:T * f + T], hid[u][:, f * P:f * P + P], ident[0:T, 0:T])
                        mm.then_inc(h_done, 1)

                    pe.wait_ge(xe_ready, 4 * k + 2)
                    for p in range(8):
                        products(p, xe_hi[0], xe_lo[0])
                    pe.wait_ge(xe_ready, 4 * k + 4)
                    pe.wait_ge(swt_ready, 4 * k + 4)
                    for p in range(8, 12):
                        products(p, xe_hi[1], xe_lo[1])
                    turn_hidden(0)
                    for p in range(12, 16):
                        products(p, xe_hi[1], xe_lo[1])
                    pe.wait_ge(ht_out, 2 * k + 1)
                    for p in range(16, 18):
                        products(p, he_hi[0], he_lo[0])
                    turn_hidden(1)
                    for p in range(18, 20):
                        products(p, he_hi[0], he_lo[0])
                    pe.wait_ge(ht_out, 2 * k + 2)
                    for p in range(20, 24):
                        products(p, he_hi[1], he_lo[1])

                    def scatter(m, u):
                        hf, t = m // 3, m % 3
                        seg = slice(512 * hf, 512 * hf + 512)
                        pe.matmul(banks[4 + m % 4][:, :], SWT[u][:, t * P:t * P + P], ye_hi[u][:, seg], start=(u == 0), stop=False)
                        return pe.matmul(banks[4 + m % 4][:, :], SWT[u][:, t * P:t * P + P], ye_lo[u][:, seg], start=False, stop=(u == 1))

                    pe.wait_ge(ye_ready, 4 * k + 2 + CREDIT)
                    for m in range(4):
                        scatter(m, 0)
                    pe.wait_ge(ye_ready, 4 * k + 3 + CREDIT)
                    for m in range(6):
                        if m == 3:
                            pe.wait_ge(ye_ready, 4 * k + 4 + CREDIT)
                        if m >= 4:
                            pe.wait_ge(acc_step, 6 * k + m - 2)
                            scatter(m, 0)
                        scatter(m, 1).then_inc(sc_done, 1)


_NAMES = ['x_prompt', 'x_sample', 'cache_mla_ckv', 'cache_mla_krope', 'state_rglru', 'c', 'c_ctx', 'norm1_g', 'norm2_g',
          'w_mod', 'b_mod', 'w_in', 'conv_w', 'conv_b', 'lru_wa', 'lru_ba', 'lru_wx', 'lru_bx', 'lru_lam', 'q_a_norm',
          'kv_a_norm', 'w_uq', 'w_uk', 'w_uv', 'q_norm', 'k_norm', 'w_o_rnn', 'w_o_mla', 'w_out', 'router_wg', 'router_bg',
          'router_we', 'router_be', 'exp_w1', 'exp_w3', 'exp_w2']
_OUTS = [(1, CTX, D), (1, LAT, D), (1, 1, CTX, KVL), (1, 1, CTX, ROPE), (1, 1, 2, D)]


def shape_constants():
    import numpy as np
    k = np.zeros((P, NK), np.float32)
    k[:, K_ID:K_ID + P] = np.eye(P)
    k[:, K_UP:K_UP + P] = np.triu(np.ones((P, P)), 1)
    k[:, K_IOTA:K_IOTA + T] = np.arange(T)
    token = np.arange(LAT)
    inv = (10000.0 ** (-np.arange(0, 16, 2, dtype=np.float32) / 16)).astype(np.float32)
    ang = np.concatenate([(token // 64).astype(np.float32)[:, None] * inv, (token % 64).astype(np.float32)[:, None] * inv], -1)
    tab = np.concatenate([np.cos(ang), np.sin(ang)], -1).astype(np.float32)
    k[:, K_ROPE:K_ROPE + 32] = tab[:P]
    k[:, K_ROPE + 32:K_ROPE + 64] = tab[P:]
    k[:, K_FIRST:K_FIRST + 4] = [4, 3, 2, 1]
    k[:, K_THR:K_THR + ROUNDS] = T * np.arange(ROUNDS)
    return k


def kernel(**inputs):
    import numpy as _np
    import concourse.bacc as _bacc
    from concourse import mybir as _mybir
    from concourse.bass_utils import run_bass_kernel_spmd as _run

    nc = _bacc.Bacc("TRN2", target_bir_lowering=False, num_devices=1)
    arrays, io = {}, {}
    for name in _NAMES:
        arrays[f"in_{name}"] = _np.ascontiguousarray(inputs[name])
    arrays["in_consts"] = shape_constants()
    for key, a in arrays.items():
        io[key[3:]] = nc.dram_tensor(key, a.shape, _mybir.dt.from_np(a.dtype), kind="ExternalInput").ap()
    outs = [nc.dram_tensor(f"out_{i}", s, _mybir.dt.float32, kind="ExternalOutput").ap() for i, s in enumerate(_OUTS)]
    hybrid_step(nc, io, *outs)
    r = _run(nc, [arrays], core_ids=[0])
    return tuple(r.results[0][f"out_{i}"] for i in range(len(_OUTS)))
```
